# Optimizing a Trainium2 kernel written in Bass

```python
import math, functools
import jax, jax.numpy as jnp
from jax import lax
import numpy as np

D_MODEL = 2048
BATCH = 1
SEQ = 256
DEPTH = 2
DEC_BATCH = 8
DEC_SEQ = 4
PAST_LEN = 1024
PAGE_SIZE = 128

N_A_LAYERS = (DEPTH + 1) // 2
N_C_LAYERS = DEPTH // 2
CONV_W = 4
GDN_HEADS = 8
GDN_DK = 128
GDN_DV = 128
GDN_QK = GDN_HEADS * GDN_DK
GDN_WIDTH = GDN_HEADS * GDN_DV
GDN_QKV = 2 * GDN_QK + GDN_WIDTH
GDN_CHUNK = 64
LRU_WIDTH = D_MODEL // 2
LRU_BLOCKS = 8
LRU_BW = LRU_WIDTH // LRU_BLOCKS
LRU_C = 8.0
IN_A = GDN_QKV + GDN_WIDTH + 2 * GDN_HEADS + 2 * LRU_WIDTH
MIX_A = GDN_WIDTH + LRU_WIDTH
MLA_HEADS = 16
Q_LORA = 512
KV_LORA = 512
QK_NOPE = 128
QK_ROPE = 64
V_HEAD = 128
IN_C = Q_LORA + KV_LORA + QK_ROPE
MLA_SCALE = (QK_NOPE + QK_ROPE) ** -0.5
ROPE_BASE = 10000.0
Q_BLOCK = 128
D_FF = 4 * D_MODEL
PLE_DIM = 256
EPS = 1e-6

kernel_name = 'hybrid_gdn_rglru_mla_decoder_step'

def _rmsnorm(x, g):
    xf = x.astype(jnp.float32)
    xf = xf * lax.rsqrt(jnp.mean(xf * xf, axis=-1, keepdims=True) + EPS)
    return (xf * g.astype(jnp.float32)).astype(x.dtype)

def _l2norm(x):
    xf = x.astype(jnp.float32)
    return xf * lax.rsqrt(jnp.sum(xf * xf, axis=-1, keepdims=True) + EPS)

def _causal_conv(x, buf, w):
    xx = jnp.concatenate([buf.astype(x.dtype), x], axis=1)
    y = lax.conv_general_dilated(xx, w[:, None, :].astype(x.dtype), (1,), 'VALID',
                                 dimension_numbers=('NWC', 'WIO', 'NWC'),
                                 feature_group_count=x.shape[-1])
    return y, xx[:, xx.shape[1] - (CONV_W - 1):]

def _rope(x, positions):
    half = QK_ROPE // 2
    inv = ROPE_BASE ** (-jnp.arange(half, dtype=jnp.float32) / half)
    ang = positions.astype(jnp.float32)[:, None] * inv[None, :]
    cos = jnp.cos(ang)[None, :, None, :]
    sin = jnp.sin(ang)[None, :, None, :]
    xf = x.astype(jnp.float32)
    x1, x2 = xf[..., :half], xf[..., half:]
    return jnp.concatenate([x1 * cos - x2 * sin, x1 * sin + x2 * cos], axis=-1).astype(x.dtype)

def _gated_delta(q, k, v, beta, g, s0):
    f32 = jnp.float32
    B, L, H, DK = q.shape
    DV = v.shape[-1]
    C = min(GDN_CHUNK, L)
    N = -(-L // C)
    pad = N * C - L
    q, k, v, beta, g = (t.astype(f32) for t in (q, k, v, beta, g))
    if pad:
        pw = lambda t: jnp.pad(t, [(0, 0), (0, pad)] + [(0, 0)] * (t.ndim - 2))
        q, k, v, beta, g = (pw(t) for t in (q, k, v, beta, g))

    def chunks(t):
        t = t.reshape((B, N, C, H) + t.shape[3:])
        return t.transpose((1, 0, 3, 2) + tuple(range(4, t.ndim)))

    qc, kc, vc, bc = chunks(q), chunks(k), chunks(v), chunks(beta)
    gc = jnp.cumsum(chunks(g), axis=-1)
    tri = jnp.tril(jnp.ones((C, C), bool))
    strict = jnp.tril(jnp.ones((C, C), bool), -1)
    decay = jnp.exp(jnp.where(tri, gc[..., :, None] - gc[..., None, :], -jnp.inf))
    kb = kc * bc[..., None]
    a = jnp.where(strict, jnp.einsum('nbhcd,nbhsd->nbhcs', kb, kc) * decay, 0.0)
    eye = jnp.eye(C, dtype=f32)
    rhs = jnp.concatenate([vc * bc[..., None], kb * jnp.exp(gc)[..., None]], axis=-1)
    sol = lax.linalg.triangular_solve(a + eye, rhs, left_side=True, lower=True)
    u, w = sol[..., :DV], sol[..., DV:]
    qk = jnp.where(tri, jnp.einsum('nbhcd,nbhsd->nbhcs', qc, kc) * decay, 0.0)

    def step(s, xs):
        q_i, k_i, u_i, w_i, qk_i, g_i = xs
        v_new = u_i - jnp.einsum('bhcd,bhde->bhce', w_i, s)
        o_i = (jnp.einsum('bhcd,bhde->bhce', q_i * jnp.exp(g_i)[..., None], s)
               + jnp.einsum('bhcs,bhse->bhce', qk_i, v_new))
        g_last = g_i[..., -1:]
        s = (s * jnp.exp(g_last)[..., None]
             + jnp.einsum('bhcd,bhce->bhde', k_i * jnp.exp(g_last - g_i)[..., None], v_new))
        return s, o_i

    s, o = lax.scan(step, s0.astype(f32), (qc, kc, u, w, qk, gc))
    o = o.transpose(1, 0, 3, 2, 4).reshape(B, N * C, H, DV)[:, :L]
    return o, s

def _lin_comb(left, right):
    a1, b1 = left
    a2, b2 = right
    return a1 * a2, a2 * b1 + b2

def _mixer_ab(hn, s0, qkv_buf, h0, lru_buf, w_in, conv_qkv_w, a_log, dt_bias, gdn_norm_g,
              conv_lru_w, conv_lru_b, lru_wa, lru_ba, lru_wi, lru_bi, lru_lambda, w_out):
    f32 = jnp.float32
    B, L, _ = hn.shape
    cuts = [GDN_QKV, GDN_QKV + GDN_WIDTH, GDN_QKV + GDN_WIDTH + GDN_HEADS,
            GDN_QKV + GDN_WIDTH + 2 * GDN_HEADS, GDN_QKV + GDN_WIDTH + 2 * GDN_HEADS + LRU_WIDTH]
    qkv, z, b_raw, a_raw, lx, ly = jnp.split(hn @ w_in, cuts, axis=-1)
    qkv, qkv_buf_new = _causal_conv(qkv, qkv_buf, conv_qkv_w)
    qkv = jax.nn.silu(qkv)
    q = _l2norm(qkv[..., :GDN_QK].reshape(B, L, GDN_HEADS, GDN_DK)) * (GDN_DK ** -0.5)
    k = _l2norm(qkv[..., GDN_QK:2 * GDN_QK].reshape(B, L, GDN_HEADS, GDN_DK))
    v = qkv[..., 2 * GDN_QK:].reshape(B, L, GDN_HEADS, GDN_DV)
    beta = jax.nn.sigmoid(b_raw.astype(f32))
    g = -jnp.exp(a_log.astype(f32)) * jax.nn.softplus(a_raw.astype(f32) + dt_bias.astype(f32))
    o, s_new = _gated_delta(q, k, v, beta, g, s0)
    o = _rmsnorm(o, gdn_norm_g) * jax.nn.silu(z.astype(f32).reshape(B, L, GDN_HEADS, GDN_DV))
    xb, lru_buf_new = _causal_conv(lx, lru_buf, conv_lru_w)
    xb = (xb + conv_lru_b).astype(f32)
    xblk = xb.reshape(B, L, LRU_BLOCKS, LRU_BW)
    r = jax.nn.sigmoid(jnp.einsum('blki,kij->blkj', xblk, lru_wa.astype(f32)) + lru_ba).reshape(B, L, LRU_WIDTH)
    ig = jax.nn.sigmoid(jnp.einsum('blki,kij->blkj', xblk, lru_wi.astype(f32)) + lru_bi).reshape(B, L, LRU_WIDTH)
    log_a = -LRU_C * r * jax.nn.softplus(-lru_lambda.astype(f32))
    a = jnp.exp(log_a)
    bt = jnp.sqrt(-jnp.expm1(2.0 * log_a)) * (ig * xb)
    bt = bt.at[:, 0].add(a[:, 0] * h0.astype(f32))
    _, hs = lax.associative_scan(_lin_comb, (a, bt), axis=1)
    ob = hs * jax.nn.gelu(ly.astype(f32))
    mix = jnp.concatenate([o.reshape(B, L, GDN_WIDTH), ob], axis=-1).astype(hn.dtype) @ w_out
    return mix, s_new.astype(s0.dtype), qkv_buf_new, hs[:, -1].astype(h0.dtype), lru_buf_new

def _attend_prompt(q_nope, q_pe, ckv, kpe, w_uk, w_uv):
    f32 = jnp.float32
    B, S, H, _ = q_nope.shape
    k_nope = jnp.einsum('bsc,chn->bshn', ckv, w_uk)
    v = jnp.einsum('bsc,chv->bshv', ckv, w_uv)
    nb = S // Q_BLOCK
    qn = q_nope.reshape(B, nb, Q_BLOCK, H, QK_NOPE).swapaxes(0, 1)
    qp = q_pe.reshape(B, nb, Q_BLOCK, H, QK_ROPE).swapaxes(0, 1)
    key_pos = jnp.arange(S)

    def block(args):
        qn_i, qp_i, start = args
        s = (jnp.einsum('bqhn,bkhn->bhqk', qn_i.astype(f32), k_nope.astype(f32))
             + jnp.einsum('bqhr,bkr->bhqk', qp_i.astype(f32), kpe.astype(f32))) * MLA_SCALE
        mask = key_pos[None, :] <= (start + jnp.arange(Q_BLOCK))[:, None]
        pr = jax.nn.softmax(jnp.where(mask, s, -jnp.inf), axis=-1)
        return jnp.einsum('bhqk,bkhv->bqhv', pr.astype(v.dtype), v)

    o = lax.map(block, (qn, qp, jnp.arange(nb) * Q_BLOCK))
    return o.swapaxes(0, 1).reshape(B, S, H, V_HEAD)

def _attend_paged(q_nope, q_pe, ckv_new, kpe_new, w_uk, w_uv, pool_ckv, pool_kpe, layer, page_table):
    f32 = jnp.float32
    B, T, H, _ = q_nope.shape
    q_lat = jnp.einsum('bthn,chn->bhtc', q_nope.astype(f32), w_uk.astype(f32)) * MLA_SCALE
    q_rot = jnp.swapaxes(q_pe.astype(f32), 1, 2) * MLA_SCALE

    def online(carry, ck, kp, mask):
        m, l, acc = carry
        s = jnp.einsum('bhtc,bkc->bhtk', q_lat, ck) + jnp.einsum('bhtr,bkr->bhtk', q_rot, kp)
        if mask is not None:
            s = jnp.where(mask, s, -jnp.inf)
        m_new = jnp.maximum(m, jnp.max(s, axis=-1))
        pr = jnp.exp(s - m_new[..., None])
        corr = jnp.exp(m - m_new)
        return (m_new, l * corr + jnp.sum(pr, axis=-1),
                acc * corr[..., None] + jnp.einsum('bhtk,bkc->bhtc', pr, ck))

    def page_step(carry, pid):
        ck = pool_ckv[layer, pid].astype(f32)
        kp = pool_kpe[layer, pid].astype(f32)
        return online(carry, ck, kp, None), None

    init = (jnp.full((B, H, T), -jnp.inf, f32), jnp.zeros((B, H, T), f32), jnp.zeros((B, H, T, KV_LORA), f32))
    carry, _ = lax.scan(page_step, init, page_table.T)
    causal = jnp.tril(jnp.ones((T, T), bool))
    _, l, acc = online(carry, ckv_new.astype(f32), kpe_new.astype(f32), causal)
    o = jnp.einsum('bhtc,chv->bthv', acc / l[..., None], w_uv.astype(f32))
    return o.astype(q_nope.dtype)

def _mixer_c(hn, positions, attend, w_in, q_norm_g, kv_norm_g, w_uq, w_ukv, w_o):
    B, L, _ = hn.shape
    cq, ckv, kpe = jnp.split(hn @ w_in, [Q_LORA, Q_LORA + KV_LORA], axis=-1)
    q = (_rmsnorm(cq, q_norm_g) @ w_uq).reshape(B, L, MLA_HEADS, QK_NOPE + QK_ROPE)
    q_nope, q_pe = q[..., :QK_NOPE], _rope(q[..., QK_NOPE:], positions)
    ckv = _rmsnorm(ckv, kv_norm_g)
    kpe = _rope(kpe[:, :, None, :], positions)[:, :, 0]
    w_r = w_ukv.reshape(KV_LORA, MLA_HEADS, QK_NOPE + V_HEAD)
    o = attend(q_nope, q_pe, ckv, kpe, w_r[..., :QK_NOPE], w_r[..., QK_NOPE:])
    return o.reshape(B, L, MLA_HEADS * V_HEAD) @ w_o, ckv, kpe

def _trunk(x, p, positions, attend, gdn_s, gdn_c, lru_s, lru_c, wa, wc, wl):
    norm_mix_g, norm_ffn_g, w_up, w_down, w_ple, w_ple_gate, norm_final_g = wl
    h = x
    o_s, o_c, o_h, o_lc, o_ckv, o_kpe = [], [], [], [], [], []
    for i in range(DEPTH):
        j = i // 2
        hn = _rmsnorm(h, norm_mix_g[i])
        if i % 2 == 0:
            mix, s_new, c_new, h_new, lc_new = _mixer_ab(hn, gdn_s[j], gdn_c[j], lru_s[j], lru_c[j],
                                                         *[w[j] for w in wa])
            o_s.append(s_new); o_c.append(c_new); o_h.append(h_new); o_lc.append(lc_new)
        else:
            mix, ckv, kpe = _mixer_c(hn, positions, functools.partial(attend, j), *[w[j] for w in wc])
            o_ckv.append(ckv); o_kpe.append(kpe)
        h = h + mix
        h = h + jnp.square(jax.nn.relu(_rmsnorm(h, norm_ffn_g[i]) @ w_up[i])) @ w_down[i]
        h = h + (p[i] @ w_ple[i]) * jax.nn.sigmoid(h @ w_ple_gate[i])
    y = _rmsnorm(h, norm_final_g)
    return (y, jnp.stack(o_s), jnp.stack(o_c), jnp.stack(o_h), jnp.stack(o_lc),
            jnp.stack(o_ckv), jnp.stack(o_kpe))

def setup_inputs(seed: int = 0) -> dict:
    key = jax.random.key(seed)
    ks = iter(jax.random.split(key, 64))
    f32 = jnp.float32
    nrm = lambda shape, scale=1.0: jax.random.normal(next(ks), shape, f32) * scale
    gain = lambda shape: 1.0 + 0.01 * jax.random.normal(next(ks), shape, f32)
    NA, NC = N_A_LAYERS, N_C_LAYERS
    n_pages = PAST_LEN // PAGE_SIZE
    n_used = DEC_BATCH * n_pages
    n_pool = n_used + max(1, n_used // 4)
    page_table = jax.random.permutation(next(ks), n_pool)[:n_used].reshape(DEC_BATCH, n_pages).astype(jnp.int32)
    dt = jnp.exp(jax.random.uniform(next(ks), (NA, GDN_HEADS), f32, math.log(1e-3), math.log(1e-1)))
    gdn_dt_bias = dt + jnp.log(-jnp.expm1(-dt))
    gdn_a_log = jnp.log(jax.random.uniform(next(ks), (NA, GDN_HEADS), f32, 1.0, 16.0))
    u = jax.random.uniform(next(ks), (NA, LRU_WIDTH), f32, 0.9, 0.999)
    lru_lambda = jnp.log(u) - jnp.log1p(-u)
    return {
        'x_prompt': nrm((BATCH, SEQ, D_MODEL)),
        'x_sample': nrm((DEC_BATCH, DEC_SEQ, D_MODEL)),
        'p_prompt': nrm((DEPTH, BATCH, SEQ, PLE_DIM)),
        'p_sample': nrm((DEPTH, DEC_BATCH, DEC_SEQ, PLE_DIM)),
        'state_gdn': nrm((NA, DEC_BATCH, GDN_HEADS, GDN_DK, GDN_DV), 0.05),
        'state_gdn_conv': nrm((NA, DEC_BATCH, CONV_W - 1, GDN_QKV)),
        'state_lru': nrm((NA, DEC_BATCH, LRU_WIDTH), 0.5),
        'state_lru_conv': nrm((NA, DEC_BATCH, CONV_W - 1, LRU_WIDTH)),
        'cache_ckv': nrm((NC, n_pool, PAGE_SIZE, KV_LORA)),
        'cache_kpe': nrm((NC, n_pool, PAGE_SIZE, QK_ROPE)),
        'page_table': page_table,
        'w_in_a': nrm((NA, D_MODEL, IN_A), D_MODEL ** -0.5),
        'conv_qkv_w': nrm((NA, CONV_W, GDN_QKV), CONV_W ** -0.5),
        'gdn_a_log': gdn_a_log,
        'gdn_dt_bias': gdn_dt_bias,
        'gdn_norm_g': gain((NA, GDN_DV)),
        'conv_lru_w': nrm((NA, CONV_W, LRU_WIDTH), CONV_W ** -0.5),
        'conv_lru_b': nrm((NA, LRU_WIDTH), 0.01),
        'lru_wa': nrm((NA, LRU_BLOCKS, LRU_BW, LRU_BW), LRU_BW ** -0.5),
        'lru_ba': nrm((NA, LRU_BLOCKS, LRU_BW), 0.01),
        'lru_wi': nrm((NA, LRU_BLOCKS, LRU_BW, LRU_BW), LRU_BW ** -0.5),
        'lru_bi': nrm((NA, LRU_BLOCKS, LRU_BW), 0.01),
        'lru_lambda': lru_lambda,
        'w_out_a': nrm((NA, MIX_A, D_MODEL), MIX_A ** -0.5),
        'w_in_c': nrm((NC, D_MODEL, IN_C), D_MODEL ** -0.5),
        'q_norm_g': gain((NC, Q_LORA)),
        'kv_norm_g': gain((NC, KV_LORA)),
        'w_uq': nrm((NC, Q_LORA, MLA_HEADS * (QK_NOPE + QK_ROPE)), Q_LORA ** -0.5),
        'w_ukv': nrm((NC, KV_LORA, MLA_HEADS * (QK_NOPE + V_HEAD)), KV_LORA ** -0.5),
        'w_o_c': nrm((NC, MLA_HEADS * V_HEAD, D_MODEL), (MLA_HEADS * V_HEAD) ** -0.5),
        'norm_mix_g': gain((DEPTH, D_MODEL)),
        'norm_ffn_g': gain((DEPTH, D_MODEL)),
        'w_up': nrm((DEPTH, D_MODEL, D_FF), D_MODEL ** -0.5),
        'w_down': nrm((DEPTH, D_FF, D_MODEL), D_FF ** -0.5),
        'w_ple': nrm((DEPTH, PLE_DIM, D_MODEL), PLE_DIM ** -0.5),
        'w_ple_gate': nrm((DEPTH, D_MODEL, D_MODEL), D_MODEL ** -0.5),
        'norm_final_g': gain((D_MODEL,)),
    }

def reference(x_prompt, x_sample, p_prompt, p_sample, state_gdn, state_gdn_conv, state_lru, state_lru_conv,
              cache_ckv, cache_kpe, page_table,
              w_in_a, conv_qkv_w, gdn_a_log, gdn_dt_bias, gdn_norm_g, conv_lru_w, conv_lru_b,
              lru_wa, lru_ba, lru_wi, lru_bi, lru_lambda, w_out_a,
              w_in_c, q_norm_g, kv_norm_g, w_uq, w_ukv, w_o_c,
              norm_mix_g, norm_ffn_g, w_up, w_down, w_ple, w_ple_gate, norm_final_g):
    wa = (w_in_a, conv_qkv_w, gdn_a_log, gdn_dt_bias, gdn_norm_g, conv_lru_w, conv_lru_b,
          lru_wa, lru_ba, lru_wi, lru_bi, lru_lambda, w_out_a)
    wc = (w_in_c, q_norm_g, kv_norm_g, w_uq, w_ukv, w_o_c)
    wl = (norm_mix_g, norm_ffn_g, w_up, w_down, w_ple, w_ple_gate, norm_final_g)
    b_p, seq = x_prompt.shape[0], x_prompt.shape[1]
    t_s = x_sample.shape[1]
    past = page_table.shape[1] * PAGE_SIZE

    def zeros_like_batch(ref, b):
        return jnp.zeros((ref.shape[0], b) + ref.shape[2:], ref.dtype)

    def attend_prompt(layer, q_nope, q_pe, ckv, kpe, w_uk, w_uv):
        return _attend_prompt(q_nope, q_pe, ckv, kpe, w_uk, w_uv)

    def attend_sample(layer, q_nope, q_pe, ckv, kpe, w_uk, w_uv):
        return _attend_paged(q_nope, q_pe, ckv, kpe, w_uk, w_uv, cache_ckv, cache_kpe, layer, page_table)

    y_prompt, gdn_p, gdn_conv_p, lru_p, lru_conv_p, ckv_p, kpe_p = _trunk(
        x_prompt, p_prompt, jnp.arange(seq), attend_prompt,
        zeros_like_batch(state_gdn, b_p), zeros_like_batch(state_gdn_conv, b_p),
        zeros_like_batch(state_lru, b_p), zeros_like_batch(state_lru_conv, b_p), wa, wc, wl)
    y_sample, gdn_s, gdn_conv_s, lru_s, lru_conv_s, ckv_s, kpe_s = _trunk(
        x_sample, p_sample, past + jnp.arange(t_s), attend_sample,
        state_gdn, state_gdn_conv, state_lru, state_lru_conv, wa, wc, wl)
    return (y_prompt, y_sample, gdn_p, gdn_s, gdn_conv_p, gdn_conv_s, lru_p, lru_s,
            lru_conv_p, lru_conv_s, ckv_p, ckv_s, kpe_p, kpe_s)


_drawn_inputs = setup_inputs


def setup_inputs(seed=0):
    import zlib

    import numpy as np

    out = dict(_drawn_inputs(seed))
    spreads = {}
    factors = {'cache_kpe': 27.88,
     'gdn_norm_g': 26.566,
     'lru_ba': 33.117,
     'lru_bi': 26.209,
     'q_norm_g': 200.0,
     'kv_norm_g': 158.512,
     'norm_mix_g': 3.536,
     'norm_ffn_g': 16.988,
     'norm_final_g': 180.251,
     'conv_lru_b': 6.793,
     'p_prompt': 8.0,
     'p_sample': 8.0,
     'cache_ckv': 7.253,
     'w_ple': 8.0,
     'w_ple_gate': 8.0}
    for name, (base, spread) in spreads.items():
        noise = np.random.default_rng([zlib.crc32(name.encode()), seed]).standard_normal(out[name].shape)
        drawn = base * np.exp(spread * noise) if base else spread * noise
        out[name] = __import__('jax').numpy.asarray(drawn.astype(out[name].dtype))
    for name, factor in factors.items():
        out[name] = (out[name] * factor).astype(out[name].dtype)
    return out
```

```python
import numpy as np
from contextlib import ExitStack

import concourse.bass as bass
from concourse import mybir

F32 = mybir.dt.float32
F32R = mybir.dt.float32r
I32 = mybir.dt.int32
ALU = mybir.AluOpType
ACT = mybir.ActivationFunctionType
AX = mybir.AxisListType
ds = bass.ds

D_MODEL, SEQ, BS, TS = 2048, 256, 8, 4
NS = BS * TS
NT = SEQ + NS
DEPTH, PLE = 2, 256
HG, DK = 8, 128
QKV, LRU = 3 * HG * DK, 1024
KT = D_MODEL // 128
HM, NOPE, ROPE, VH = 16, 128, 64, 128
QLORA, KVLORA = 512, 512
DFF = 8192
NPG, PAGE = 8, 128
PAST = NPG * PAGE
EPS = 1e-6
MLA_SCALE = (NOPE + ROPE) ** -0.5
CHUNK = 128
LEVELS = 7
PRE = 3 + SEQ + BS * (3 + TS)
PADS = PRE - BS * 7

C_MIX, C_FFN, C_FIN, C_CONV = 0, 32, 64, 80
C_LCONV = C_CONV + 96
C_LB, C_BA, C_BI, C_LAM = C_LCONV + 32, C_LCONV + 40, C_LCONV + 48, C_LCONV + 56
C_GN, C_QN, C_H0 = C_LCONV + 64, C_LCONV + 65, C_LCONV + 73
NPAR = C_H0 + 64

S_QKV = 0
S_Z = S_QKV + 24
S_BA = S_Z + 8
S_LX = S_BA + 2
S_LY = S_LX + 8
S_OUT = S_LY + 8
S_FFN0 = S_OUT + 16
S_PLE0 = S_FFN0 + 128
S_GATE0 = S_PLE0 + 2
S_INC = S_GATE0 + 16
S_KPE = S_INC + 8
S_UQ = S_KPE + 2
S_UKV = S_UQ + 8
S_OV = S_UKV + 8
S_WO = S_OV + 4
S_FFN1 = S_WO + 16
S_PLE1 = S_FFN1 + 128
S_GATE1 = S_PLE1 + 2
S_END = S_GATE1 + 16


def constants():
    f = np.float32
    i = np.arange(128)
    lev = np.zeros((128, LEVELS, 128), f)
    for n in range(LEVELS):
        s = 1 << n
        same = (i[:, None] // (2 * s)) == (i[None, :] // (2 * s))
        lev[:, n, :] = same & ((i[:, None] // s) % 2 == 0) & ((i[None, :] // s) % 2 == 1)
    up = (i[:, None] <= i[None, :]).astype(f)
    j = np.arange(NS)
    up_s = np.zeros((128, NS), f)
    up_s[:NS] = (j[:, None] <= j[None, :]) & (j[:, None] // TS == j[None, :] // TS)
    own = np.zeros((128, BS), f)
    own[:NS] = j[:, None] // TS == np.arange(BS)[None, :]
    keep = np.ones((128, NT), f)
    keep[:, 0:SEQ:CHUNK] = 0
    keep[:, SEQ::TS] = 0
    c0 = np.concatenate([lev.reshape(128, -1), up, up_s, own, keep], axis=1)
    causal = np.where(i[:, None] >= i[None, :], 0.0, -1e30).astype(f)
    cm3 = np.concatenate([causal, np.zeros((128, 128), f), causal], axis=1)
    t = i % TS
    b2 = i // 64
    c8 = np.arange(2 * TS)
    new = np.where((c8[None, :] // TS == b2[:, None]) & (c8[None, :] % TS <= t[:, None]), 0.0, -1e30).astype(f)
    half = ROPE // 2
    inv = (f(10000.0) ** (-np.arange(half, dtype=f) / f(half))).astype(f)
    pos = np.concatenate([np.arange(SEQ), np.tile(PAST + np.arange(TS), BS)]).astype(f)
    ang = (inv[i % half][:, None] * pos[None, :]).astype(f)
    rot = np.zeros((128, 128), f)
    for m in range(128):
        if (m % ROPE) < half:
            rot[m + half, m] = -1.0
        else:
            rot[m - half, m] = 1.0
    c1 = np.concatenate([cm3, new, np.cos(ang).astype(f), np.sin(ang).astype(f), rot], axis=1)
    return np.eye(128, dtype=f), c0.astype(f), c1.astype(f)


NC0 = LEVELS * 128 + 128 + NS + BS + NT
NC1 = 3 * 128 + 2 * TS + 2 * NT + 128


STEPS = {
    "pe_steps": """par_tr hist_tr cs_tr:2 lo_tr l2_mm:2 scal_tr bb_mm:2 on_mm c_mm:2 kp_rot ctok_tr:4 qp_rot""",
    "act_steps": """identr_set lam_ln lat_done lroot_done l2_sq:2 l2_rt:2 beta_e a_ln eg_done kde_done on_sq on_rt c_sq:2
    c_rt cqh_done ckh_done ach_done atth_done""",
    "dve_steps": """par_done lam_abs nb_done hist_done ba_done csr_done:2 lm_done lt_done lo_done:2 ob_done lrow_done
    l2_inv:2 l2_done:2 beta_done a_abs gc_done dl_done nbg_done scal_done bb_done:2 on_inv og_done kpr_done
    c_inv cn_done cql_done kpe_done ckl_done ctok_done:6 qp_done acl_done attl_done""",
}


def bases():
    base = {}
    for steps in STEPS.values():
        total = 0
        for step in steps.split():
            name, _, count = step.partition(":")
            base[name] = total
            total += int(count or 1)
    return base


BASE = bases()


class Own:

    def __init__(self, eng, sem):
        self.eng, self.sem, self.n, self.turns = eng, sem, 0, []

    def after(self, ins):
        ins.then_inc(self.sem, 1)
        self.n += 1
        value = self.n
        for t, per in self.turns:
            value = value + t * per
        self.eng.wait_ge(self.sem, value)

    def loop(self, count, per, body, first=0):
        n0 = self.n
        with self.eng.Fori(first, count) as t:
            if per:
                self.turns.append((t, per))
                self.n = n0 - first * per
            body(t)
            if per:
                self.turns.pop()
                assert self.n - (n0 - first * per) == per, (self.n - n0 + first * per, per)
        self.n = n0 + (count - first) * per


class Row:

    def __init__(self, nc, start):
        self.nc, self.at = nc, start

    def next(self, name, shape):
        t = self.nc.alloc_sbuf_tensor_at(name, [128] + shape, F32, offset=self.at)
        self.at += 4 * int(np.prod(shape))
        return t


class Memory:
    pass


def semaphores(nc, ctx, m):
    def sem(name):
        return ctx.enter_context(nc.semaphore(name))

    def sems(names):
        return [sem(name) for name in names.split()]

    m.l_id, m.l_par, m.l_x, m.l_hist, m.l_ab, m.l_pg = sems(
        "l_id l_par l_x l_hist l_ab l_pg")
    m.l_c0, m.l_c1, m.l_p, m.o_cs, m.o_lru, m.o_s2 = sems(
        "l_c0 l_c1 l_p o_cs o_lru o_s2")
    m.o_s8, m.o_c, m.o_y, m.cache_full, m.s8_full, m.wh_done = sems(
        "o_s8 o_c o_y cache_full s8_full wh_done")
    m.split_done, m.slot_used, m.act_own, m.dve_own, m.pool_own, m.ones_set = sems(
        "split_done slot_used act_own dve_own pool_own ones_set")
    m.x_tr, m.h_ready, m.fh_done, m.fl_done, m.ss_done, m.ss_mm = sems(
        "x_tr h_ready fh_done fl_done ss_done ss_mm")
    m.r_inv, m.r_ready, m.pre_ready, m.pre_saved, m.hist_in, m.conv_done = sems(
        "r_inv r_ready pre_ready pre_saved hist_in conv_done")
    m.conv_act, m.z_raw, m.z_act, m.ly_raw, m.ly_act, m.gate_mm = sems(
        "conv_act z_raw z_act ly_raw ly_act gate_mm")
    m.gate_act, m.mixh_done, m.mixl_done, m.head_end, m.g_stage, m.g_eb = sems(
        "gate_act mixh_done mixl_done head_end g_stage g_eb")
    m.g_diff, m.g_dec, m.g_decb, m.g_tr, m.g_gram, m.g_bt1 = sems(
        "g_diff g_dec g_decb g_tr g_gram g_bt1")
    m.g_t1, m.g_lt, m.g_q, m.g_qc, m.g_tb, m.g_inv = sems(
        "g_t1 g_lt g_q g_qc g_tb g_inv")
    m.g_v0, m.g_vn0, m.g_xs, m.g_xt, m.g_xtr, m.g_s1 = sems(
        "g_v0 g_vn0 g_xs g_xt g_xtr g_s1")
    m.g_s1c, m.g_x1, m.g_v1, m.g_vn1, m.g_rs, m.g_vs = sems(
        "g_s1c g_x1 g_v1 g_vn1 g_rs g_vs")
    m.g_vns, m.g_vm, m.g_s2, m.g_o, m.g_ds, m.s2_done = sems(
        "g_vns g_vm g_s2 g_o g_ds s2_done")
    m.s8_done, m.u_done, m.fuh_done, m.fu_done, m.p_tr, m.pt_done = sems(
        "s8_done u_done fuh_done fu_done p_tr pt_done")
    m.ph_done, m.pl_done, m.ple_mm, m.ple_ev, m.gt_raw, m.gt_act = sems(
        "ph_done pl_done ple_mm ple_ev gt_raw gt_act")
    m.c_raw, m.uq_ev, m.kv_t, m.kv_tc, m.kv_k, m.kv_q = sems(
        "c_raw uq_ev kv_t kv_tc kv_k kv_q")
    m.kv_ev, m.pa_stage, m.pa_s, m.pa_m, m.pa_e, m.pa_p = sems(
        "kv_ev pa_stage pa_s pa_m pa_e pa_p")
    m.pa_t, m.pa_tc, m.pa_o, m.pa_ah, m.patt_out, m.sa_stage = sems(
        "pa_t pa_tc pa_o pa_ah patt_out sa_stage")
    m.sa_t, m.sa_ckc, m.sa_kpc, m.sa_s, m.sa_nt, m.sa_m = sems(
        "sa_t sa_ckc sa_kpc sa_s sa_nt sa_m")
    m.sa_e, m.sa_p, m.sa_pt, m.sa_ptc, m.spv_mm, m.sa_acc = sems(
        "sa_e sa_p sa_pt sa_ptc spv_mm sa_acc")
    m.yn_done, m.y_tr, m.y_done = sems(
        "yn_done y_tr y_done")
    m.par_tr = m.hist_tr = m.cs_tr = m.lo_tr = m.l2_mm = m.scal_tr = m.bb_mm = m.on_mm = m.c_mm = \
        m.kp_rot = m.ctok_tr = m.qp_rot = sem("pe_steps")
    m.identr_set = m.lam_ln = m.lat_done = m.lroot_done = m.l2_sq = m.l2_rt = m.beta_e = m.a_ln = \
        m.eg_done = m.kde_done = m.on_sq = m.on_rt = m.c_sq = m.c_rt = m.cqh_done = m.ckh_done = m.ach_done \
        = m.atth_done = sem("act_steps")
    m.par_done = m.lam_abs = m.nb_done = m.hist_done = m.ba_done = m.csr_done = m.lm_done = m.lt_done = \
        m.lo_done = m.ob_done = m.lrow_done = m.l2_inv = m.l2_done = m.beta_done = m.a_abs = m.gc_done = \
        m.dl_done = m.nbg_done = m.scal_done = m.bb_done = m.on_inv = m.og_done = m.kpr_done = m.c_inv = \
        m.cn_done = m.cql_done = m.kpe_done = m.ckl_done = m.ctok_done = m.qp_done = m.acl_done = \
        m.attl_done = sem("dve_steps")
    m.w_full = [sem(f"w_full{i}") for i in range(4)]
    m.gw_full = [sem(f"gw_full{i}") for i in range(2)]


def memory(nc, ctx):
    m = Memory()
    m.nc = nc
    semaphores(nc, ctx, m)

    def at(name, offset, shape, dt=F32):
        return nc.alloc_sbuf_tensor_at(name, [128] + shape, dt, offset=offset)

    K = 1024
    o = (nc.sbuf_base + 31) // 32 * 32
    end = nc.sbuf_usable_end // 32 * 32 - 320
    m.W = at("W", o, [4, 2048])
    m.Wh = at("Wh", o + 32 * K, [2, 2048], F32R)
    m.Wl = at("Wl", o + 48 * K, [2, 2048], F32R)
    o += 64 * K
    T1 = NT * 4
    R = KT * T1
    m.hT = at("hT", o, [KT, NT])
    oA, oB = o + R, o + 3 * R
    oAl, oBl = oA + R, oB + R
    m.Ah, m.Al = at("Ah", oA, [KT, NT], F32R), at("Al", oAl, [KT, NT], F32R)
    m.Bh, m.Bl = at("Bh", oB, [KT, NT], F32R), at("Bl", oBl, [KT, NT], F32R)
    o += 5 * R
    m.ident = at("ident", o, [128])
    m.identr = at("identr", o + 512, [128], F32R)
    m.ones = at("ones", o + 1024, [128])
    m.par = at("par", o + 1536, [320])
    o += 1536 + 1280
    oR = o
    m.rB = at("rB", o, [NT])
    m.ssacc = at("ssacc", o + T1, [2, NT])
    m.sqt = at("sqt", o + 3 * T1, [2, NT])
    o += 5 * T1
    oL = o
    m.betaR = at("betaR", o, [NT])
    m.gR = at("gR", o + T1, [NT])
    m.gcR = at("gcR", o + 2 * T1, [NT])
    m.eR = at("eR", o + 3 * T1, [NT])
    o += 4 * T1
    m.conv = at("conv", o, [3 * HG, NT])
    m.xtok = at("xtok", o, [2, D_MODEL])
    m.xstok = at("xstok", o + 16 * K, [D_MODEL])
    o += 3 * HG * T1
    m.z = at("z", o, [HG, NT])
    m.hrow = at("hrow", o, [QKV + LRU])
    o += HG * T1
    oX = o
    m.xb = at("xb", o, [8, NT])
    m.ly = at("ly", o + 8 * T1, [8, NT])
    m.prow = at("prow", o + 8 * T1, [4, 128])
    m.hist = at("hist", oB, [32, 24])
    m.cs = at("cs", oB + 3 * K, [32, 27])
    m.pre = at("pre", oB + 8 * T1, [2, 2, PRE])
    m.acc = at("acc", oBl, [2, 2, PRE])
    m.lm = at("lm", oA, [2, 8, NT])
    m.la = at("la", oAl, [8, NT])
    m.lt = at("lt", oAl + 8 * T1, [8, NT])
    m.csrow = at("csrow", oAl, [4096])
    m.gw = at("gw", oBl, [2, 2, 128])
    m.cst0 = at("cst0", oBl + 2 * K, [NC0])
    m.lsp = at("lsp", oB + 6656, [4, 16])
    m.lo = at("lo", oB + 7168, [72])
    m.lrow = at("lrow", oB + 7680, [128])
    m.sqg = at("sqg", oA, [16, NT])
    m.GB = at("GB", oA, [HG, NT])
    m.BB = at("BB", oA + 8 * T1, [HG, NT])
    m.S8 = at("S8", oAl, [BS, 128])
    m.Vm = at("Vm", oAl + 4096, [BS, 128])
    m.Bt = at("Bt", oAl + 8192, [LEVELS, 2, 128])
    m.kd = at("kd", oAl + 15360, [3, 128])
    m.vb = at("vb", oAl + 16896, [3, 128])
    p = Row(nc, oX)
    m.qkv = p.next("qkv", [3, NT])
    m.dec = p.next("dec", [NT])
    m.decU = p.next("decU", [NT])
    m.decB = p.next("decB", [NT])
    m.AQ = p.next("AQ", [2, NT])
    m.Eb = p.next("Eb", [NT])
    m.qe = p.next("qe", [NT])
    m.TT = p.next("TT", [2, 2, 128])
    m.Qs = p.next("Qs", [2, 128])
    m.vn = p.next("vn", [3, 128])
    m.S1 = p.next("S1", [128])
    m.Ts = p.next("Ts", [2, NS])
    m.Qss = p.next("Qss", [NS])
    m.Bts = p.next("Bts", [2, NS])
    m.kq = p.next("kq", [BS, 2, TS])
    m.XT = p.next("XT", [NS])
    m.oS = p.next("oS", [NS])
    assert p.at <= oX + 16 * T1
    p = Row(nc, oB)
    m.S2 = p.next("S2", [128])
    m.R1 = p.next("R1", [128])
    m.Rs = p.next("Rs", [128])
    m.scal = p.next("scal", [HG, 12])
    m.sc1 = p.next("sc1", [12])
    assert p.at <= oB + 6656
    o = oL
    m.u = at("u", o, [2, NT])
    m.usq = at("usq", o + 2 * T1, [2, NT])
    m.gt = at("gt", o + 4 * T1, [2, NT])
    m.ptok = at("ptok", o + 6 * T1, [3, PLE])
    m.pTh = at("pTh", o + 6 * T1 + 3072, [2, NT], F32R)
    m.pTl = at("pTl", o + 8 * T1 + 3072, [2, NT], F32R)
    m.ple = at("ple", o + 10 * T1 + 3072, [KT, NT])
    m.ytok = at("ytok", oA, [3, D_MODEL])
    o = oL
    m.cst1 = at("cst1", o, [NC1])
    o += (NC1 * 4 + 31) // 32 * 32
    m.cqh = at("cqh", o, [4, NT], F32R)
    m.cql = at("cql", o + 4 * T1, [4, NT], F32R)
    m.c = at("c", o + 8 * T1, [8, NT])
    m.qlat = at("qlat", o, [4, HM, NS])
    m.wukT = at("wukT", o + 8192, [2, 512])
    oq = o + 8192
    m.qs2 = at("qs2", oq, [2, SEQ])
    m.qp2 = at("qp2", oq + 2048, [SEQ])
    m.vs2 = at("vs2", oq + 3072, [2, 256])
    assert oq + 5120 <= o + 12 * T1
    m.qrs = at("qrs", oq, [BS, HM, TS])
    m.qls = at("qls", oq + 2048, [4, 2, HM, TS])
    m.qrs2 = at("qrs2", oq + 4096, [2, HM, TS])
    o += 16 * T1
    m.kpR = at("kpR", oA + 17 * T1, [NT])
    m.kpe = at("kpe", o, [NT])
    o += T1
    m.ckh = at("ckh", o, [4, NT], F32R)
    m.ckl = at("ckl", o + 4 * T1, [4, NT], F32R)
    m.sc2 = at("sc2", o, [2, 384])
    m.PT2 = at("PT2", o + 3072, [2, 384])
    m.mx2 = at("mx2", o + 6144, [4, 4])
    m.PT = at("PT", o, [NPG, 128])
    m.PTn = at("PTn", o + 4096, [128])
    m.ckn = at("ckn", o + 4608, [512])
    m.ckns = at("ckns", o + 6656, [5, 2 * TS])
    m.mx8 = at("mx8", o + 6848, [4])
    o += 8 * T1
    m.qn = at("qn", o, [HM, NT])
    m.qp = at("qp", o + HM * T1, [8, NT])
    o -= 2 * K
    m.ckT = at("ckT", o, [4, PAST])
    m.kpT = at("kpT", o + 16 * K, [PAST])
    m.accT = at("accT", o + 20 * K, [4, HM, NS])
    assert o + 20 * K + 8192 <= end, (o + 20 * K + 8192, end)
    m.ach = at("ach", o, [4, HM, NS], F32R)
    m.acl = at("acl", o + 8 * K, [4, HM, NS], F32R)
    m.sc8 = at("sc8", oR, [PAST + 2 * TS])
    m.csq = at("csq", oA, [8, NT])
    m.rtmp = at("rtmp", oA, [8, NT])
    m.rc = at("rc", oA + 8 * T1, [2, NT])
    m.ctok = at("ctok", oA + 10 * T1, [3, 576])
    m.kno = at("kno", oB, [HM, SEQ])
    m.vtok = at("vtok", oB + 16 * K, [2, HM * VH])
    m.CK = at("CK", oB, [2, NPG, KVLORA])
    m.KP = at("KP", oB + 32 * K, [2, NPG, ROPE])
    m.pgs = at("pgs", end + 64, [64], I32)
    m.alog = at("alog", end, [4])

    m.ps = ctx.enter_context(nc.psum_tensor("ps", [128, 8, 512], F32))
    return m




def pieces(slot, w, x):
    if S_BA <= slot < S_BA + 2:
        return [(w[:, 0:128].rearrange("p (k g c) -> p k g c", k=8, g=2),
                 x[:, 0:512].rearrange("p (k g c) -> p k g c", k=8, g=2)[:, :, :, 0:8])]
    if S_KPE <= slot < S_KPE + 2:
        return [(w[:, 0:512].rearrange("p (k c) -> p k c", k=8).unsqueeze(2).to_broadcast([128, 8, 2, ROPE]),
                 x[:, 0:1024].rearrange("p (k g c) -> p k g c", k=8, g=2))]
    if S_UQ <= slot < S_UQ + 8:
        heads = w[:, 0:1536].rearrange("p (k h n) -> p k h n", k=4, h=2)
        blocks = x[:, 0:1536].rearrange("p (k n) -> p k n", k=4)
        return [(heads[:, :, :, 0:NOPE], blocks[:, :, 0:256].rearrange("p k (h n) -> p k h n", h=2)),
                (heads[:, :, :, NOPE:], blocks[:, :, 256:384].rearrange("p k (h n) -> p k h n", h=2))]
    return [(w, x)]


def ring(S, i):
    return (S + i) % 4


def sync_program(sp, m, a):

    def load(S, i, it, src, view=None):
        j = ring(S, i)
        if not (isinstance(it, int) and S + i + 4 * it < 4):
            sp.wait_ge(m.split_done, it * 4 + (S + i - 3))
        dst = m.W[:, j, :].rearrange("p (k n) -> p k n", k=8) if view is None else view(m.W[:, j, :])
        sp.dma_start(dst, src).then_inc(m.w_full[j], 16)

    def k16(S, w, col0, count, it0=0, rows=None, first=0):
        wv = w.rearrange("(k p) n -> p k n", p=128)

        def turn(t):
            for i in range(4):
                r = slice(8 * (i % 2), 8 * (i % 2) + 8) if rows is None else ds(rows + 8 * (i % 2), 8)
                load(S, i, it0 + t, wv[:, r, ds(t * 512 + (col0 + 256 * (i // 2)), 256)])
        for t in range(first):
            turn(t)
        with sp.Fori(first, count) as t:
            turn(t)

    def small(dst, src, s):
        sp.dma_start(dst, src).then_inc(s, 16)

    small(m.ident[:], a["ident"], m.l_id)
    small(m.prow[0:32, 0, :], a["norm_mix_g"].rearrange("l (k p) -> (l k) p", p=128), m.l_par)
    small(m.prow[32:64, 0, :], a["norm_ffn_g"].rearrange("l (k p) -> (l k) p", p=128), m.l_par)
    small(m.prow[64:80, 0, :], a["norm_final_g"].rearrange("(k p) -> k p", p=128), m.l_par)
    small(m.prow[0:96, 1, :], a["conv_qkv_w"][0].rearrange("w (k p) -> (w k) p", p=128), m.l_par)
    small(m.prow[0:32, 2, :], a["conv_lru_w"][0].rearrange("w (k p) -> (w k) p", p=128), m.l_par)
    small(m.prow[32:40, 2, :], a["conv_lru_b"].rearrange("l (k p) -> (l k) p", p=128), m.l_par)
    small(m.prow[40:48, 2, :], a["lru_ba"][0], m.l_par)
    small(m.prow[48:56, 2, :], a["lru_bi"][0], m.l_par)
    small(m.prow[56:64, 2, :], a["lru_lambda"].rearrange("l (k p) -> (l k) p", p=128), m.l_par)
    small(m.prow[64:65, 2, :], a["gdn_norm_g"], m.l_par)
    small(m.prow[65:69, 2, :], a["q_norm_g"].rearrange("l (k p) -> (l k) p", p=128), m.l_par)
    small(m.prow[69:73, 2, :], a["kv_norm_g"].rearrange("l (k p) -> (l k) p", p=128), m.l_par)
    small(m.prow[0:64, 3, :], a["state_lru"][0].rearrange("b (k p) -> (b k) p", p=128), m.l_par)
    small(m.xtok[:], a["x_prompt"][0].rearrange("(c p) n -> p c n", p=128), m.l_x)
    small(m.xstok[0:NS, :], a["x_sample"].rearrange("b t n -> (b t) n"), m.l_x)
    small(m.hrow[0:24, 0:QKV], a["state_gdn_conv"][0].rearrange("b w n -> (b w) n"), m.l_hist)
    small(m.hrow[0:24, QKV:], a["state_lru_conv"][0].rearrange("b w n -> (b w) n"), m.l_hist)
    small(m.alog[0:8, 0:1], a["gdn_a_log"][0].unsqueeze(1), m.l_ab)
    small(m.alog[0:8, 1:2], a["gdn_dt_bias"][0].unsqueeze(1), m.l_ab)
    small(m.pgs[0:1, :], a["page_table"].rearrange("b n -> (b n)").unsqueeze(0), m.l_pg)

    w = a["w_in_a"][0]
    k16(S_QKV, w, 0, 6, first=1)
    k16(S_Z, w, QKV, 2)
    wv = w.rearrange("(k p) n -> p k n", p=128)
    c0 = QKV + HG * DK
    for i in range(2):
        load(S_BA, i, 0, wv[:, 8 * i:8 * i + 8, c0:c0 + 16],
             lambda x: x[:, 0:128].rearrange("p (k c) -> p k c", k=8))
    k16(S_LX, w, c0 + 16, 2)
    k16(S_LY, w, c0 + 16 + LRU, 2)

    wo = a["w_out_a"][0]
    wov = wo.rearrange("(k p) n -> p k n", p=128)
    for i in range(4):
        load(S_OUT, i, 0, wov[:, 8 * (i % 2):8 * (i % 2) + 8, 256 * (i // 2):256 * (i // 2) + 256])

    sp.wait_ge(m.csr_done, BASE["csr_done"] + 2)
    small(a["gdn_conv_p"][0, 0], m.csrow[0:3, 0:QKV], m.o_cs)
    small(a["lru_conv_p"][0, 0], m.csrow[0:3, QKV:], m.o_cs)
    small(a["gdn_conv_s"][0].rearrange("b w n -> (b w) n"), m.csrow[3:27, 0:QKV], m.o_cs)
    small(a["lru_conv_s"][0].rearrange("b w n -> (b w) n"), m.csrow[3:27, QKV:], m.o_cs)

    def gates(t):
        for u in range(2):
            if not isinstance(t, int):
                sp.wait_ge(m.gate_mm, 2 * t + (u - 1))
            sp.dma_start(m.gw[:, u, 0, :], a["lru_wa"][0, ds(2 * t + u, 1), :, :].rearrange("k p n -> (k p) n")
                         ).then_inc(m.gw_full[u], 16)
            sp.dma_start(m.gw[:, u, 1, :], a["lru_wi"][0, ds(2 * t + u, 1), :, :].rearrange("k p n -> (k p) n")
                         ).then_inc(m.gw_full[u], 16)
    sp.wait_ge(m.conv_act, 16)
    gates(0)
    small(m.cst0[:], a["cst0"], m.l_c0)
    with sp.Fori(1, 4) as t:
        gates(t)
    sp.wait_ge(m.lrow_done, BASE["lrow_done"] + 1)
    small(a["lru_p"][0, 0].rearrange("(k p) -> k p", p=128), m.lrow[0:8, :], m.o_lru)
    small(a["lru_s"][0].rearrange("b (k p) -> (b k) p", p=128), m.lrow[8:72, :], m.o_lru)

    sp.wait_ge(m.l2_done, BASE["l2_done"] + 2)
    st = a["state_gdn"][0].rearrange("b h k v -> k b h v")
    so = a["gdn_s"][0].rearrange("b h k v -> k b h v")

    def head(t):
        if not isinstance(t, int):
            sp.wait_ge(m.o_s8, 16 * t)
            sp.wait_ge(m.o_s2, 16 * t)
        sp.dma_start(m.S8[:], st[:, :, ds(t, 1), :].rearrange("k b h v -> k b (h v)")).then_inc(m.s8_full, 16)
        sp.wait_ge(m.s2_done, t + 1)
        sp.dma_start(a["gdn_p"][0, 0, ds(t, 1), :, :].rearrange("h k v -> (h k) v"), m.S2[:]).then_inc(m.o_s2, 16)
        sp.wait_ge(m.s8_done, t + 1)
        sp.dma_start(so[:, :, ds(t, 1), :].rearrange("k b h v -> k b (h v)"), m.S8[:]).then_inc(m.o_s8, 16)
    head(0)
    with sp.Fori(1, HG) as t:
        head(t)

    with sp.Fori(1, 4) as t:
        for i in range(4):
            load(S_OUT, i, t, wov[:, 8 * (i % 2):8 * (i % 2) + 8, ds(t * 512 + 256 * (i // 2), 256)])

    def mlp_and_inputs(layer, S, S_P, S_G):
        up, down = a["w_up"][layer], a["w_down"][layer]
        pp = a["p_prompt"][layer, 0].rearrange("(c p) n -> p c n", p=128)
        if layer == 0:
            sp.wait_ge(m.mixl_done, 2)
        else:
            sp.wait_ge(m.attl_done, BASE["attl_done"] + 1)
        small(m.ptok[:, 0:2, :], pp, m.l_p)
        small(m.ptok[0:NS, 2, :], a["p_sample"][layer].rearrange("b t n -> (b t) n"), m.l_p)
        upv = up.rearrange("(k p) n -> p k n", p=128)
        dnv = down.rearrange("(k p) n -> p k n", p=128)
        with sp.Fori(0, 4) as c:
            with sp.Fori(0, 4) as t:
                for i in range(4):
                    load(S, i, c * 8 + t, upv[:, 8 * (i % 2):8 * (i % 2) + 8,
                                              ds(c * 2048 + t * 512 + 256 * (i // 2), 256)])
            with sp.Fori(0, 4) as t:
                for i in range(4):
                    load(S, i, c * 8 + t + 4, dnv[:, ds(c * 16 + 8 * (i % 2), 8), ds(t * 512 + 256 * (i // 2), 256)])
        pv = a["w_ple"][layer].rearrange("(k p) n -> p k n", p=128)
        for i in range(2):
            load(S_P, i, 0, pv[:, :, 1024 * i:1024 * i + 1024], lambda x: x.rearrange("p (k n) -> p k n", k=2))
        k16(S_G, a["w_ple_gate"][layer], 0, 4)

    mlp_and_inputs(0, S_FFN0, S_PLE0, S_GATE0)

    w = a["w_in_c"][0]
    k16(S_INC, w, 0, 2)
    sp.wait_ge(m.pl_done, 1)
    small(m.cst1[:], a["cst1"], m.l_c1)
    wv = w.rearrange("(k p) n -> p k n", p=128)
    for i in range(2):
        load(S_KPE, i, 0, wv[:, 8 * i:8 * i + 8, 1024:1088],
             lambda x: x[:, 0:512].rearrange("p (k c) -> p k c", k=8))
    wq = a["w_uq"][0].rearrange("(k p) n -> p k n", p=128)
    with sp.Fori(0, 2) as t:
        for i in range(4):
            load(S_UQ, i, t, wq[:, :, ds(t * 1536 + 384 * i, 384)],
                 lambda x: x[:, 0:1536].rearrange("p (k n) -> p k n", k=4))
    wk = a["w_ukv"][0].rearrange("(k p) n -> p k n", p=128)
    with sp.Fori(0, 2) as t:
        for i in range(4):
            load(S_UKV, i, t, wk[:, :, ds(t * 2048 + 512 * i, 512)], lambda x: x.rearrange("p (k n) -> p k n", k=4))
    sp.wait_ge(m.ctok_done, BASE["ctok_done"] + 6)
    small(a["ckv_p"][0, 0].rearrange("(c p) n -> p c n", p=128), m.ctok[:, 0:2, 0:512], m.o_c)
    small(a["ckv_s"][0].rearrange("b t n -> (b t) n"), m.ctok[0:NS, 2, 0:512], m.o_c)
    small(a["kpe_p"][0, 0].rearrange("(c p) n -> p c n", p=128), m.ctok[:, 0:2, 512:576], m.o_c)
    small(a["kpe_s"][0].rearrange("b t n -> (b t) n"), m.ctok[0:NS, 2, 512:576], m.o_c)
    wk4 = a["w_ukv"][0].rearrange("(k p) (h g n) -> p k h g n", p=128, h=HM, g=2)
    for i in range(4):
        if i == 2:
            cache_pages(sp, m, a)
        load(S_OV, i, 0, wk4[:, i, :, 1, :], lambda x: x.rearrange("p (h n) -> p h n", h=HM))
    k16(S_WO, a["w_o_c"][0], 0, 4)
    mlp_and_inputs(1, S_FFN1, S_PLE1, S_GATE1)

    sp.wait_ge(m.y_done, 12)
    small(a["y_prompt"][0].rearrange("(c p) n -> p c n", p=128), m.ytok[:, 0:2, :], m.o_y)
    small(a["y_sample"].rearrange("b t n -> (b t) n"), m.ytok[0:NS, 2, :], m.o_y)
    for s, n in ((m.o_cs, 4), (m.o_lru, 2), (m.o_s2, HG), (m.o_s8, HG), (m.o_c, 4), (m.o_y, 2)):
        sp.wait_ge(s, 16 * n)


def cache_pages(sp, m, a):
    ck, kp = a["cache_ckv"][0], a["cache_kpe"][0]
    sp.wait_ge(m.l_pg, 16)
    sp.wait_ge(m.patt_out, 8)

    def pair(t):
        if not isinstance(t, int):
            sp.wait_ge(m.spv_mm, t)
        for b in range(2):
            for n in range(NPG):
                page = sp.value_load(m.pgs[0:1, ds(t * 2 * NPG + (b * NPG + n), 1)], min_val=0,
                                     max_val=ck.shape[0] - 1)
                sp.dma_start(m.CK[:, b, n, :], ck[ds(page, 1), :, :].rearrange("g p n -> (g p) n")
                             ).then_inc(m.cache_full, 16)
                sp.dma_start(m.KP[:, b, n, :], kp[ds(page, 1), :, :].rearrange("g p n -> (g p) n")
                             ).then_inc(m.cache_full, 16)
    pair(0)
    with sp.Fori(1, 4) as t:
        pair(t)


def tensor_program(pe, m):
    mm, tr = pe_matmul(m), pe_transpose(m)
    pe.sem_inc(m.pa_o, 1)
    ps = m.ps
    TOK = ((0, 128, 0), (128, 128, 1), (256, NS, 2))

    def products(out, wh, wl, xh, xl, start, stop):
        mm(out, wh, xh, start, False)
        mm(out, wh, xl, False, False)
        return mm(out, wl, xh, False, stop)

    def slot_parts(S, i, k):
        j = ring(S, i) % 2
        n = 2048 // k
        return m.Wh[:, j, :].rearrange("p (k n) -> p k n", n=n), m.Wl[:, j, :].rearrange("p (k n) -> p k n", n=n)

    def k16(S, it, Xh, Xl, x_ready, X0, cols=256):
        for u in range(len(cols) if isinstance(cols, tuple) else 2):
            b = 2 * ((S // 2 + u) % 2)
            for half in range(2):
                i = 2 * u + half
                wh, wl = slot_parts(S, i, 8)
                pe.wait_ge(m.split_done, it * 4 + (S + i + 1))
                for k in range(8):
                    kt = 8 * half + k
                    if kt % 2 == 0 and x_ready is not None:
                        pe.wait_ge(x_ready, X0 + (kt // 2 + 1))
                    for n in range(2):
                        last = products(ps[:, b + n, 0:NT], wh[:, k, 128 * n:128 * n + 128],
                                        wl[:, k, 128 * n:128 * n + 128], m_x(Xh, kt), m_x(Xl, kt), kt == 0, kt == 15)
                last.then_inc(m.slot_used, 1)

    def m_x(X, kt):
        return X[:, kt, :]

    def one_tile(S, Xh, Xl, x_ready, X0, width, cols):
        b = 2 * (S // 2 % 2)
        for half in range(2):
            j = ring(S, half) % 2
            wh, wl = (x[:, j, 0:8 * width].rearrange("p (k c) -> p k c", k=8) for x in (m.Wh, m.Wl))
            pe.wait_ge(m.split_done, S + half + 1)
            for k in range(8):
                kt = 8 * half + k
                if kt % 2 == 0 and x_ready is not None:
                    pe.wait_ge(x_ready, X0 + (kt // 2 + 1))
                last = products(ps[0:cols, b, 0:NT], wh[:, k, 0:cols], wl[:, k, 0:cols], m_x(Xh, kt), m_x(Xl, kt),
                                kt == 0, kt == 15)
            last.then_inc(m.slot_used, 1)

    def norm_sum(n):
        pe.wait_ge(m.ss_done, 8 * n + 8)
        if n:
            pe.wait_ge(m.r_inv, n)
        mm(ps[:, 7, 0:NT], m.ones[:], m.ssacc[:, 0, :], True, False)
        mm(ps[:, 7, 0:NT], m.ones[:], m.ssacc[:, 1, :], False, True).then_inc(m.ss_mm, 1)

    pe.wait_ge(m.l_id, 16)
    pe.wait_ge(m.l_par, 16 * 13)
    at = 0
    for g, rows in enumerate((80, 96, 73, 64)):
        last = tr(ps[:, 4, at:at + rows], m.prow[0:rows, g, :], rows)
        at += rows
    last.then_inc(m.par_tr, 1)
    pe.wait_ge(m.l_x, 32)
    for n in range(8):
        if n >= 2:
            pe.wait_ge(m.h_ready, n - 1)
        for i in range(2):
            b, d = 2 * (n % 2) + i, 2 * n + i
            for c in range(2):
                tr(ps[:, b, 128 * c:128 * c + 128], m.xtok[:, c, 128 * d:128 * d + 128], 128)
            last = tr(ps[:, b, 256:NT], m.xstok[0:NS, 128 * d:128 * d + 128], NS)
        last.then_inc(m.x_tr, 1)
    pe.wait_ge(m.l_hist, 32)
    for k in range(32):
        last = tr(ps[:, 5 + k // 16, 24 * (k % 16):24 * (k % 16) + 24], m.hrow[0:24, 128 * k:128 * k + 128], 24)
    last.then_inc(m.hist_tr, 1)
    pe.wait_ge(m.ones_set, 1)
    norm_sum(0)
    pe.wait_ge(m.h_ready, 8)

    A, B = (m.Ah, m.Al), (m.Bh, m.Bl)
    with pe.Fori(0, 6) as t:
        k16(S_QKV, t, *A, m.fl_done, 0)
    with pe.Fori(0, 2) as t:
        k16(S_Z, t, *A, None, 0)
    one_tile(S_BA, *A, None, 0, 64, 40)
    for S in (S_LX, S_LY):
        with pe.Fori(0, 2) as t:
            k16(S, t, *A, None, 0)

    pe.wait_ge(m.pre_saved, 16)
    for g in range(2):
        if g:
            pe.wait_ge(m.csr_done, BASE["csr_done"] + 1)
        for k in range(16):
            last = tr(ps[0:27, 4 + k // 4, 128 * (k % 4):128 * (k % 4) + 128], m.cs[:, 16 * g + k, :], 128)
        last.then_inc(m.cs_tr, 1)

    pe.wait_ge(m.csr_done, BASE["csr_done"] + 2)
    pe.wait_ge(m.conv_act, 16)

    def gates(t):
        for u in range(2):
            pe.wait_ge(m.gw_full[u], 32 * t + 32)
            if not isinstance(t, int):
                pe.wait_ge(m.gate_act, 2 * t + (u - 1))
            for g in range(2):
                last = mm(ps[:, 4 + 2 * u + g, 0:NT], m.gw[:, u, g, :], m.xb[:, ds(2 * t + u, 1), :], True, True)
            last.then_inc(m.gate_mm, 1)
    gates(0)
    with pe.Fori(1, 4) as t:
        gates(t)
    pe.wait_ge(m.lo_done, BASE["lo_done"] + 2)
    pe.wait_ge(m.gate_act, 8)
    tr(ps[0:72, 4, 0:128], m.lo[:], 128).then_inc(m.lo_tr, 1)

    for g in range(2):
        pe.wait_ge(m.l2_sq, BASE["l2_sq"] + g + 1)
        if g:
            pe.wait_ge(m.l2_inv, BASE["l2_inv"] + 1)
        else:
            pe.wait_ge(m.lrow_done, BASE["lrow_done"] + 1)
        for h in range(HG):
            last = mm(ps[:, h, 0:NT], m.ones[:], m.sqg[:, 8 * g + h, :], True, True)
        last.then_inc(m.l2_mm, 1)
    pe.wait_ge(m.l2_inv, BASE["l2_inv"] + 2)
    pe.wait_ge(m.nbg_done, BASE["nbg_done"] + 1)
    pe.wait_ge(m.kde_done, BASE["kde_done"] + 1)
    for q, row in enumerate((m.betaR, m.gR, m.eR, m.gcR)):
        for c0, n, c in TOK:
            last = tr(ps[0:n, 0, (q * 3 + c) * 8:(q * 3 + c) * 8 + 8], row[0:8, c0:c0 + n], 8)
    last.then_inc(m.scal_tr, 1)
    pe.wait_ge(m.scal_done, BASE["scal_done"] + 1)
    for g, row in enumerate((m.gcR, m.betaR)):
        if g:
            pe.wait_ge(m.bb_done, BASE["bb_done"] + 1)
        for h in range(HG):
            last = mm(ps[:, h, 0:NT], m.ident[0:8, h:h + 1].to_broadcast([8, 128]), row[0:8, :], True, True)
        last.then_inc(m.bb_mm, 1)
    pe.wait_ge(m.bb_done, BASE["bb_done"] + 2)

    def head(t):
        q, k, v = m.qkv[:, 0, :], m.qkv[:, 1, :], m.qkv[:, 2, :]
        pe.wait_ge(m.g_stage, t + 1)
        for b, x in ((0, k), (1, v)):
            for c0, n, c in TOK:
                last = tr(ps[0:n, b, 128 * c:128 * c + 128], x[:, c0:c0 + n], 128)
        last.then_inc(m.g_tr, 1)
        for b, x in ((2, k), (3, q)):
            for c0, n, c in TOK:
                last = mm(ps[0:n, b, c0:c0 + n], k[:, c0:c0 + n], x[:, c0:c0 + n], True, True)
        last.then_inc(m.g_gram, 1)
        pe.wait_ge(m.g_bt1, t + 1)
        for c in range(2):
            tr(ps[:, 4, 128 * c:128 * c + 128], m.Bt[:, 0, c, :], 128)
        tr(ps[0:NS, 5, 0:NS], m.Bts[0:NS, 0, :], NS).then_inc(m.g_t1, 1)
        for n in range(1, LEVELS):
            pe.wait_ge(m.g_lt, 6 * t + n)
            for c in range(2):
                last = mm(ps[:, 4, 128 * c:128 * c + 128], m.Bt[:, n, c, :], m.TT[:, 0, c, :], True, True)
            if n == 1:
                last = mm(ps[0:NS, 5, 0:NS], m.Bts[0:NS, 1, :], m.Ts[0:NS, 0, :], True, True)
            last.then_inc(m.g_q, 1)
            pe.wait_ge(m.g_qc, 6 * t + n)
            for c in range(2):
                mm(ps[:, 6, 128 * c:128 * c + 128], m.TT[:, 1, c, :], m.Qs[:, c, :], True, True)
                last = mm(ps[:, 6, 256 + 128 * c:384 + 128 * c], m.Qs[:, c, :], m.TT[:, 1, c, :], True, True)
            if n == 1:
                mm(ps[0:NS, 7, 0:NS], m.Ts[0:NS, 1, :], m.Qss[0:NS, :], True, True)
                last = mm(ps[0:NS, 7, NS:2 * NS], m.Qss[0:NS, :], m.Ts[0:NS, 1, :], True, True)
            last.then_inc(m.g_tb, 1)
        pe.wait_ge(m.g_inv, t + 1)
        mm(ps[:, 4, 0:128], m.TT[:, 1, 0, :], m.vb[:, 0, :], True, True).then_inc(m.g_v0, 1)
        pe.wait_ge(m.s8_full, 16 * t + 16)
        for b in range(BS):
            last = mm(ps[:, 7, 64 + 8 * b:72 + 8 * b], m.S8[:, b, :], m.kq[:, b, :, :].rearrange("p a t -> p (a t)"),
                      True, True)
        last.then_inc(m.g_xs, 1)
        pe.wait_ge(m.g_vn0, t + 1)
        mm(ps[:, 4, 128:256], m.kd[:, 0, :], m.vn[:, 0, :], True, True).then_inc(m.g_s1, 1)
        mm(ps[:, 2, 0:128], m.vn[:, 0, :], m.AQ[:, 1, 0:128], True, True)
        pe.wait_ge(m.g_xt, t + 1)
        tr(ps[0:NS, 5, 256:384], m.XT[:], 128).then_inc(m.g_xtr, 1)
        pe.wait_ge(m.g_s1c, t + 1)
        mm(ps[:, 6, 0:128], k[:, 128:256], m.S1[:], True, True).then_inc(m.g_x1, 1)
        pe.wait_ge(m.g_rs, t + 1)
        mm(ps[:, 3, 0:128], m.TT[:, 1, 1, :], m.R1[:], True, True).then_inc(m.g_v1, 1)
        mm(ps[0:NS, 7, 384:512], m.Ts[0:NS, 1, :], m.Rs[0:NS, :], True, True).then_inc(m.g_vs, 1)
        pe.wait_ge(m.g_vn1, t + 1)
        mm(ps[:, 4, 256:384], m.kd[:, 1, :], m.vn[:, 1, :], True, True).then_inc(m.g_s2, 1)
        mm(ps[:, 2, 128:256], m.S1[:], m.qe[:, 128:256], True, False)
        mm(ps[:, 2, 128:256], m.vn[:, 1, :], m.AQ[:, 1, 128:256], False, True)
        pe.wait_ge(m.g_vns, t + 1)
        mm(ps[:, 2, 256:NT], m.vn[0:NS, 2, :], m.AQ[0:NS, 1, 256:NT], True, True).then_inc(m.g_o, 1)
        pe.wait_ge(m.g_vm, t + 1)
        for g in range(2):
            last = mm(ps[:, g, :], m.kd[0:NS, 2, :], m.Vm[0:NS, 4 * g:4 * g + 4, :].rearrange("p b v -> p (b v)"),
                      True, True)
        last.then_inc(m.g_ds, 1)
    with pe.Fori(0, HG) as t:
        head(t)
    pe.wait_ge(m.on_sq, BASE["on_sq"] + 1)
    for h in range(HG):
        last = mm(ps[:, h, 0:NT], m.ones[:], m.sqg[:, h, :], True, True)
    last.then_inc(m.on_mm, 1)

    pe.wait_ge(m.on_inv, BASE["on_inv"] + 1)
    pe.wait_ge(m.mixl_done, 2)
    with pe.Fori(0, 4) as t:
        k16(S_OUT, t, *B, None, 0)
    norm_sum(1)

    def mlp(layer, S, S_P, S_G, X, Y, X0, U0):
        with pe.Fori(0, 4) as c:
            with pe.Fori(0, 4) as t:
                k16(S, c * 8 + t, *X, m.fl_done, X0)
            with pe.Fori(0, 4) as t:
                k16(S, c * 8 + t + 4, *Y, m.fu_done, c * 8 + U0)
        pe.wait_ge(m.l_p, 32 * layer + 32)
        for d in range(2):
            for c in range(2):
                tr(ps[:, 4 + d, 128 * c:128 * c + 128], m.ptok[:, c, 128 * d:128 * d + 128], 128)
            last = tr(ps[:, 4 + d, 256:NT], m.ptok[0:NS, 2, 128 * d:128 * d + 128], NS)
        last.then_inc(m.p_tr, 1)
        pe.wait_ge(m.pl_done, layer + 1)
        pe.wait_ge(m.h_ready, 24 * layer + 24)
        for i in range(2):
            wh, wl = slot_parts(S_P, i, 2)
            pe.wait_ge(m.split_done, S_P + i + 1)
            for n in range(4):
                q = 4 * i + n
                b = 2 * ((S_P // 2 + n) % 2)
                if q >= 2:
                    pe.wait_ge(m.ple_ev, 8 * layer + q - 1)
                for o in range(2):
                    c0 = 256 * n + 128 * o
                    for k in range(2):
                        last = products(ps[:, b + o, 0:NT], wh[:, k, c0:c0 + 128], wl[:, k, c0:c0 + 128],
                                        m.pTh[:, k, :], m.pTl[:, k, :], k == 0, k == 1)
                last.then_inc(m.slot_used if n == 3 else m.ple_mm, 1)
        pe.wait_ge(m.ple_ev, 8 * layer + 8)
        with pe.Fori(0, 4) as t:
            k16(S_G, t, *X, m.fl_done, X0 + 8)

    mlp(0, S_FFN0, S_PLE0, S_GATE0, A, B, 8, 0)
    norm_sum(2)

    with pe.Fori(0, 2) as t:
        k16(S_INC, t, *B, m.fl_done, 24)
    one_tile(S_KPE, *B, None, 0, 128, 128)
    for g in range(2):
        pe.wait_ge(m.c_sq, BASE["c_sq"] + g + 1)
        for k in range(4):
            last = mm(ps[:, 4 + g, 0:NT], m.ones[:], m.csq[:, 4 * g + k, :], k == 0, k == 3)
        last.then_inc(m.c_mm, 1)
    pe.wait_ge(m.kpr_done, BASE["kpr_done"] + 1)
    pe.wait_ge(m.l_c1, 16)
    ROT = m.cst1[:, NC1 - 128:NC1]
    mm(ps[:, 6, 0:NT], ROT, m.kpR[:], True, True).then_inc(m.kp_rot, 1)
    pe.wait_ge(m.cn_done, BASE["cn_done"] + 1)
    pe.wait_ge(m.kpe_done, BASE["kpe_done"] + 1)
    for c0, n, c in TOK:
        for k in range(4):
            last = tr(ps[0:n, (0, 1, 2)[c], 128 * k:128 * k + 128], m.c[:, 4 + k, c0:c0 + n], 128)
        last.then_inc(m.ctok_tr, 1)
    for c0, n, c in TOK:
        last = tr(ps[0:n, 7, 64 * c:64 * c + 64], m.kpe[0:64, c0:c0 + n], 64)
    last.then_inc(m.ctok_tr, 1)
    pe.wait_ge(m.ctok_done, BASE["ctok_done"] + 6)

    pe.wait_ge(m.cql_done, BASE["cql_done"] + 1)
    with pe.Fori(0, 2) as t:
        for i in range(4):
            j = ring(S_UQ, i) % 2
            wh, wl = (x[:, j, 0:1536].rearrange("p (k n) -> p k n", k=4) for x in (m.Wh, m.Wl))
            pe.wait_ge(m.split_done, t * 4 + (S_UQ + i + 1))
            b = 4 * (i % 2)
            for n in range(3):
                for k in range(4):
                    last = products(ps[:, b + n, 0:NT], wh[:, k, 128 * n:128 * n + 128],
                                    wl[:, k, 128 * n:128 * n + 128], m.cqh[:, k, :], m.cql[:, k, :], k == 0, k == 3)
            last.then_inc(m.slot_used, 1)
    pe.wait_ge(m.uq_ev, 8)
    for k in range(8):
        last = mm(ps[:, k, 0:NT], ROT, m.qp[:, k, :], True, True)
    last.then_inc(m.qp_rot, 1)

    pe.wait_ge(m.qp_done, BASE["qp_done"] + 1)
    pe.wait_ge(m.ckl_done, BASE["ckl_done"] + 1)
    pe.wait_ge(m.identr_set, BASE["identr_set"] + 1)
    with pe.Fori(0, 2) as t:
        for i in range(4):
            j = ring(S_UKV, i) % 2
            wh = m.Wh[:, j, :].rearrange("p (k h g n) -> p k h g n", k=4, h=2, g=2)
            wl = m.Wl[:, j, :].rearrange("p (k h g n) -> p k h g n", k=4, h=2, g=2)
            pe.wait_ge(m.split_done, t * 4 + (S_UKV + i + 1))
            pe.wait_ge(m.kv_ev, 4 * t + (i + 1))
            for h in range(2):
                for k in range(4):
                    mm(ps[:, h, 128 * k:128 * k + 128], wh[:, k, h, 0, :], m.identr[:], True, False)
                    last = mm(ps[:, h, 128 * k:128 * k + 128], wl[:, k, h, 0, :], m.identr[:], False, True)
            last.then_inc(m.kv_t, 1)
            for h in range(2):
                for k in range(4):
                    last = products(ps[:, 2, 256 * h:256 * h + 256], wh[:, k, h, 0, :], wl[:, k, h, 0, :],
                                    m.ckh[:, k, 0:SEQ], m.ckl[:, k, 0:SEQ], k == 0, k == 3)
            last.then_inc(m.kv_k, 1)
            for c in range(2):
                o = ps[:, 3, 256 * c:256 * c + 256]
                for k in range(4):
                    xh, xl = m.ckh[:, k, 128 * c:128 * c + 128], m.ckl[:, k, 128 * c:128 * c + 128]
                    mm(o, xh, wh[:, k, :, 1, :], k == 0, False)
                    mm(o, xh, wl[:, k, :, 1, :], False, False)
                    last = mm(o, xl, wh[:, k, :, 1, :], False, k == 3)
            last.then_inc(m.slot_used, 1)
            pe.wait_ge(m.kv_tc, 4 * t + (i + 1))
            for h in range(2):
                for k in range(4):
                    last = mm(ps[:, 4, 128 * h + 32 * k:128 * h + 32 * k + 32], m.wukT[:, h, 128 * k:128 * k + 128],
                              m.qn[:, ds(t * 8 + (2 * i + h), 1), SEQ:NT], True, True)
            last.then_inc(m.kv_q, 1)

    pe.wait_ge(m.kv_ev, 9)
    with pe.Fori(0, 8) as t:
        pe.wait_ge(m.pa_stage, 2 * t + 2)
        for u in range(2):
            qp, kp = m.qp2[64 * u:64 * u + 64, :], m.kpe[64 * u:64 * u + 64, :]
            for c0, at, n in ((0, 0, 128), (128, 128, 256)):
                mm(ps[:, u, at:at + n], m.qs2[:, u, c0:c0 + 128], m.kno[:, ds(2 * t + u, 1), 0:n], True, False)
                last = mm(ps[:, u, at:at + n], qp[:, c0:c0 + 128], kp[:, 0:n], False, True)
            last.then_inc(m.pa_s, 1)
        for u in range(2):
            pe.wait_ge(m.pa_p, 2 * t + (u + 1))
            for g in range(3):
                last = tr(ps[:, 2 + u, 128 * g:128 * g + 128], m.sc2[:, u, 128 * g:128 * g + 128], 128)
            last.then_inc(m.pa_t, 1)
        for u in range(2):
            pe.wait_ge(m.pa_tc, 2 * t + (u + 1))
            mm(ps[:, 4 + u, 0:128], m.vs2[:, 0, 128 * u:128 * u + 128], m.PT2[:, u, 0:128], True, True)
            mm(ps[:, 4 + u, 128:256], m.vs2[:, 0, 128 * u:128 * u + 128], m.PT2[:, u, 128:256], True, False)
            last = mm(ps[:, 4 + u, 128:256], m.vs2[:, 1, 128 * u:128 * u + 128], m.PT2[:, u, 256:384], False, True)
        last.then_inc(m.pa_o, 1)

    pe.wait_ge(m.patt_out, 8)
    with pe.Fori(0, 4) as t:
        pe.wait_ge(m.cache_full, 16 * 32 * t + 16 * 32)
        pe.wait_ge(m.sa_stage, t + 1)
        for b in range(2):
            for n in range(NPG):
                s = b * NPG + n
                if s >= 2:
                    pe.wait_ge(m.sa_ckc, 16 * t + (s - 1))
                    pe.wait_ge(m.sa_kpc, 16 * t + (s - 1))
                for k in range(4):
                    tr(ps[:, 4 + s % 2, 128 * k:128 * k + 128], m.CK[:, b, n, 128 * k:128 * k + 128], 128)
                tr(ps[0:64, 6 + s % 2, 0:128], m.KP[:, b, n, :], 128).then_inc(m.sa_t, 1)
            pe.wait_ge(m.sa_ckc, 16 * t + 8 * (b + 1))
            pe.wait_ge(m.sa_kpc, 16 * t + 8 * (b + 1))
            for g in range(2):
                o = ps[64 * b:64 * b + 64, g, :]
                for k in range(4):
                    mm(o, m.qls[:, k, b, :, :].rearrange("p h t -> p (h t)"), m.ckT[:, k, 512 * g:512 * g + 512],
                       k == 0, False)
                mm(o, m.qrs2[0:64, b, :, :].rearrange("p h t -> p (h t)"), m.kpT[0:64, 512 * g:512 * g + 512],
                   False, True)
            o = ps[64 * b:64 * b + 64, 2, 0:8]
            for k in range(4):
                mm(o, m.qls[:, k, b, :, :].rearrange("p h t -> p (h t)"), m.ckns[:, k, :], k == 0, False)
            mm(o, m.qrs2[0:64, b, :, :].rearrange("p h t -> p (h t)"),
               m.ckns[0:64, 4, :], False, True).then_inc(m.sa_s, 1)
        for k in range(4):
            last = tr(ps[0:8, 3, 128 * k:128 * k + 128], m.ckns[:, k, :], 128)
        last.then_inc(m.sa_nt, 1)
        pe.wait_ge(m.sa_p, t + 1)
        for n in range(NPG):
            last = tr(ps[:, 4 + n // 4, 128 * (n % 4):128 * (n % 4) + 128], m.sc8[:, 128 * n:128 * n + 128], 128)
        tr(ps[0:8, 6, 0:128], m.sc8[:, PAST:PAST + 8], 128).then_inc(m.sa_pt, 1)
        pe.wait_ge(m.sa_ptc, 2 * t + 2)
        for b in range(2):
            for k in range(4):
                o = ps[:, 7, 256 * b + 64 * k:256 * b + 64 * k + 64]
                for n in range(NPG):
                    mm(o, m.CK[:, b, n, 128 * k:128 * k + 128], m.PT[:, n, 64 * b:64 * b + 64], n == 0, False)
                last = mm(o, m.ckn[0:8, 128 * k:128 * k + 128], m.PTn[0:8, 64 * b:64 * b + 64], False, True)
        last.then_inc(m.spv_mm, 1)

    pe.wait_ge(m.acl_done, BASE["acl_done"] + 1)
    for i in range(4):
        j = ring(S_OV, i) % 2
        wh = m.Wh[:, j, :].rearrange("p (h n) -> p h n", h=HM)
        wl = m.Wl[:, j, :].rearrange("p (h n) -> p h n", h=HM)
        pe.wait_ge(m.split_done, S_OV + i + 1)
        for h in range(HM):
            last = products(ps[:, 0, NS * h:NS * h + NS], wh[:, h, :], wl[:, h, :], m.ach[:, i, h, :],
                            m.acl[:, i, h, :], i == 0 and h == 0, i == 3 and h == HM - 1)
        last.then_inc(m.slot_used, 1)
    pe.wait_ge(m.attl_done, BASE["attl_done"] + 1)
    with pe.Fori(0, 4) as t:
        k16(S_WO, t, *A, None, 0)
    norm_sum(3)
    mlp(1, S_FFN1, S_PLE1, S_GATE1, B, A, 32, 32)
    norm_sum(4)
    for g in range(4):
        pe.wait_ge(m.yn_done, 4 * g + 4)
        if g >= 2:
            pe.wait_ge(m.y_done, 3 * g - 3)
        for c0, n, c in TOK:
            for k in range(4):
                last = tr(ps[0:n, 3 * (g % 2) + c, 128 * k:128 * k + 128], m.hT[:, 4 * g + k, c0:c0 + n], 128)
            last.then_inc(m.y_tr, 1)


def pe_matmul(m):
    def mm(out, w, x, start, stop):
        if len(x.shape) == 3 and x.shape[1] == 1:
            x = x.rearrange("p a n -> p (a n)")
        return m.nc.tensor.matmul(out, w, x, start=start, stop=stop)
    return mm


def pe_transpose(m):
    def tr(out, x, rows):
        return m.nc.tensor.transpose(out, x, m.ident[0:x.shape[0], 0:x.shape[0]])
    return tr


def split_value(S, i, it):
    return 16 * ((S + i) // 4 + 1) + it * 16


def scalar_program(act, m):
    ps = m.ps
    A = m.nc.scalar.activation
    own = Own(act, m.act_own)

    def split(S, i, it):
        s = S + i
        j = ring(S, i)
        act.wait_ge(m.w_full[j], split_value(S, i, it))
        if not (isinstance(it, int) and s + 4 * it < 2):
            act.wait_ge(m.slot_used, it * 4 + (s - 1))
        for w, x in pieces(s + 4 * it if isinstance(it, int) else -1, m.W[:, j, :], m.Wh[:, j % 2, :]):
            last = A(x, w, ACT.Copy)
        last.then_inc(m.wh_done, 1)

    def k16(S, it, evac, more=True):
        for u in range(2):
            if more or u == 0:
                split(S, 2 * u + 2, it)
                split(S, 2 * u + 3, it)
            if evac:
                evac(u)

    def f_round(n, F, gcol, Xh):
        act.wait_ge(m.h_ready, n + (8 * F + 1))
        for i in range(2):
            g = 1.0 if gcol is None else m.par[:, ds(n * 2 + (gcol + i), 1)]
            last = A(Xh[:, ds(n * 2 + i, 1), :], m.hT[:, ds(n * 2 + i, 1), :], ACT.Copy, scale=g)
        last.then_inc(m.fh_done, 1)

    def root(n):
        act.wait_ge(m.r_inv, n + 1)
        A(m.rB[:], m.rB[:], ACT.Sqrt).then_inc(m.r_ready, 1)

    act.wait_ge(m.l_id, 16)
    A(m.identr[:], m.ident[:], ACT.Copy).then_inc(m.identr_set, 1)
    split(0, 0, 0)
    split(0, 1, 0)
    act.wait_ge(m.lam_abs, BASE["lam_abs"] + 1)
    own.after(A(m.lsp[:, 1, 0:8], m.lsp[:, 0, 8:16], ACT.Exp, scale=-1.0))
    A(m.lsp[:, 1, 8:16], m.lsp[:, 1, 0:8], ACT.Ln, bias=1.0).then_inc(m.lam_ln, 1)
    act.wait_ge(m.par_done, BASE["par_done"] + 1)
    with act.Fori(0, 8) as n:
        f_round(n, 0, C_MIX, m.Ah)
    root(0)

    def conv(n, k, dst):
        u = 0 if k is None else k[1]
        act.wait_ge(m.conv_done, n + 1)
        tail = m.acc[:, u, :, PADS:PRE].rearrange("p i (b s) -> p i b s", s=7)[:, :, :, 0:TS]
        if dst is m.conv:
            A(dst[:, ds(k[0] * 2, 2), 0:SEQ], m.acc[:, u, :, 0:SEQ], ACT.Silu)
            A(dst[:, ds(k[0] * 2, 2), SEQ:NT].rearrange("p i (b t) -> p i b t", t=TS), tail, ACT.Silu
              ).then_inc(m.conv_act, 1)
        else:
            for i in range(2):
                b = m.par[:, ds(k[0] * 2 + (C_LB + i), 1)]
                A(dst[:, ds(k[0] * 2 + i, 1), 0:SEQ].rearrange("p i n -> p (i n)"), m.acc[:, u, i, 0:SEQ],
                  ACT.Identity, bias=b)
                last = A(dst[:, ds(k[0] * 2 + i, 1), SEQ:NT].rearrange("p i (b t) -> p (i b) t", t=TS), tail[:, i],
                         ACT.Identity, bias=b)
            last.then_inc(m.conv_act, 1)

    with act.Fori(0, 6) as t:
        k16(S_QKV, t, lambda u: conv(t * 2 + u, (t * 2 + u, u), m.conv))

    def gated(x, func, raw, done):
        def turn(t):
            def evac(u):
                act.wait_ge(raw, t * 2 + (u + 1))
                A(x[:, ds(t * 4 + 2 * u, 2), :], x[:, ds(t * 4 + 2 * u, 2), :], func).then_inc(done, 1)
            return evac
        return turn
    zt, lyt = gated(m.z, ACT.Silu, m.z_raw, m.z_act), gated(m.ly, ACT.Gelu_apprx_tanh, m.ly_raw, m.ly_act)
    for t in range(2):
        k16(S_Z, t, zt(t))
    split(S_BA, 2, 0)
    split(S_BA, 3, 0)
    with act.Fori(0, 2) as t:
        k16(S_LX, t, lambda u: conv(t * 2 + (12 + u), (t * 2 + u, u), m.xb))
    with act.Fori(0, 2) as t:
        k16(S_LY, t, lyt(t))

    act.wait_ge(m.nb_done, BASE["nb_done"] + 1)

    def gates(t):
        for u in range(2):
            act.wait_ge(m.gate_mm, 2 * t + (u + 1))
            for g in range(2):
                last = A(m.lm[:, g, ds(2 * t + u, 1), :].rearrange("p k n -> p (k n)"), ps[:, 4 + 2 * u + g, 0:NT],
                         ACT.Exp, scale=-1.0, bias=m.lsp[:, 3, ds(2 * t + (u + 8 * g), 1)])
            last.then_inc(m.gate_act, 1)
    with act.Fori(0, 4) as t:
        gates(t)
    act.wait_ge(m.o_cs, 64)
    act.wait_ge(m.lm_done, BASE["lm_done"] + 1)
    A(m.la[:], m.lm[:, 0], ACT.Exp, scale=-1.0)
    A(m.lt[:], m.lm[:, 0], ACT.Tanh).then_inc(m.lat_done, 1)
    act.wait_ge(m.lt_done, BASE["lt_done"] + 1)
    A(m.lt[:], m.lt[:], ACT.Sqrt).then_inc(m.lroot_done, 1)
    act.wait_ge(m.ob_done, BASE["ob_done"] + 1)
    A(m.Bh[:, 8:16, :], m.la[:], ACT.Copy).then_inc(m.mixh_done, 1)

    act.wait_ge(m.conv_act, 12)
    for g in range(2):
        A(m.sqg[:, 8 * g:8 * g + 8, :], m.conv[:, 8 * g:8 * g + 8, :], ACT.Square).then_inc(m.l2_sq, 1)
    for g in range(2):
        act.wait_ge(m.l2_inv, BASE["l2_inv"] + g + 1)
        A(m.sqg[:, 8 * g:8 * g + 8, :], m.sqg[:, 8 * g:8 * g + 8, :], ACT.Sqrt, scale=1.0 if g else 1.0 / DK
          ).then_inc(m.l2_rt, 1)
    act.wait_ge(m.ba_done, BASE["ba_done"] + 1)
    A(m.betaR[0:8, :], m.betaR[0:8, :], ACT.Exp, scale=-1.0).then_inc(m.beta_e, 1)
    act.wait_ge(m.l_ab, 32)
    A(m.alog[0:8, 2:3], m.alog[0:8, 0:1], ACT.Exp)
    act.wait_ge(m.a_abs, BASE["a_abs"] + 1)
    own.after(A(m.eR[0:8, :], m.eR[0:8, :], ACT.Exp, scale=-1.0))
    A(m.eR[0:8, :], m.eR[0:8, :], ACT.Ln, bias=1.0).then_inc(m.a_ln, 1)
    act.wait_ge(m.gc_done, BASE["gc_done"] + 1)
    A(m.gR[0:8, :], m.gcR[0:8, :], ACT.Exp).then_inc(m.eg_done, 1)
    act.wait_ge(m.dl_done, BASE["dl_done"] + 1)
    A(m.eR[0:8, :], m.eR[0:8, :], ACT.Exp).then_inc(m.kde_done, 1)
    act.wait_ge(m.bb_done, BASE["bb_done"] + 2)

    conv3 = m.conv[:].rearrange("p (a h) n -> p a h n", a=3)
    with act.Fori(0, HG) as t:
        act.wait_ge(m.head_end, t + 1)
        A(m.qkv[:], conv3[:, :, ds(t, 1), :].rearrange("p a h n -> p a (h n)"), ACT.Copy).then_inc(m.g_stage, 1)
        A(m.Eb[:], m.GB[:, ds(t, 1), :].rearrange("p h n -> p (h n)"), ACT.Exp).then_inc(m.g_eb, 1)
        act.wait_ge(m.g_diff, t + 1)
        A(m.dec[:, 0:SEQ], m.dec[:, 0:SEQ], ACT.Exp)
        A(m.dec[0:NS, SEQ:NT], m.dec[0:NS, SEQ:NT], ACT.Exp).then_inc(m.g_dec, 1)
        for n in range(1, LEVELS):
            act.wait_ge(m.g_q, 6 * t + n)
            if n == 1:
                A(m.Qss[0:NS, :], ps[0:NS, 5, 0:NS], ACT.Copy)
            A(m.Qs[:].rearrange("p c n -> p (c n)"), ps[:, 4, 0:256], ACT.Copy).then_inc(m.g_qc, 1)
        act.wait_ge(m.g_v0, t + 1)
        A(m.vn[:, 0, :], ps[:, 4, 0:128], ACT.Copy).then_inc(m.g_vn0, 1)
        act.wait_ge(m.g_xs, t + 1)
        old = ps[:, 7, 64:128].rearrange("p (b a t) -> p b a t", b=BS, a=2)
        A(m.XT[:].rearrange("p (b t) -> p b t", b=BS), old[:, :, 0, :], ACT.Copy).then_inc(m.g_xt, 1)
        A(m.oS[:].rearrange("p (b t) -> p b t", b=BS), old[:, :, 1, :], ACT.Copy)
        act.wait_ge(m.g_s1, t + 1)
        A(m.S1[:], ps[:, 4, 128:256], ACT.Copy).then_inc(m.g_s1c, 1)
        act.wait_ge(m.g_v1, t + 1)
        A(m.vn[:, 1, :], ps[:, 3, 0:128], ACT.Copy).then_inc(m.g_vn1, 1)
        act.wait_ge(m.g_vs, t + 1)
        A(m.vn[0:NS, 2, :], ps[0:NS, 7, 384:512], ACT.Copy).then_inc(m.g_vns, 1)

    act.wait_ge(m.head_end, HG + 1)
    A(m.sqg[:, 0:8, :], m.conv[:, 0:8, :], ACT.Square).then_inc(m.on_sq, 1)
    act.wait_ge(m.on_inv, BASE["on_inv"] + 1)
    A(m.sqg[:, 0:8, :], m.sqg[:, 0:8, :], ACT.Sqrt).then_inc(m.on_rt, 1)
    act.wait_ge(m.og_done, BASE["og_done"] + 1)
    act.wait_ge(m.o_lru, 32)
    act.wait_ge(m.o_s2, 16 * HG)
    A(m.Bh[:, 0:8, :], m.conv[:, 0:8, :], ACT.Copy).then_inc(m.mixh_done, 1)

    act.wait_ge(m.o_s8, 16 * HG)
    with act.Fori(0, 4) as t:
        k16(S_OUT, t, lambda u: f_round(t * 2 + u, 1, C_FFN, m.Ah))
    root(1)

    def mlp(layer, S, S_P, S_G, Xh, Yh, F):
        def up(c, t):
            def evac(u):
                act.wait_ge(m.u_done, c * 8 + t * 2 + (32 * layer + u + 1))
                own.after(A(m.usq[:], m.u[:], ACT.Square))
                A(Yh[:, ds(t * 4 + 2 * u, 2), :], m.usq[:], ACT.Copy).then_inc(m.fuh_done, 1)
            return evac

        def chunk(c):
            own.loop(4, 2, lambda t: k16(S, c * 8 + t, up(c, t)))
            with act.Fori(0, 4) as t:
                k16(S, c * 8 + t + 4, None)
        own.loop(3, 8, chunk)
        own.loop(4, 2, lambda t: k16(S, t + 24, up(3, t)))
        with act.Fori(0, 4) as t:
            k16(S, t + 28, lambda u: f_round(t * 2 + u, F, None, Xh))
        act.wait_ge(m.pt_done, layer + 1)
        A(m.pTh[:], m.usq[:], ACT.Copy).then_inc(m.ph_done, 1)
        split(S_P, 2, 0)
        split(S_P, 3, 0)

        def gate(t, last):
            def evac(u):
                n = t * 2 + u
                act.wait_ge(m.gt_raw, n + (8 * layer + 1))
                A(m.gt[:], m.gt[:], ACT.Sigmoid).then_inc(m.gt_act, 1)
                if layer == 0:
                    f_round(n, F + 1, C_MIX + 16, Yh)
            k16(S_G, t, evac, more=not last)
        with act.Fori(0, 3 + (layer == 0)) as t:
            gate(t, False)
        if layer:
            gate(3, True)

    mlp(0, S_FFN0, S_PLE0, S_GATE0, m.Ah, m.Bh, 2)
    root(2)

    for t in range(2):
        k16(S_INC, t, None)
    split(S_KPE, 2, 0)
    split(S_KPE, 3, 0)
    act.wait_ge(m.c_raw, 4)
    for g in range(2):
        A(m.csq[:, 4 * g:4 * g + 4, :], m.c[:, 4 * g:4 * g + 4, :], ACT.Square).then_inc(m.c_sq, 1)
    act.wait_ge(m.c_inv, BASE["c_inv"] + 1)
    A(m.rc[:], m.rc[:], ACT.Sqrt).then_inc(m.c_rt, 1)
    act.wait_ge(m.cn_done, BASE["cn_done"] + 1)
    A(m.cqh[:], m.c[:, 0:4, :], ACT.Copy).then_inc(m.cqh_done, 1)
    A(m.ckh[:], m.c[:, 4:8, :], ACT.Copy).then_inc(m.ckh_done, 1)
    for i in range(8):
        split(S_UQ, i + 2, 0)
    with act.Fori(0, 2) as t:
        for i in range(4):
            act.wait_ge(m.kv_t, t * 4 + (i + 1))
            A(m.wukT[:], ps[:, 0:2, :], ACT.Copy).then_inc(m.kv_tc, 1)
            split(S_UKV, i + 2, t)

    act.wait_ge(m.o_c, 64)
    with act.Fori(0, 8) as t:
        act.wait_ge(m.pa_o, t + 1)
        act.wait_ge(m.kv_ev, 9)
        A(m.qs2[:], m.qn[:, ds(t * 2, 2), 0:SEQ], ACT.Copy)
        A(m.qp2[:], m.qp[:, ds(t, 1), 0:SEQ].rearrange("p k n -> p (k n)"), ACT.Copy).then_inc(m.pa_stage, 1)
        for u in range(2):
            act.wait_ge(m.pa_m, 2 * t + (u + 1))
            for g, (c0, c1) in enumerate(((0, 128), (128, 384))):
                w = m.mx2[:, 2 * u + g, :]
                last = A(m.sc2[:, u, c0:c1], m.sc2[:, u, c0:c1], ACT.Exp, bias=w[:, 1:2], scale=MLA_SCALE,
                         accum_out=w[:, 2:3])
            last.then_inc(m.pa_e, 1)
        for u in range(2):
            act.wait_ge(m.pa_t, 2 * t + (u + 1))
            A(m.PT2[:, u, :], ps[:, 2 + u, 0:384], ACT.Copy).then_inc(m.pa_tc, 1)
        act.wait_ge(m.pa_o, t + 2)
        A(m.Ah[:, ds(t * 2, 2), 0:SEQ], ps[:, 4:6, 0:SEQ], ACT.Copy).then_inc(m.pa_ah, 1)

    with act.Fori(0, 4) as t:
        for s in range(2 * NPG):
            n = s % NPG
            act.wait_ge(m.sa_t, 16 * t + (s + 1))
            A(m.ckT[:, :, 128 * n:128 * n + 128], ps[:, 4 + s % 2, :].rearrange("p (k n) -> p k n", k=4), ACT.Copy
              ).then_inc(m.sa_ckc, 1)
        act.wait_ge(m.sa_nt, t + 1)
        A(m.ckn[0:8, :], ps[0:8, 3, :], ACT.Copy)
        act.wait_ge(m.sa_m, t + 1)
        A(m.sc8[:], m.sc8[:], ACT.Exp, bias=m.mx8[:, 1:2], scale=MLA_SCALE, accum_out=m.mx8[:, 2:3]
          ).then_inc(m.sa_e, 1)
        act.wait_ge(m.sa_pt, t + 1)
        A(m.PT[:].rearrange("p n r -> p (n r)"), ps[:, 4:6, :].rearrange("p b n -> p (b n)"), ACT.Copy
          ).then_inc(m.sa_ptc, 1)
        A(m.PTn[0:8, :], ps[0:8, 6, 0:128], ACT.Copy).then_inc(m.sa_ptc, 1)
    act.wait_ge(m.sa_acc, 4)
    A(m.ach[:], m.accT[:], ACT.Copy).then_inc(m.ach_done, 1)
    for i in range(4):
        split(S_OV, i + 2, 0)
    act.wait_ge(m.slot_used, S_OV + 4)
    A(m.Ah[:, :, SEQ:NT], ps[:, 0, :].rearrange("p (h t) -> p h t", h=HM), ACT.Copy).then_inc(m.atth_done, 1)
    with act.Fori(0, 4) as t:
        k16(S_WO, t, lambda u: f_round(t * 2 + u, 4, C_FFN + 16, m.Bh))
    root(3)
    mlp(1, S_FFN1, S_PLE1, S_GATE1, m.Bh, m.Ah, 5)
    root(4)
    for g in range(4):
        for c, n in ((0, 128), (1, 128), (2, NS)):
            act.wait_ge(m.y_tr, 3 * g + c + 1)
            A(m.ytok[0:n, c, 512 * g:512 * g + 512], ps[0:n, 3 * (g % 2) + c, :], ACT.Copy).then_inc(m.y_done, 1)


def vector_program(dve, m):
    ps = m.ps
    V = m.nc.vector
    own = Own(dve, m.dve_own)
    TT, TS2, STT = V.tensor_tensor, V.tensor_scalar, V.scalar_tensor_tensor
    MUL, ADD, SUB, MAX = ALU.mult, ALU.add, ALU.subtract, ALU.max

    def f(x):
        return x.bitcast(F32)

    def over(ap, n):
        return ap.unsqueeze(1).to_broadcast([ap.shape[0], n, ap.shape[1]])

    def split(S, i, it):
        j = ring(S, i)
        dve.wait_ge(m.wh_done, it * 4 + (S + i + 1))
        parts = [pieces(S + i + 4 * it if isinstance(it, int) else -1, m.W[:, j, :], x[:, j % 2, :])
                 for x in (m.Wl, m.Wh)]
        for (w, low), (_, high) in zip(*parts):
            last = TT(low, w, f(high), SUB)
        last.then_inc(m.split_done, 1)

    def k16(S, it, evac, more=True):
        for u in range(2):
            if more or u == 0:
                split(S, 2 * u + 2, it)
                split(S, 2 * u + 3, it)
            dve.wait_ge(m.slot_used, it * 4 + (S + 2 * u + 2))
            b = 2 * ((S // 2 + u) % 2)
            evac(u, ps[:, b:b + 2, 0:NT])

    def f_low(n, F, gcol, Xh, Xl):
        dve.wait_ge(m.fh_done, n + (8 * F + 1))
        if gcol is None:
            last = TT(Xl[:, ds(n * 2, 2), :], m.hT[:, ds(n * 2, 2), :], f(Xh[:, ds(n * 2, 2), :]), SUB)
        else:
            for i in range(2):
                t = ds(n * 2 + i, 1)
                last = STT(Xl[:, t, :], m.hT[:, t, :], m.par[:, ds(n * 2 + (gcol + i), 1)], f(Xh[:, t, :]), MUL, SUB)
        last.then_inc(m.fl_done, 1)

    def add_to_h(n, x):
        TT(m.hT[:, ds(n * 2, 2), :], m.hT[:, ds(n * 2, 2), :], x, ADD).then_inc(m.h_ready, 1)

    def norm(n):
        dve.wait_ge(m.ss_mm, n + 1)
        own.after(TS2(m.rB[:], ps[:, 7, 0:NT], 1.0 / D_MODEL, EPS, MUL, ADD))
        V.reciprocal(m.rB[:], m.rB[:]).then_inc(m.r_inv, 1)

    dve.sem_inc(m.head_end, 1)
    dve.sem_inc(m.kv_ev, 1)
    dve.wait_ge(m.par_tr, BASE["par_tr"] + 1)
    V.tensor_copy(m.par[:, 0:NPAR], ps[:, 4, 0:NPAR]).then_inc(m.par_done, 1)
    dve.wait_ge(m.par_done, BASE["par_done"] + 1)
    lam, nl = m.par[:, C_LAM:C_LAM + 8], m.lsp[:, 0, 0:8]
    own.after(TS2(nl, lam, -1.0, None, MUL))
    TT(m.lsp[:, 0, 8:16], nl, lam, MAX).then_inc(m.lam_abs, 1)
    dve.wait_ge(m.lam_ln, BASE["lam_ln"] + 1)
    own.after(STT(m.lsp[:, 2, 0:8], nl, 0.0, m.lsp[:, 1, 8:16], MAX, ADD))
    own.after(TS2(m.lsp[:, 2, 8:16], m.lsp[:, 2, 0:8], 8.0, None, MUL))
    TS2(m.lsp[:, 3, 0:16], m.par[:, C_BA:C_BA + 16], -1.0, None, MUL).then_inc(m.nb_done, 1)
    for n in range(8):
        dve.wait_ge(m.x_tr, n + 1)
        b = 2 * (n % 2)
        V.tensor_copy(m.hT[:, 2 * n:2 * n + 2, :], ps[:, b:b + 2, 0:NT]).then_inc(m.h_ready, 1)
        f_low(n, 0, C_MIX, m.Ah, m.Al)
    split(0, 0, 0)
    split(0, 1, 0)
    dve.wait_ge(m.hist_tr, BASE["hist_tr"] + 1)
    V.tensor_copy(m.hist[:, 0:16, :].rearrange("p k n -> p (k n)"), ps[:, 5, 0:384])
    V.tensor_copy(m.hist[:, 16:32, :].rearrange("p k n -> p (k n)"), ps[:, 6, 0:384]).then_inc(m.hist_done, 1)
    norm(0)
    dve.wait_ge(m.r_ready, 1)

    r_p, r_s = m.rB[:, 0:SEQ], m.rB[:, SEQ:NT]

    def conv(n, tile, col, taps):
        def evac(u, x):
            if not isinstance(n, int):
                dve.wait_ge(m.pre_saved, n + (u - 1))
            TT(m.pre[:, u, :, 3:3 + SEQ], x[:, :, 0:SEQ], over(r_p, 2), MUL)
            rows = m.pre[:, u, :, PADS:PRE].rearrange("p i (b s) -> p i b s", s=7)
            for i in range(2):
                last = TT(rows[:, i, :, 3:7], x[:, i, SEQ:NT].rearrange("p (b t) -> p b t", t=TS),
                          r_s.rearrange("p (b t) -> p b t", t=TS), MUL)
            last.then_inc(m.pre_ready, 1)
            dve.wait_ge(m.pre_ready, n + (u + 1))
            dve.wait_ge(m.hist_in, n + (u + 1))
            if not isinstance(n, int):
                dve.wait_ge(m.conv_act, n + (u - 1))
            for w in range(4):
                for i in range(2):
                    g = m.par[:, ds(tile + (2 * u + i + col + taps * w), 1)]
                    x_w, o = m.pre[:, u, i, w:w + PRE - 3], m.acc[:, u, i, 0:PRE - 3]
                    last = STT(o, x_w, g, o, MUL, ADD) if w else TS2(o, x_w, g, None, MUL)
                if w < 3:
                    own.after(last)
            last.then_inc(m.conv_done, 1)
        return evac
    k16(S_QKV, 0, conv(0, 0, C_CONV, 24))
    own.loop(6, 6, lambda t: k16(S_QKV, t, conv(t * 2, t * 4, C_CONV, 24)), first=1)

    def scaled(dst, sem):
        def turn(t):
            def evac(u, x):
                TT(dst[:, ds(t * 4 + 2 * u, 2), :], x, over(m.rB[:], 2), MUL).then_inc(sem, 1)
            return evac
        return turn
    zt, lyt, ct = scaled(m.z, m.z_raw), scaled(m.ly, m.ly_raw), scaled(m.c, m.c_raw)
    for t in range(2):
        k16(S_Z, t, zt(t))
    split(S_BA, 2, 0)
    split(S_BA, 3, 0)
    dve.wait_ge(m.slot_used, S_BA + 2)
    b = 2 * (S_BA // 2 % 2)
    TT(m.betaR[0:8, :], ps[0:8, b, 0:NT], m.rB[0:8, :], MUL)
    TT(m.gR[0:8, :], ps[32:40, b, 0:NT], m.rB[32:40, :], MUL).then_inc(m.ba_done, 1)
    own.loop(2, 6, lambda t: k16(S_LX, t, conv(t * 2 + 12, t * 4, C_LCONV, 8)))
    with dve.Fori(0, 2) as t:
        k16(S_LY, t, lyt(t))

    for g in range(2):
        dve.wait_ge(m.cs_tr, BASE["cs_tr"] + g + 1)
        V.tensor_copy(m.csrow[0:27, 2048 * g:2048 * g + 2048], ps[0:27, 4:8, :].rearrange("p b n -> p (b n)")
                      ).then_inc(m.csr_done, 1)

    dve.wait_ge(m.gate_act, 8)
    own.after(TS2(m.lm[:], m.lm[:], 1.0, None, ADD))
    own.after(V.reciprocal(m.lm[:], m.lm[:]))
    dve.wait_ge(m.conv_act, 16)
    TT(m.lm[:, 1], m.lm[:, 1], m.xb[:], MUL)
    sp8 = m.lsp[:, 2, 8:16].unsqueeze(2).to_broadcast([128, 8, NT])
    TT(m.lm[:, 0], m.lm[:, 0], sp8, MUL).then_inc(m.lm_done, 1)
    dve.wait_ge(m.lat_done, BASE["lat_done"] + 1)
    own.after(TS2(m.lm[:, 0], m.lt[:], 1.0, None, ADD))
    own.after(V.reciprocal(m.lm[:, 0], m.lm[:, 0]))
    STT(m.lt[:], m.lt[:], 2.0, m.lm[:, 0], MUL, MUL).then_inc(m.lt_done, 1)
    dve.wait_ge(m.lroot_done, BASE["lroot_done"] + 1)
    own.after(TT(m.lt[:], m.lt[:], m.lm[:, 1], MUL))
    hs = m.lm[:, 0]
    for k in range(8):
        V.tensor_tensor_scan(hs[:, k, 0:SEQ], m.la[:, k, 0:SEQ], m.lt[:, k, 0:SEQ], 0.0, MUL, ADD)
    row = lambda x, t: x[:, :, SEQ:NT].rearrange("p k (b t) -> p k b t", t=TS)[:, :, :, t]
    before = m.par[:, C_H0:C_H0 + 64].rearrange("p (b k) -> p k b", k=8)
    for t in range(TS):
        own.after(TT(row(hs, t), row(m.la, t), before, MUL))
        own.after(TT(row(hs, t), row(hs, t), row(m.lt, t), ADD))
        before = row(hs, t)
    V.tensor_copy(m.lo[:, 0:8], hs[:, :, SEQ - 1]).then_inc(m.lo_done, 1)
    V.tensor_copy(m.lo[:, 8:72].rearrange("p (b k) -> p k b", k=8), row(hs, TS - 1)).then_inc(m.lo_done, 1)
    dve.wait_ge(m.ly_act, 4)
    TT(m.la[:], hs, m.ly[:], MUL).then_inc(m.ob_done, 1)
    dve.wait_ge(m.lo_tr, BASE["lo_tr"] + 1)
    V.tensor_copy(m.lrow[0:72, :], ps[0:72, 4, 0:128]).then_inc(m.lrow_done, 1)
    dve.wait_ge(m.mixh_done, 1)
    TT(m.Bl[:, 8:16, :], m.la[:], f(m.Bh[:, 8:16, :]), SUB).then_inc(m.mixl_done, 1)

    for g in range(2):
        dve.wait_ge(m.l2_mm, BASE["l2_mm"] + g + 1)
        x = m.sqg[:, 8 * g:8 * g + 8, :]
        own.after(TS2(x, ps[:, :, 0:NT], EPS, None, ADD))
        V.reciprocal(x, x).then_inc(m.l2_inv, 1)
    for g in range(2):
        dve.wait_ge(m.l2_rt, BASE["l2_rt"] + g + 1)
        x = m.conv[:, 8 * g:8 * g + 8, :]
        TT(x, x, m.sqg[:, 8 * g:8 * g + 8, :], MUL).then_inc(m.l2_done, 1)
    be, g_, gc, e = m.betaR[0:8, :], m.gR[0:8, :], m.gcR[0:8, :], m.eR[0:8, :]
    dve.wait_ge(m.beta_e, BASE["beta_e"] + 1)
    own.after(TS2(be, be, 1.0, None, ADD))
    V.reciprocal(be, be).then_inc(m.beta_done, 1)
    dve.wait_ge(m.l_ab, 32)
    dve.wait_ge(m.ba_done, BASE["ba_done"] + 1)
    own.after(TS2(g_, g_, m.alog[0:8, 1:2], None, ADD))
    STT(e, g_, -1.0, g_, MUL, MAX).then_inc(m.a_abs, 1)
    dve.wait_ge(m.a_ln, BASE["a_ln"] + 1)
    own.after(STT(g_, g_, 0.0, e, MAX, ADD))
    own.after(TS2(g_, g_, m.alog[0:8, 2:3], -1.0, MUL, MUL))
    dve.wait_ge(m.l_c0, 16)
    V.tensor_tensor_scan(gc, m.cst0[0:8, NC0 - NT:NC0], g_, 0.0, MUL, ADD).then_inc(m.gc_done, 1)
    dve.wait_ge(m.gc_done, BASE["gc_done"] + 1)
    for c0, c1, n in ((0, SEQ, CHUNK), (SEQ, NT, TS)):
        x = gc[:, c0:c1].rearrange("p (c n) -> p c n", n=n)
        end = x[:, :, n - 1:n].to_broadcast([8, (c1 - c0) // n, n])
        last = TT(e[:, c0:c1].rearrange("p (c n) -> p c n", n=n), end, x, SUB)
    last.then_inc(m.dl_done, 1)
    dve.wait_ge(m.eg_done, BASE["eg_done"] + 1)
    dve.wait_ge(m.beta_done, BASE["beta_done"] + 1)
    STT(g_, g_, -1.0, be, MUL, MUL).then_inc(m.nbg_done, 1)
    own.after(V.memset(m.scal[:], 0.0))
    dve.wait_ge(m.scal_tr, BASE["scal_tr"] + 1)
    sc = m.scal[:].rearrange("p h (q c) -> p q c h", q=4)
    pv = ps[:, 0, 0:96].rearrange("p (q c h) -> p q c h", q=4, c=3)
    for c, n in ((0, 128), (1, 128), (2, NS)):
        last = V.tensor_copy(sc[0:n, :, c, :], pv[0:n, :, c, :])
    last.then_inc(m.scal_done, 1)
    for g, dst in enumerate((m.GB, m.BB)):
        dve.wait_ge(m.bb_mm, BASE["bb_mm"] + g + 1)
        V.tensor_copy(dst[:], ps[:, :, 0:NT]).then_inc(m.bb_done, 1)

    lev = m.cst0[:, 0:LEVELS * 128].rearrange("p (n x) -> p n x", n=LEVELS)
    belongs = m.cst0[0:NS, LEVELS * 128 + 128 + NS:LEVELS * 128 + 128 + NS + BS]
    AT = m.AQ[:, 0, 0:SEQ].rearrange("p (c n) -> p c n", c=2)

    def head(t):
        h = ds(t, 1)
        dve.wait_ge(m.head_end, t + 1)
        own.after(V.tensor_copy(m.sc1[:], m.scal[:, h, :].rearrange("p h q -> p (h q)")))
        beta, nbg, kde, gcs = ([m.sc1[:, 3 * q + c:3 * q + c + 1] for c in range(3)] for q in range(4))
        GBh = m.GB[:, h, :].rearrange("p h n -> p (h n)")
        for c in range(2):
            TS2(m.dec[:, 128 * c:128 * c + 128], GBh[:, 128 * c:128 * c + 128], gcs[c], 0.0, SUB, ALU.min)
        TS2(m.dec[0:NS, SEQ:NT], GBh[0:NS, SEQ:NT], gcs[2][0:NS], 0.0, SUB, ALU.min).then_inc(m.g_diff, 1)
        dve.wait_ge(m.g_tr, t + 1)
        for c, n in ((0, 128), (1, 128), (2, NS)):
            TS2(m.vb[0:n, c, :], ps[0:n, 1, 128 * c:128 * c + 128], beta[c][0:n], None, MUL)
            TS2(m.kd[0:n, c, :], ps[0:n, 0, 128 * c:128 * c + 128], kde[c][0:n], None, MUL)
        dve.wait_ge(m.g_eb, t + 1)
        own.after(TT(m.qe[:], m.qkv[:, 0, :], m.Eb[:], MUL))
        for a, x in ((0, m.qkv[:, 1, SEQ:NT]), (1, m.qe[:, SEQ:NT])):
            V.tensor_copy(m.kq[:, :, a, :], x.rearrange("p (b t) -> p b t", t=TS))
        dve.wait_ge(m.g_gram, t + 1)
        dve.wait_ge(m.g_decb, t + 1)
        TT(m.AQ[:, 0, 0:SEQ], ps[:, 2, 0:SEQ], m.decB[:, 0:SEQ], MUL)
        own.after(TT(m.AQ[0:NS, 0, SEQ:NT], ps[0:NS, 2, SEQ:NT], m.decB[0:NS, SEQ:NT], MUL))
        TT(m.Bt[:, 0], AT, over(lev[:, 0], 2), MUL)
        ats = m.AQ[0:NS, 0, SEQ:NT]
        TT(m.Bts[0:NS], over(ats, 2), lev[0:NS, 0:2, 0:NS], MUL).then_inc(m.g_bt1, 1)
        dve.wait_ge(m.g_bt1, t + 1)
        TT(m.TT[:, 1], over(m.ident[:], 2), m.Bt[:, 0], SUB)
        TT(m.Ts[0:NS, 1, :], m.ident[0:NS, 0:NS], m.Bts[0:NS, 0, :], SUB)
        for n in range(1, LEVELS):
            TT(m.Bt[:, n], AT, over(lev[:, n], 2), MUL)
        TT(m.AQ[:, 1, 0:SEQ], ps[:, 3, 0:SEQ], m.decU[:, 0:SEQ], MUL)
        TT(m.AQ[0:NS, 1, SEQ:NT], ps[0:NS, 3, SEQ:NT], m.decU[0:NS, SEQ:NT], MUL)
        dve.wait_ge(m.g_t1, t + 1)
        TT(m.Ts[0:NS, 0, :], m.ident[0:NS, 0:NS], ps[0:NS, 5, 0:NS], SUB)
        TT(m.TT[:, 0], over(m.ident[:], 2), ps[:, 4, 0:256].rearrange("p (c n) -> p c n", c=2), SUB
           ).then_inc(m.g_lt, 1)
        flat = m.TT[:].rearrange("p a c n -> p (a c n)")
        fs = m.Ts[0:NS].rearrange("p a n -> p (a n)")
        for n in range(1, LEVELS):
            dve.wait_ge(m.g_tb, 6 * t + n)
            if n == 1:
                TT(fs, fs, ps[0:NS, 7, 0:2 * NS], SUB)
            TT(flat, flat, ps[:, 6, :], SUB).then_inc(m.g_lt if n < LEVELS - 1 else m.g_inv, 1)
        dve.wait_ge(m.g_xs, t + 1)
        ends = m.Eb[:, SEQ:NT].rearrange("p (b t) -> p b t", t=TS)[:, :, TS - 1:TS].to_broadcast([128, BS, 128])
        TT(m.S8[:], m.S8[:], ends, MUL)
        dve.wait_ge(m.g_x1, t + 1)
        STT(m.R1[:], ps[:, 6, 0:128], nbg[1], m.vb[:, 1, :], MUL, ADD)
        dve.wait_ge(m.g_xtr, t + 1)
        STT(m.Rs[0:NS, :], ps[0:NS, 5, 256:384], nbg[2][0:NS], m.vb[0:NS, 2, :], MUL, ADD).then_inc(m.g_rs, 1)
        dve.wait_ge(m.g_s2, t + 1)
        STT(m.S2[:], m.S1[:], m.Eb[:, SEQ - 1:SEQ], ps[:, 4, 256:384], MUL, ADD).then_inc(m.s2_done, 1)
        dve.wait_ge(m.g_vns, t + 1)
        TT(m.Vm[0:NS], over(m.vn[0:NS, 2, :], BS), belongs.unsqueeze(2).to_broadcast([NS, BS, 128]), MUL
           ).then_inc(m.g_vm, 1)
        dve.wait_ge(m.g_o, t + 1)
        o = m.conv[:, h, :].rearrange("p h n -> p (h n)")
        V.tensor_copy(o[:, 0:SEQ], ps[:, 2, 0:SEQ])
        TT(o[:, SEQ:NT], ps[:, 2, SEQ:NT], m.oS[:], ADD)
        dve.wait_ge(m.g_ds, t + 1)
        s8 = m.S8[:].rearrange("p b v -> p (b v)")
        TT(s8, s8, ps[:, 0:2, :].rearrange("p b n -> p (b n)"), ADD).then_inc(m.s8_done, 1)
        dve.wait_ge(m.s8_done, t + 1)
        V.tensor_copy(m.sc1[:, 0:1], m.scal[:, 0, 0:1]).then_inc(m.head_end, 1)
    own.loop(HG, 3, head)

    dve.wait_ge(m.on_mm, BASE["on_mm"] + 1)
    x = m.sqg[:, 0:8, :]
    own.after(TS2(x, ps[:, :, 0:NT], 1.0 / DK, EPS, MUL, ADD))
    V.reciprocal(x, x).then_inc(m.on_inv, 1)
    dve.wait_ge(m.on_rt, BASE["on_rt"] + 1)
    dve.wait_ge(m.z_act, 4)
    o = m.conv[:, 0:8, :]
    own.after(TT(o, o, x, MUL))
    STT(o, o, m.par[:, C_GN:C_GN + 1], m.z[:], MUL, MUL).then_inc(m.og_done, 1)
    dve.wait_ge(m.mixh_done, 2)
    TT(m.Bl[:, 0:8, :], o, f(m.Bh[:, 0:8, :]), SUB).then_inc(m.mixl_done, 1)

    def residual(F, gcol, Xh, Xl):
        def turn(t):
            def evac(u, x):
                add_to_h(t * 2 + u, x)
                f_low(t * 2 + u, F, gcol, Xh, Xl)
            return evac
        return turn
    res = residual(1, C_FFN, m.Ah, m.Al)
    with dve.Fori(0, 4) as t:
        k16(S_OUT, t, res(t))
    norm(1)

    def mlp(layer, S, S_P, S_G, X, Y, F):
        dve.wait_ge(m.r_ready, 2 + 2 * layer)

        def up(c, t):
            def evac(u, x):
                n = t * 2 + u
                STT(m.u[:], x, 0.0, over(m.rB[:], 2), MAX, MUL).then_inc(m.u_done, 1)
                dve.wait_ge(m.fuh_done, c * 8 + n + (32 * layer + 1))
                TT(Y[1][:, ds(n * 2, 2), :], m.usq[:], f(Y[0][:, ds(n * 2, 2), :]), SUB).then_inc(m.fu_done, 1)
            return evac

        def down(t):
            def evac(u, x):
                hh = m.hT[:, ds(t * 4 + 2 * u, 2), :]
                TT(hh, hh, x, ADD)
            return evac
        with dve.Fori(0, 3) as c:
            with dve.Fori(0, 4) as t:
                k16(S, c * 8 + t, up(c, t))
            with dve.Fori(0, 4) as t:
                k16(S, c * 8 + t + 4, down(t))
        with dve.Fori(0, 4) as t:
            k16(S, t + 24, up(3, t))
        res = residual(F, None, *X)
        with dve.Fori(0, 4) as t:
            k16(S, t + 28, res(t))
        dve.wait_ge(m.p_tr, layer + 1)
        V.tensor_copy(m.usq[:], ps[:, 4:6, 0:NT]).then_inc(m.pt_done, 1)
        dve.wait_ge(m.ph_done, layer + 1)
        TT(m.pTl[:], m.usq[:], f(m.pTh[:]), SUB).then_inc(m.pl_done, 1)
        for i in range(2):
            for n in range(4):
                if n < 3:
                    dve.wait_ge(m.ple_mm, 6 * layer + 3 * i + n + 1)
                else:
                    dve.wait_ge(m.slot_used, S_P + i + 1)
                b, q = 2 * ((S_P // 2 + n) % 2), 4 * i + n
                V.tensor_copy(m.ple[:, 2 * q:2 * q + 2, :], ps[:, b:b + 2, 0:NT]).then_inc(m.ple_ev, 1)
            split(S_P, i + 2, 0)
        dve.wait_ge(m.ple_ev, 8 * layer + 8)

        def gate(t):
            def evac(u, x):
                n = t * 2 + u
                dve.wait_ge(m.h_ready, n + 8 * (F + 1))
                V.tensor_copy(m.gt[:], x).then_inc(m.gt_raw, 1)
                dve.wait_ge(m.gt_act, n + (8 * layer + 1))
                own.after(TT(m.gt[:], m.gt[:], m.ple[:, ds(n * 2, 2), :], MUL))
                add_to_h(n, m.gt[:])
                if layer == 0:
                    f_low(n, F + 1, C_MIX + 16, *Y)
            return evac
        if layer:
            own.loop(3, 2, lambda t: k16(S_G, t, gate(t)))
            k16(S_G, 3, gate(3), more=False)
        else:
            own.loop(4, 2, lambda t: k16(S_G, t, gate(t)))

    mlp(0, S_FFN0, S_PLE0, S_GATE0, (m.Ah, m.Al), (m.Bh, m.Bl), 2)
    norm(2)
    dve.wait_ge(m.r_ready, 3)

    for t in range(2):
        k16(S_INC, t, ct(t))
    split(S_KPE, 2, 0)
    split(S_KPE, 3, 0)
    dve.wait_ge(m.slot_used, S_KPE + 2)
    TT(m.kpR[:], ps[:, 2 * (S_KPE // 2 % 2), 0:NT], m.rB[:], MUL).then_inc(m.kpr_done, 1)
    for g in range(2):
        dve.wait_ge(m.c_mm, BASE["c_mm"] + g + 1)
        last = TS2(m.rc[:, g, :], ps[:, 4 + g, 0:NT], 1.0 / QLORA, EPS, MUL, ADD)
    own.after(last)
    V.reciprocal(m.rc[:], m.rc[:]).then_inc(m.c_inv, 1)
    dve.wait_ge(m.c_rt, BASE["c_rt"] + 1)
    for g in range(2):
        x = m.c[:, 4 * g:4 * g + 4, :]
        last = TT(x, x, over(m.rc[:, g, :], 4), MUL)
    own.after(last)
    TT(m.c[:], m.c[:], m.par[:, C_QN:C_QN + 8].unsqueeze(2).to_broadcast([128, 8, NT]), MUL).then_inc(m.cn_done, 1)
    cm3, new = m.cst1[:, 0:384], m.cst1[:, 384:392]
    cos, sin = m.cst1[:, 392:392 + NT], m.cst1[:, 392 + NT:392 + 2 * NT]
    dve.wait_ge(m.cqh_done, BASE["cqh_done"] + 1)
    TT(m.cql[:], m.c[:, 0:4, :], f(m.cqh[:]), SUB).then_inc(m.cql_done, 1)
    dve.wait_ge(m.l_c1, 16)
    dve.wait_ge(m.kpr_done, BASE["kpr_done"] + 1)
    TT(m.kpe[:], m.kpR[:], cos, MUL)
    dve.wait_ge(m.kp_rot, BASE["kp_rot"] + 1)
    own.after(TT(m.rtmp[:, 0, :], ps[:, 6, 0:NT], sin, MUL))
    TT(m.kpe[:], m.kpe[:], m.rtmp[:, 0, :], ADD).then_inc(m.kpe_done, 1)
    dve.wait_ge(m.ckh_done, BASE["ckh_done"] + 1)
    TT(m.ckl[:], m.c[:, 4:8, :], f(m.ckh[:]), SUB).then_inc(m.ckl_done, 1)
    for c, n in ((0, 128), (1, 128), (2, NS)):
        dve.wait_ge(m.ctok_tr, BASE["ctok_tr"] + c + 1)
        V.tensor_copy(m.ctok[0:n, c, 0:512], ps[0:n, c, :]).then_inc(m.ctok_done, 1)
    dve.wait_ge(m.ctok_tr, BASE["ctok_tr"] + 4)
    for c, n in ((0, 128), (1, 128), (2, NS)):
        V.tensor_copy(m.ctok[0:n, c, 512:576], ps[0:n, 7, 64 * c:64 * c + 64]).then_inc(m.ctok_done, 1)

    for i in range(8):
        dve.wait_ge(m.slot_used, S_UQ + i + 1)
        b = 4 * (i % 2)
        V.tensor_copy(m.qn[:, 2 * i:2 * i + 2, :], ps[:, b:b + 2, 0:NT])
        V.tensor_copy(m.qp[:, i, :], ps[:, b + 2, 0:NT]).then_inc(m.uq_ev, 1)
        split(S_UQ, i + 2, 0)
    dve.wait_ge(m.qp_rot, BASE["qp_rot"] + 1)
    TT(m.rtmp[:], ps[:, :, 0:NT], over(sin, 8), MUL)
    own.after(TT(m.qp[:], m.qp[:], over(cos, 8), MUL))
    TT(m.qp[:], m.qp[:], m.rtmp[:], ADD).then_inc(m.qp_done, 1)

    with dve.Fori(0, 2) as t:
        for i in range(4):
            dve.wait_ge(m.kv_k, t * 4 + (i + 1))
            V.tensor_copy(m.kno[:, ds(t * 8 + 2 * i, 2), :], ps[:, 2, :].rearrange("p (h n) -> p h n", h=2))
            dve.wait_ge(m.slot_used, t * 4 + (S_UKV + i + 1))
            V.tensor_copy(m.vtok[:, :, ds(t * 1024 + 256 * i, 256)], ps[:, 3, :].rearrange("p (c n) -> p c n", c=2))
            dve.wait_ge(m.kv_q, t * 4 + (i + 1))
            V.tensor_copy(m.qlat[:, :, ds(t * 8 + 2 * i, 2), :],
                          ps[:, 4, 0:256].rearrange("p (h k n) -> p k h n", h=2, k=4)).then_inc(m.kv_ev, 1)
            split(S_UKV, i + 2, t)

    def heads(t):
        for u in range(2):
            dve.wait_ge(m.pa_s, 2 * t + (u + 1))
            own.after(TT(m.sc2[:, u, :], ps[:, u, 0:384], cm3, ADD))
            V.reduce_max(m.mx2[:, 2 * u, 0:1], m.sc2[:, u, 0:128], AX.X)
            own.after(V.reduce_max(m.mx2[:, 2 * u + 1, 0:1], m.sc2[:, u, 128:384], AX.X))
            TS2(m.mx2[:, 2 * u:2 * u + 2, 1:2], m.mx2[:, 2 * u:2 * u + 2, 0:1], -MLA_SCALE, None, MUL
                ).then_inc(m.pa_m, 1)
        for u in range(2):
            dve.wait_ge(m.pa_e, 2 * t + (u + 1))
            own.after(V.reciprocal(m.mx2[:, 2 * u:2 * u + 2, 3:4], m.mx2[:, 2 * u:2 * u + 2, 2:3]))
            TS2(m.sc2[:, u, 0:128], m.sc2[:, u, 0:128], m.mx2[:, 2 * u, 3:4], None, MUL)
            TS2(m.sc2[:, u, 128:384], m.sc2[:, u, 128:384], m.mx2[:, 2 * u + 1, 3:4], None, MUL).then_inc(m.pa_p, 1)
        dve.wait_ge(m.pa_ah, t + 1)
        TT(m.Al[:, ds(t * 2, 2), 0:SEQ], ps[:, 4:6, 0:SEQ], f(m.Ah[:, ds(t * 2, 2), 0:SEQ]), SUB
           ).then_inc(m.patt_out, 1)
    own.loop(8, 6, heads)

    for g in range(2):
        x = m.qp[64 * g:64 * g + 64, :, SEQ:NT].rearrange("p k (b t) -> p b k t", t=TS)
        out = m.qrs[0:64].rearrange("p b (k g) t -> p b k g t", g=2)[:, :, :, g, :]
        last = V.tensor_copy(out, x)
    own.after(last)

    def pair(t):
        V.tensor_copy(m.ckns[:, 0:4, :], m.c[:, 4:8, ds(t * 8 + SEQ, 8)])
        V.tensor_copy(m.ckns[0:64, 4, :], m.kpe[0:64, ds(t * 8 + SEQ, 8)])
        for b in range(2):
            V.tensor_copy(m.qls[:, :, b, :, :], m.qlat[:, :, :, ds(t * 8 + 4 * b, 4)])
        V.tensor_copy(m.qrs2[0:64], m.qrs[0:64, ds(t * 2, 2)]).then_inc(m.sa_stage, 1)
        for s in range(2 * NPG):
            n = s % NPG
            dve.wait_ge(m.sa_t, 16 * t + (s + 1))
            V.tensor_copy(m.kpT[0:64, 128 * n:128 * n + 128], ps[0:64, 6 + s % 2, 0:128]).then_inc(m.sa_kpc, 1)
        dve.wait_ge(m.sa_s, 2 * t + 2)
        V.tensor_copy(m.sc8[:, 0:PAST], ps[:, 0:2, :].rearrange("p b n -> p (b n)"))
        own.after(TT(m.sc8[:, PAST:], ps[:, 2, 0:8], new, ADD))
        own.after(V.reduce_max(m.mx8[:, 0:1], m.sc8[:], AX.X))
        TS2(m.mx8[:, 1:2], m.mx8[:, 0:1], -MLA_SCALE, None, MUL).then_inc(m.sa_m, 1)
        dve.wait_ge(m.sa_e, t + 1)
        own.after(V.reciprocal(m.mx8[:, 3:4], m.mx8[:, 2:3]))
        TS2(m.sc8[:], m.sc8[:], m.mx8[:, 3:4], None, MUL).then_inc(m.sa_p, 1)
        dve.wait_ge(m.spv_mm, t + 1)
        for b in range(2):
            last = V.tensor_copy(m.accT[:, :, :, ds(t * 8 + 4 * b, 4)],
                                 ps[:, 7, 256 * b:256 * b + 256].rearrange("p (k h t) -> p k h t", k=4, h=HM))
        last.then_inc(m.sa_acc, 1)
    own.loop(4, 3, pair)
    dve.wait_ge(m.ach_done, BASE["ach_done"] + 1)
    TT(m.acl[:], m.accT[:], f(m.ach[:]), SUB).then_inc(m.acl_done, 1)
    for i in range(4):
        split(S_OV, i + 2, 0)
    dve.wait_ge(m.atth_done, BASE["atth_done"] + 1)
    TT(m.Al[:, :, SEQ:NT], ps[:, 0, :].rearrange("p (h t) -> p h t", h=HM), f(m.Ah[:, :, SEQ:NT]), SUB
       ).then_inc(m.attl_done, 1)

    res = residual(4, C_FFN + 16, m.Bh, m.Bl)
    with dve.Fori(0, 4) as t:
        k16(S_WO, t, res(t))
    norm(3)
    mlp(1, S_FFN1, S_PLE1, S_GATE1, (m.Bh, m.Bl), (m.Ah, m.Al), 5)
    norm(4)
    dve.wait_ge(m.r_ready, 5)
    for k in range(KT):
        STT(m.hT[:, k, :], m.hT[:, k, :], m.par[:, C_FIN + k:C_FIN + k + 1], m.rB[:], MUL, MUL
            ).then_inc(m.yn_done, 1)


def gpsimd_program(g, m):
    G = m.nc.gpsimd
    own = Own(g, m.pool_own)
    MUL, ADD = ALU.mult, ALU.add

    def squares(n, F):
        if n:
            g.wait_ge(m.ss_mm, n)
        own.after(G.memset(m.ssacc[:], 0.0))

        def tiles(t):
            g.wait_ge(m.h_ready, t + (8 * F + 1))
            x = m.hT[:, ds(t * 2, 2), :]
            own.after(G.tensor_tensor(m.sqt[:], x, x, MUL))
            G.tensor_tensor(m.ssacc[:], m.ssacc[:], m.sqt[:], ADD).then_inc(m.ss_done, 1)
            g.wait_ge(m.ss_done, t + (8 * n + 1))
        own.loop(8, 1, tiles)

    G.memset(m.ones[:], 1.0).then_inc(m.ones_set, 1)
    G.memset(m.pre[:, :, :, 0:3], 0.0)
    squares(0, 0)
    g.wait_ge(m.hist_done, BASE["hist_done"] + 1)

    def conv(n, tile):
        for u in range(2):
            if not isinstance(n, int):
                g.wait_ge(m.conv_done, n + (u - 1))
            rows = m.pre[:, u, :, PADS:PRE].rearrange("p i (b s) -> p i b s", s=7)
            x = m.hist[:, ds(tile + 2 * u, 2), :].rearrange("p i (b w) -> p i b w", w=3)
            G.tensor_copy(rows[:, :, :, 0:3], x).then_inc(m.hist_in, 1)
            g.wait_ge(m.pre_ready, n + (u + 1))
            out = m.cs[:, ds(tile + 2 * u, 2), :]
            G.tensor_copy(out[:, :, 0:3], m.pre[:, u, :, SEQ:SEQ + 3])
            G.tensor_copy(out[:, :, 3:27].rearrange("p i (b w) -> p i b w", w=3), rows[:, :, :, 4:7]
                          ).then_inc(m.pre_saved, 1)
    conv(0, 0)
    with g.Fori(1, 6) as t:
        conv(t * 2, t * 4)
    with g.Fori(0, 2) as t:
        conv(t * 2 + 12, t * 4 + 24)

    up = m.cst0[:, LEVELS * 128:LEVELS * 128 + 128]
    up_s = m.cst0[0:NS, LEVELS * 128 + 128:LEVELS * 128 + 128 + NS]
    g.wait_ge(m.l_c0, 16)
    g.wait_ge(m.bb_done, BASE["bb_done"] + 2)

    def head(t):
        g.wait_ge(m.g_dec, t + 1)
        G.tensor_tensor(m.decU[:, 0:SEQ].rearrange("p (c n) -> p c n", c=2),
                        m.dec[:, 0:SEQ].rearrange("p (c n) -> p c n", c=2),
                        up.unsqueeze(1).to_broadcast([128, 2, 128]), MUL)
        own.after(G.tensor_tensor(m.decU[0:NS, SEQ:NT], m.dec[0:NS, SEQ:NT], up_s, MUL))
        bb = m.BB[:, ds(t, 1), :].rearrange("p h n -> p (h n)")
        G.tensor_tensor(m.decB[:, 0:SEQ], m.decU[:, 0:SEQ], bb[:, 0:SEQ], MUL)
        G.tensor_tensor(m.decB[0:NS, SEQ:NT], m.decU[0:NS, SEQ:NT], bb[0:NS, SEQ:NT], MUL).then_inc(m.g_decb, 1)
    own.loop(HG, 1, head)
    squares(1, 1)
    squares(2, 3)
    g.wait_ge(m.pa_o, 1)

    def stage(t):
        g.wait_ge(m.kv_ev, 9)
        g.wait_ge(m.pa_o, t + 1)
        G.tensor_copy(m.vs2[:], m.vtok[:, :, ds(t * 256, 256)]).then_inc(m.pa_stage, 1)
    with g.Fori(0, 8) as t:
        stage(t)
    g.wait_ge(m.acl_done, BASE["acl_done"] + 1)
    squares(3, 4)
    squares(4, 6)


def trunk(nc, a):
    with ExitStack() as ctx:
        m = memory(nc, ctx)
        block = ctx.enter_context(nc.Block())

        @block.sync
        def _(sp):
            sync_program(sp, m, a)

        @block.scalar
        def _(act):
            scalar_program(act, m)

        @block.vector
        def _(dve):
            vector_program(dve, m)

        @block.tensor
        def _(pe):
            tensor_program(pe, m)

        @block.gpsimd
        def _(g):
            gpsimd_program(g, m)


_OUTS = [("y_prompt", (1, SEQ, D_MODEL)), ("y_sample", (BS, TS, D_MODEL)), ("gdn_p", (1, 1, HG, DK, DK)),
         ("gdn_s", (1, BS, HG, DK, DK)), ("gdn_conv_p", (1, 1, 3, QKV)), ("gdn_conv_s", (1, BS, 3, QKV)),
         ("lru_p", (1, 1, LRU)), ("lru_s", (1, BS, LRU)), ("lru_conv_p", (1, 1, 3, LRU)),
         ("lru_conv_s", (1, BS, 3, LRU)), ("ckv_p", (1, 1, SEQ, KVLORA)), ("ckv_s", (1, BS, TS, KVLORA)),
         ("kpe_p", (1, 1, SEQ, ROPE)), ("kpe_s", (1, BS, TS, ROPE))]


def kernel(**inputs):
    import concourse.bacc as bacc
    from concourse.bass_utils import run_bass_kernel_spmd

    nc = bacc.Bacc("TRN2", target_bir_lowering=False, num_devices=1, dynamic_dma_scratch_size=1024)
    ident, c0, c1 = constants()
    arrays, aps = {}, {}
    for name, x in [*inputs.items(), ("ident", ident), ("cst0", c0), ("cst1", c1)]:
        x = np.ascontiguousarray(x)
        arrays[f"in_{name}"] = x
        aps[name] = nc.dram_tensor(f"in_{name}", x.shape, mybir.dt.from_np(x.dtype), kind="ExternalInput").ap()
    for name, shape in _OUTS:
        aps[name] = nc.dram_tensor(f"out_{name}", shape, F32, kind="ExternalOutput").ap()
    trunk(nc, aps)
    r = run_bass_kernel_spmd(nc, [arrays], core_ids=[0])
    return tuple(r.results[0][f"out_{name}"] for name, _ in _OUTS)
```

```python
import numpy as np
from contextlib import ExitStack

import concourse.bass as bass
from concourse import mybir

F32 = mybir.dt.float32
F32R = mybir.dt.float32r
I32 = mybir.dt.int32
ALU = mybir.AluOpType
ACT = mybir.ActivationFunctionType
AX = mybir.AxisListType
ds = bass.ds

D_MODEL, SEQ, BS, TS = 2048, 256, 8, 4
NS = BS * TS
NT = SEQ + NS
DEPTH, PLE = 2, 256
HG, DK = 8, 128
QKV, LRU = 3 * HG * DK, 1024
KT = D_MODEL // 128
HM, NOPE, ROPE, VH = 16, 128, 64, 128
QLORA, KVLORA = 512, 512
DFF = 8192
NPG, PAGE = 8, 128
PAST = NPG * PAGE
EPS = 1e-6
MLA_SCALE = (NOPE + ROPE) ** -0.5
CHUNK = 128
LEVELS = 7
PRE = 3 + SEQ + BS * (3 + TS)
PADS = PRE - BS * 7

C_MIX, C_FFN, C_FIN, C_CONV = 0, 32, 64, 80
C_LCONV = C_CONV + 96
C_LB, C_BA, C_BI, C_LAM = C_LCONV + 32, C_LCONV + 40, C_LCONV + 48, C_LCONV + 56
C_GN, C_QN, C_H0 = C_LCONV + 64, C_LCONV + 65, C_LCONV + 73
NPAR = C_H0 + 64

S_QKV = 0
S_Z = S_QKV + 24
S_BA = S_Z + 8
S_LX = S_BA + 2
S_LY = S_LX + 8
S_OUT = S_LY + 8
S_FFN0 = S_OUT + 16
S_PLE0 = S_FFN0 + 128
S_GATE0 = S_PLE0 + 2
S_INC = S_GATE0 + 16
S_KPE = S_INC + 8
S_UQ = S_KPE + 2
S_UKV = S_UQ + 8
S_OV = S_UKV + 8
S_WO = S_OV + 4
S_FFN1 = S_WO + 16
S_PLE1 = S_FFN1 + 128
S_GATE1 = S_PLE1 + 2
S_END = S_GATE1 + 16


def constants():
    f = np.float32
    i = np.arange(128)
    lev = np.zeros((128, LEVELS, 128), f)
    for n in range(LEVELS):
        s = 1 << n
        same = (i[:, None] // (2 * s)) == (i[None, :] // (2 * s))
        lev[:, n, :] = same & ((i[:, None] // s) % 2 == 1) & ((i[None, :] // s) % 2 == 0)
    lev[:, 0, :] = lev[:, 0, :].T.copy()
    up = np.where(i[:, None] <= i[None, :], 0.0, -1e30).astype(f)
    j = np.arange(NS)
    up_s = np.zeros((128, NS), f)
    up_s[:NS] = np.where((j[:, None] <= j[None, :]) & (j[:, None] // TS == j[None, :] // TS), 0.0, -1e30)
    own = np.zeros((128, BS), f)
    own[:NS] = j[:, None] // TS == np.arange(BS)[None, :]
    keep = np.ones((128, NT), f)
    keep[:, 0:SEQ:CHUNK] = 0
    keep[:, SEQ::TS] = 0
    sel = np.zeros((128, 4 * HG), f)
    sel[:, 2 * HG - 1] = 1
    sel[:2 * HG, 4 * HG - 1] = np.where(np.arange(2 * HG) < HG, 1.0 / DK, 1.0)
    c0 = np.concatenate([lev.reshape(128, -1), up, up_s, own, sel, keep], axis=1)
    causal = np.where(i[:, None] >= i[None, :], 0.0, -1e30).astype(f)
    cm3 = np.concatenate([causal, np.zeros((128, 128), f), causal], axis=1)
    c8 = np.arange(NS + NS - TS) - (NS - TS)
    new = np.where((c8[None, :] >= 0) & (c8[None, :] <= i[:, None] % TS), 0.0, -1e30).astype(f)
    half = ROPE // 2
    inv = (f(10000.0) ** (-np.arange(half, dtype=f) / f(half))).astype(f)
    pos = np.concatenate([np.arange(SEQ), np.tile(PAST + np.arange(TS), BS)]).astype(f)
    ang = (inv[i % half][:, None] * pos[None, :]).astype(f)
    rot = np.zeros((128, 128), f)
    for m in range(128):
        if (m % ROPE) < half:
            rot[m + half, m] = -1.0
        else:
            rot[m - half, m] = 1.0
    c1 = np.concatenate([cm3, new, np.cos(ang).astype(f), np.sin(ang).astype(f), rot], axis=1)
    return np.eye(128, dtype=f), c0.astype(f), c1.astype(f)


NC0 = LEVELS * 128 + 128 + NS + BS + 4 * HG + NT
NC1 = 3 * 128 + 2 * NS - TS + 2 * NT + 128


STEPS = {
    "pe_steps": """par_tr hist_tr cs_tr:2 lo_tr l2_sum l2_mm:2 scal_tr on_sum on_mm c_mm:2 kp_rot ctok_tr:4 qp_rot ckn_tr""",
    "act_steps": """identr_set lam_ln lat_done lroot_done l2_sq:2 l2_rt beta_e a_ln eg_done kde_done on_sq on_rt c_sq:2
    c_rt cqh_done ckh_done ckn_done ach_done atth_done""",
    "dve_steps": """par_done lam_abs hist_done ba_done csr_done:2 lm_done lt_done lo_done:2 ob_done lrow_done
    l2_inv l2_done:2 beta_done a_abs gc_done dl_done nbg_done scal_done on_inv og_done kpr_done
    c_inv cn_done cql_done kpe_done ckl_done ctok_done:6 qp_done acl_done attl_done""",
}


def bases():
    base = {}
    for steps in STEPS.values():
        total = 0
        for step in steps.split():
            name, _, count = step.partition(":")
            base[name] = total
            total += int(count or 1)
    return base


BASE = bases()


class Own:

    def __init__(self, eng, sem):
        self.eng, self.sem, self.n, self.turns = eng, sem, 0, []

    def after(self, ins):
        ins.then_inc(self.sem, 1)
        self.n += 1
        value = self.n
        for t, per in self.turns:
            value = value + t * per
        self.eng.wait_ge(self.sem, value)

    def loop(self, count, per, body, first=0):
        n0 = self.n
        with self.eng.Fori(first, count) as t:
            if per:
                self.turns.append((t, per))
                self.n = n0 - first * per
            body(t)
            if per:
                self.turns.pop()
                assert self.n - (n0 - first * per) == per, (self.n - n0 + first * per, per)
        self.n = n0 + (count - first) * per


class Row:

    def __init__(self, nc, start):
        self.nc, self.at = nc, start

    def next(self, name, shape):
        t = self.nc.alloc_sbuf_tensor_at(name, [128] + shape, F32, offset=self.at)
        self.at += 4 * int(np.prod(shape))
        return t


class Memory:
    pass


def semaphores(nc, ctx, m):
    def sem(name):
        return ctx.enter_context(nc.semaphore(name))

    def sems(names):
        return [sem(name) for name in names.split()]

    m.l_id, m.l_par, m.l_x, m.l_hist, m.l_ab, m.l_pg = sems(
        "l_id l_par l_x l_hist l_ab l_pg")
    m.l_c0, m.l_c1, m.l_p, m.o_cs, m.o_lru = sems(
        "l_c0 l_c1 l_p o_cs o_lru")
    m.o_c, m.o_y, m.wh_done = sems(
        "o_c o_y wh_done")
    m.split_done, m.slot_used, m.act_own, m.dve_own, m.pool_own, m.ones_set = sems(
        "split_done slot_used act_own dve_own pool_own ones_set")
    m.x_tr, m.h_ready, m.fh_done, m.fl_done, m.ss_done, m.ss_mm = sems(
        "x_tr h_ready fh_done fl_done ss_done ss_mm")
    m.r_inv, m.r_ready, m.pre_ready, m.pre_saved, m.hist_in, m.conv_done = sems(
        "r_inv r_ready pre_ready pre_saved hist_in conv_done")
    m.conv_act, m.z_raw, m.z_act, m.ly_raw, m.ly_act, m.gate_mm = sems(
        "conv_act z_raw z_act ly_raw ly_act gate_mm")
    m.gate_act, m.mixh_done, m.mixl_done, m.head_end, m.g_stage, m.g_eb = sems(
        "gate_act mixh_done mixl_done head_end g_stage g_eb")
    m.g_diff, m.g_dec, m.g_row, m.g_tr, m.g_gram, m.g_bt1 = sems(
        "g_diff g_dec g_row g_tr g_gram g_bt1")
    m.g_t1, m.g_lt, m.g_q, m.g_qc, m.g_tb, m.g_inv = sems(
        "g_t1 g_lt g_q g_qc g_tb g_inv")
    m.g_v0, m.g_vn0, m.g_xs, m.g_xt, m.g_xtr, m.g_s1 = sems(
        "g_v0 g_vn0 g_xs g_xt g_xtr g_s1")
    m.g_s1c, m.g_x1, m.g_v1, m.g_vn1, m.g_rs, m.g_vs = sems(
        "g_s1c g_x1 g_v1 g_vn1 g_rs g_vs")
    m.g_vns, m.g_vm, m.g_s2, m.g_o, m.g_ds, m.s2_done = sems(
        "g_vns g_vm g_s2 g_o g_ds s2_done")
    m.s8_done, m.u_done, m.fuh_done, m.fu_done, m.p_tr, m.pt_done = sems(
        "s8_done u_done fuh_done fu_done p_tr pt_done")
    m.ph_done, m.pl_done, m.ple_mm, m.ple_ev, m.gt_raw, m.gt_act = sems(
        "ph_done pl_done ple_mm ple_ev gt_raw gt_act")
    m.c_raw, m.uq_ev, m.kv_t, m.kv_tc, m.kv_k, m.kv_q = sems(
        "c_raw uq_ev kv_t kv_tc kv_k kv_q")
    m.kv_ev, m.pa_stage, m.pa_s, m.pa_m, m.pa_e, m.pa_p = sems(
        "kv_ev pa_stage pa_s pa_m pa_e pa_p")
    m.pa_t, m.pa_tc, m.pa_o, m.pa_ah, m.patt_out, m.sa_stage = sems(
        "pa_t pa_tc pa_o pa_ah patt_out sa_stage")
    m.sa_t, m.sa_ckc, m.sa_kpc, m.sa_s, m.sa_nt, m.sa_m = sems(
        "sa_t sa_ckc sa_kpc sa_s sa_nt sa_m")
    m.sa_e, m.sa_p, m.sa_pt, m.sa_ptc, m.spv_mm, m.sa_acc = sems(
        "sa_e sa_p sa_pt sa_ptc spv_mm sa_acc")
    m.yn_done, m.y_tr, m.y_done = sems(
        "yn_done y_tr y_done")
    m.par_tr = m.hist_tr = m.cs_tr = m.lo_tr = m.l2_sum = m.l2_mm = m.scal_tr = m.on_sum = m.on_mm = m.c_mm = \
        m.kp_rot = m.ctok_tr = m.qp_rot = m.ckn_tr = sem("pe_steps")
    m.identr_set = m.lam_ln = m.lat_done = m.lroot_done = m.l2_sq = m.l2_rt = m.beta_e = m.a_ln = \
        m.eg_done = m.kde_done = m.on_sq = m.on_rt = m.c_sq = m.c_rt = m.cqh_done = m.ckh_done = m.ckn_done = m.ach_done \
        = m.atth_done = sem("act_steps")
    m.par_done = m.lam_abs = m.hist_done = m.ba_done = m.csr_done = m.lm_done = m.lt_done = \
        m.lo_done = m.ob_done = m.lrow_done = m.l2_inv = m.l2_done = m.beta_done = m.a_abs = m.gc_done = \
        m.dl_done = m.nbg_done = m.scal_done = m.on_inv = m.og_done = m.kpr_done = m.c_inv = \
        m.cn_done = m.cql_done = m.kpe_done = m.ckl_done = m.ctok_done = m.qp_done = m.acl_done = \
        m.attl_done = sem("dve_steps")
    m.g_bb, m.g_kd = sems("g_bb g_kd")
    m.sa_r, m.sa_av, m.sa_at = sems("sa_r sa_av sa_at")
    m.cache_full = [sem(f"cache_full{i}") for i in range(4)]
    m.w_full = [sem(f"w_full{i}") for i in range(4)]
    m.s8_full, m.o_s2, m.o_s8 = ([sem(f"{n}{i}") for i in range(2)] for n in ("s8_full", "o_s2", "o_s8"))
    m.gw_full = [sem(f"gw_full{i}") for i in range(2)]


def memory(nc, ctx):
    m = Memory()
    m.nc = nc
    semaphores(nc, ctx, m)

    def at(name, offset, shape, dt=F32):
        return nc.alloc_sbuf_tensor_at(name, [128] + shape, dt, offset=offset)

    K = 1024
    o = (nc.sbuf_base + 31) // 32 * 32
    end = nc.sbuf_usable_end // 32 * 32 - 320
    m.W = at("W", o, [4, 2048])
    m.Wh = at("Wh", o + 32 * K, [2, 2048], F32R)
    m.Wl = at("Wl", o + 48 * K, [2, 2048], F32R)
    o += 64 * K
    T1 = NT * 4
    R = KT * T1
    m.hT = at("hT", o, [KT, NT])
    oA, oB = o + R, o + 3 * R
    oAl, oBl = oA + R, oB + R
    m.Ah, m.Al = at("Ah", oA, [KT, NT], F32R), at("Al", oAl, [KT, NT], F32R)
    m.Bh, m.Bl = at("Bh", oB, [KT, NT], F32R), at("Bl", oBl, [KT, NT], F32R)
    o += 5 * R
    m.ident = at("ident", o, [128])
    m.identr = at("identr", o + 512, [128], F32R)
    m.ones = at("ones", o + 1024, [128])
    m.par = at("par", o + 1536, [320])
    o += 1536 + 1280
    oR = o
    m.rB = at("rB", o, [NT])
    m.ssacc = at("ssacc", o + T1, [2, NT])
    m.sqt = at("sqt", o + 3 * T1, [2, NT])
    o += 5 * T1
    oL = o
    m.bg = at("bg", o, [2, NT])
    m.betaR, m.gcR = m.bg[:, 0, :], m.bg[:, 1, :]
    m.gR = at("gR", o + 2 * T1, [NT])
    m.eR = at("eR", o + 3 * T1, [NT])
    o += 4 * T1
    m.conv = at("conv", o, [3 * HG, NT])
    m.xtok = at("xtok", o, [2, D_MODEL])
    m.xstok = at("xstok", o + 16 * K, [D_MODEL])
    o += 3 * HG * T1
    m.z = at("z", o, [HG, NT])
    m.hrow = at("hrow", o, [QKV + LRU])
    o += HG * T1
    oX = o
    m.xb = at("xb", o, [8, NT])
    m.ly = at("ly", o + 8 * T1, [8, NT])
    m.prow = at("prow", o + 8 * T1, [4, 128])
    m.hist = at("hist", oB, [32, 24])
    m.cs = at("cs", oB + 3 * K, [32, 27])
    m.pre = at("pre", oB + 8 * T1, [2, 2, PRE])
    m.acc = at("acc", oBl, [2, 2, PRE])
    m.lm = at("lm", oA, [2, 8, NT])
    m.la = at("la", oAl, [8, NT])
    m.lt = at("lt", oAl + 8 * T1, [8, NT])
    m.csrow = at("csrow", oAl, [4096])
    m.gw = at("gw", oBl, [2, 2, 128])
    m.cst0 = at("cst0", oBl + 2 * K, [NC0])
    m.lsp = at("lsp", oB + 6656, [4, 16])
    m.lo = at("lo", oB + 7168, [72])
    m.lrow = at("lrow", oB + 7680, [128])
    m.sqg = at("sqg", oA, [16, NT])
    m.scal = at("scal", oB, [HG, 12])
    m.rs16 = at("rs16", oB + 512, [NT])
    m.g = []
    rest = Row(nc, oAl)
    for x, start in enumerate((oX, oA)):
        g, p = Memory(), Row(nc, start)
        g.qkv, g.dec, g.BB = p.next(f"qkv{x}", [3, NT]), p.next(f"dec{x}", [NT]), p.next(f"BB{x}", [NT])
        g.AQ, g.Eb, g.qe = p.next(f"AQ{x}", [2, NT]), p.next(f"Eb{x}", [NT]), p.next(f"qe{x}", [NT])
        g.rows, g.Vm = at(f"rows{x}", p.at, [2, NT]), at(f"Vm{x}", p.at, [BS, 128])
        g.TT, g.Qs, g.Bt = p.next(f"TT{x}", [2, 2, 128]), p.next(f"Qs{x}", [2, 128]), p.next(f"Bt{x}", [2, 128])
        g.vn, g.S1 = p.next(f"vn{x}", [3, 128]), p.next(f"S1{x}", [128])
        g.Ts, g.Qss, g.Bts = p.next(f"Ts{x}", [2, NS]), p.next(f"Qss{x}", [NS]), p.next(f"Bts{x}", [NS])
        g.kq, g.XT, g.oS = p.next(f"kq{x}", [BS, 2, TS]), p.next(f"XT{x}", [NS]), p.next(f"oS{x}", [NS])
        g.sc1 = p.next(f"sc1{x}", [12])
        assert p.at <= start + 16 * T1
        g.S8, g.kd, g.vb = rest.next(f"S8{x}", [BS, 128]), rest.next(f"kd{x}", [3, 128]), rest.next(f"vb{x}", [3, 128])
        g.S2, g.R1, g.Rs = rest.next(f"S2{x}", [128]), rest.next(f"R1{x}", [128]), rest.next(f"Rs{x}", [128])
        m.g.append(g)
    assert rest.at <= oAl + 16 * T1
    o = oL
    m.u = at("u", o, [2, NT])
    m.usq = at("usq", o + 2 * T1, [2, NT])
    m.gt = at("gt", o + 4 * T1, [2, NT])
    m.ptok = at("ptok", o + 6 * T1, [3, PLE])
    m.pTh = at("pTh", o + 6 * T1 + 3072, [2, NT], F32R)
    m.pTl = at("pTl", o + 8 * T1 + 3072, [2, NT], F32R)
    m.ple = at("ple", o + 10 * T1 + 3072, [KT, NT])
    m.ytok = at("ytok", oA, [3, D_MODEL])
    o = oL
    m.cst1 = at("cst1", o, [NC1])
    o += (NC1 * 4 + 31) // 32 * 32
    m.cqh = at("cqh", o, [4, NT], F32R)
    m.cql = at("cql", o + 4 * T1, [4, NT], F32R)
    m.c = at("c", o + 8 * T1, [8, NT])
    m.qlat = at("qlat", o, [4, HM, NS])
    m.wukT = at("wukT", o + 8192, [2, 512])
    oq = o + 8192
    m.qs2 = at("qs2", oq, [2, SEQ])
    m.qp2 = at("qp2", oq + 2048, [SEQ])
    m.vs2 = at("vs2", oq + 3072, [2, 256])
    assert oq + 5120 <= o + 12 * T1
    m.qrs = at("qrs", oq, [BS, HM, TS])
    m.qls = at("qls", oq + 2048, [2, 4, HM, TS])
    m.qrs2 = at("qrs2", oq + 4096, [2, HM, TS])
    o += 16 * T1
    m.kpR = at("kpR", oA + 17 * T1, [NT])
    m.kpe = at("kpe", o, [NT])
    o += T1
    m.ckh = at("ckh", o, [4, NT], F32R)
    m.ckl = at("ckl", o + 4 * T1, [4, NT], F32R)
    m.sc2 = at("sc2", o, [2, 384])
    m.PT2 = at("PT2", o + 3072, [2, 384])
    m.mx2 = at("mx2", o + 6144, [4, 4])
    m.PT = at("PT", o, [NPG, 64])
    m.PTn = at("PTn", o + 2048, [64])
    m.nsc = at("nsc", o + 2304, [NS])
    m.mx8 = at("mx8", o + 2432, [2, 8])
    m.ckn = at("ckn", o + 2560, [512])
    m.acc64 = at("acc64", o + 4608, [512])
    o += 8 * T1
    m.qn = at("qn", o, [HM, NT])
    m.qp = at("qp", o + HM * T1, [8, NT])
    o -= 2 * K
    m.ckT = at("ckT", o, [4, PAST])
    m.kpT = at("kpT", o + 16 * K, [PAST])
    m.accT = at("accT", o + 20 * K, [4, HM, NS])
    assert o + 20 * K + 8192 <= end, (o + 20 * K + 8192, end)
    m.ach = at("ach", o, [4, HM, NS], F32R)
    m.acl = at("acl", o + 8 * K, [4, HM, NS], F32R)
    m.sc8 = at("sc8", oR, [PAST + NS])
    m.csq = at("csq", oA, [8, NT])
    m.rtmp = at("rtmp", oA, [8, NT])
    m.rc = at("rc", oA + 8 * T1, [2, NT])
    m.ctok = at("ctok", oA + 10 * T1, [3, 576])
    m.kno = at("kno", oB, [HM, SEQ])
    m.vtok = at("vtok", oB + 16 * K, [2, HM * VH])
    oW = (nc.sbuf_base + 31) // 32 * 32
    m.CK = [at(f"CK{r}", (oB if r > 1 else oW) + r % 2 * 16 * K, [NPG, KVLORA]) for r in range(4)]
    m.KP = [at(f"KP{r}", oB + 32 * K + (r - 2) * 2 * K if r > 1 else oW + 32 * K + r * 2 * K, [NPG, ROPE])
            for r in range(4)]
    m.pgs = at("pgs", end + 64, [64], I32)
    m.alog = at("alog", end, [4])

    m.ps = ctx.enter_context(nc.psum_tensor("ps", [128, 8, 512], F32))
    return m




def pieces(slot, w, x):
    if S_BA <= slot < S_BA + 2:
        return [(w[:, 0:128].rearrange("p (k g c) -> p k g c", k=8, g=2),
                 x[:, 0:512].rearrange("p (k g c) -> p k g c", k=8, g=2)[:, :, :, 0:8])]
    if S_KPE <= slot < S_KPE + 2:
        return [(w[:, 0:512].rearrange("p (k c) -> p k c", k=8).unsqueeze(2).to_broadcast([128, 8, 2, ROPE]),
                 x[:, 0:1024].rearrange("p (k g c) -> p k g c", k=8, g=2))]
    if S_UQ <= slot < S_UQ + 8:
        heads = w[:, 0:1536].rearrange("p (k h n) -> p k h n", k=4, h=2)
        blocks = x[:, 0:1536].rearrange("p (k n) -> p k n", k=4)
        return [(heads[:, :, :, 0:NOPE], blocks[:, :, 0:256].rearrange("p k (h n) -> p k h n", h=2)),
                (heads[:, :, :, NOPE:], blocks[:, :, 256:384].rearrange("p k (h n) -> p k h n", h=2))]
    return [(w, x)]


def ring(S, i):
    return (S + i) % 4


def sync_program(sp, m, a):

    def load(S, i, it, src, view=None):
        j = ring(S, i)
        if not (isinstance(it, int) and S + i + 4 * it < 4):
            sp.wait_ge(m.split_done, it * 4 + (S + i - 3))
        dst = m.W[:, j, :].rearrange("p (k n) -> p k n", k=8) if view is None else view(m.W[:, j, :])
        sp.dma_start(dst, src).then_inc(m.w_full[j], 16)

    def k16(S, w, col0, count, it0=0, rows=None, first=0):
        wv = w.rearrange("(k p) n -> p k n", p=128)

        def turn(t):
            for i in range(4):
                r = slice(8 * (i % 2), 8 * (i % 2) + 8) if rows is None else ds(rows + 8 * (i % 2), 8)
                load(S, i, it0 + t, wv[:, r, ds(t * 512 + (col0 + 256 * (i // 2)), 256)])
        for t in range(first):
            turn(t)
        with sp.Fori(first, count) as t:
            turn(t)

    def small(dst, src, s):
        sp.dma_start(dst, src).then_inc(s, 16)

    small(m.ident[:], a["ident"], m.l_id)
    small(m.prow[0:32, 0, :], a["norm_mix_g"].rearrange("l (k p) -> (l k) p", p=128), m.l_par)
    small(m.prow[32:64, 0, :], a["norm_ffn_g"].rearrange("l (k p) -> (l k) p", p=128), m.l_par)
    small(m.prow[64:80, 0, :], a["norm_final_g"].rearrange("(k p) -> k p", p=128), m.l_par)
    small(m.prow[0:96, 1, :], a["conv_qkv_w"][0].rearrange("w (k p) -> (w k) p", p=128), m.l_par)
    small(m.prow[0:32, 2, :], a["conv_lru_w"][0].rearrange("w (k p) -> (w k) p", p=128), m.l_par)
    small(m.prow[32:40, 2, :], a["conv_lru_b"].rearrange("l (k p) -> (l k) p", p=128), m.l_par)
    small(m.prow[40:48, 2, :], a["lru_ba"][0], m.l_par)
    small(m.prow[48:56, 2, :], a["lru_bi"][0], m.l_par)
    small(m.prow[56:64, 2, :], a["lru_lambda"].rearrange("l (k p) -> (l k) p", p=128), m.l_par)
    small(m.prow[64:65, 2, :], a["gdn_norm_g"], m.l_par)
    small(m.prow[65:69, 2, :], a["q_norm_g"].rearrange("l (k p) -> (l k) p", p=128), m.l_par)
    small(m.prow[69:73, 2, :], a["kv_norm_g"].rearrange("l (k p) -> (l k) p", p=128), m.l_par)
    small(m.prow[0:64, 3, :], a["state_lru"][0].rearrange("b (k p) -> (b k) p", p=128), m.l_par)
    small(m.xtok[:], a["x_prompt"][0].rearrange("(c p) n -> p c n", p=128), m.l_x)
    small(m.xstok[0:NS, :], a["x_sample"].rearrange("b t n -> (b t) n"), m.l_x)
    small(m.hrow[0:24, 0:QKV], a["state_gdn_conv"][0].rearrange("b w n -> (b w) n"), m.l_hist)
    small(m.hrow[0:24, QKV:], a["state_lru_conv"][0].rearrange("b w n -> (b w) n"), m.l_hist)
    small(m.alog[0:8, 0:1], a["gdn_a_log"][0].unsqueeze(1), m.l_ab)
    small(m.alog[0:8, 1:2], a["gdn_dt_bias"][0].unsqueeze(1), m.l_ab)
    small(m.pgs[0:1, :], a["page_table"].rearrange("b n -> (b n)").unsqueeze(0), m.l_pg)

    w = a["w_in_a"][0]
    k16(S_QKV, w, 0, 6, first=1)
    k16(S_Z, w, QKV, 2)
    wv = w.rearrange("(k p) n -> p k n", p=128)
    c0 = QKV + HG * DK
    for i in range(2):
        load(S_BA, i, 0, wv[:, 8 * i:8 * i + 8, c0:c0 + 16],
             lambda x: x[:, 0:128].rearrange("p (k c) -> p k c", k=8))
    k16(S_LX, w, c0 + 16, 2)
    k16(S_LY, w, c0 + 16 + LRU, 2)

    wo = a["w_out_a"][0]
    wov = wo.rearrange("(k p) n -> p k n", p=128)
    for i in range(4):
        load(S_OUT, i, 0, wov[:, 8 * (i % 2):8 * (i % 2) + 8, 256 * (i // 2):256 * (i // 2) + 256])

    sp.wait_ge(m.csr_done, BASE["csr_done"] + 2)
    small(a["gdn_conv_p"][0, 0], m.csrow[0:3, 0:QKV], m.o_cs)
    small(a["lru_conv_p"][0, 0], m.csrow[0:3, QKV:], m.o_cs)
    small(a["gdn_conv_s"][0].rearrange("b w n -> (b w) n"), m.csrow[3:27, 0:QKV], m.o_cs)
    small(a["lru_conv_s"][0].rearrange("b w n -> (b w) n"), m.csrow[3:27, QKV:], m.o_cs)

    def gates(t):
        for u in range(2):
            if not isinstance(t, int):
                sp.wait_ge(m.gate_mm, 2 * t + (u - 1))
            sp.dma_start(m.gw[:, u, 0, :], a["lru_wa"][0, ds(2 * t + u, 1), :, :].rearrange("k p n -> (k p) n")
                         ).then_inc(m.gw_full[u], 16)
            sp.dma_start(m.gw[:, u, 1, :], a["lru_wi"][0, ds(2 * t + u, 1), :, :].rearrange("k p n -> (k p) n")
                         ).then_inc(m.gw_full[u], 16)
    sp.wait_ge(m.conv_act, 16)
    gates(0)
    small(m.cst0[:], a["cst0"], m.l_c0)
    with sp.Fori(1, 4) as t:
        gates(t)
    sp.wait_ge(m.lrow_done, BASE["lrow_done"] + 1)
    small(a["lru_p"][0, 0].rearrange("(k p) -> k p", p=128), m.lrow[0:8, :], m.o_lru)
    small(a["lru_s"][0].rearrange("b (k p) -> (b k) p", p=128), m.lrow[8:72, :], m.o_lru)

    sp.wait_ge(m.l2_done, BASE["l2_done"] + 2)
    st = a["state_gdn"][0].rearrange("b h k v -> k b h v")
    so = a["gdn_s"][0].rearrange("b h k v -> k b h v")

    def heads(t):
        for x, g in enumerate(m.g):
            if not isinstance(t, int):
                sp.wait_ge(m.o_s8[x], 16 * t)
                sp.wait_ge(m.o_s2[x], 16 * t)
            sp.dma_start(g.S8[:], st[:, :, ds(2 * t + x, 1), :].rearrange("k b h v -> k b (h v)")
                         ).then_inc(m.s8_full[x], 16)
        for x, g in enumerate(m.g):
            sp.wait_ge(m.s2_done, 2 * t + (x + 1))
            sp.dma_start(a["gdn_p"][0, 0, ds(2 * t + x, 1), :, :].rearrange("h k v -> (h k) v"), g.S2[:]
                         ).then_inc(m.o_s2[x], 16)
        for x, g in enumerate(m.g):
            sp.wait_ge(m.s8_done, 2 * t + (x + 1))
            sp.dma_start(so[:, :, ds(2 * t + x, 1), :].rearrange("k b h v -> k b (h v)"), g.S8[:]
                         ).then_inc(m.o_s8[x], 16)
    heads(0)
    with sp.Fori(1, HG // 2) as t:
        heads(t)

    with sp.Fori(1, 4) as t:
        for i in range(4):
            load(S_OUT, i, t, wov[:, 8 * (i % 2):8 * (i % 2) + 8, ds(t * 512 + 256 * (i // 2), 256)])

    def mlp_and_inputs(layer, S, S_P, S_G):
        up, down = a["w_up"][layer], a["w_down"][layer]
        pp = a["p_prompt"][layer, 0].rearrange("(c p) n -> p c n", p=128)
        if layer == 0:
            sp.wait_ge(m.mixl_done, 2)
        else:
            sp.wait_ge(m.attl_done, BASE["attl_done"] + 1)
        small(m.ptok[:, 0:2, :], pp, m.l_p)
        small(m.ptok[0:NS, 2, :], a["p_sample"][layer].rearrange("b t n -> (b t) n"), m.l_p)
        upv = up.rearrange("(k p) n -> p k n", p=128)
        dnv = down.rearrange("(k p) n -> p k n", p=128)
        with sp.Fori(0, 4) as c:
            with sp.Fori(0, 4) as t:
                for i in range(4):
                    load(S, i, c * 8 + t, upv[:, 8 * (i % 2):8 * (i % 2) + 8,
                                              ds(c * 2048 + t * 512 + 256 * (i // 2), 256)])
            with sp.Fori(0, 4) as t:
                for i in range(4):
                    load(S, i, c * 8 + t + 4, dnv[:, ds(c * 16 + 8 * (i % 2), 8), ds(t * 512 + 256 * (i // 2), 256)])
        pv = a["w_ple"][layer].rearrange("(k p) n -> p k n", p=128)
        for i in range(2):
            load(S_P, i, 0, pv[:, :, 1024 * i:1024 * i + 1024], lambda x: x.rearrange("p (k n) -> p k n", k=2))
        k16(S_G, a["w_ple_gate"][layer], 0, 4)

    mlp_and_inputs(0, S_FFN0, S_PLE0, S_GATE0)

    w = a["w_in_c"][0]
    k16(S_INC, w, 0, 2)
    sp.wait_ge(m.pl_done, 1)
    small(m.cst1[:], a["cst1"], m.l_c1)
    wv = w.rearrange("(k p) n -> p k n", p=128)
    for i in range(2):
        load(S_KPE, i, 0, wv[:, 8 * i:8 * i + 8, 1024:1088],
             lambda x: x[:, 0:512].rearrange("p (k c) -> p k c", k=8))
    wq = a["w_uq"][0].rearrange("(k p) n -> p k n", p=128)
    with sp.Fori(0, 2) as t:
        for i in range(4):
            load(S_UQ, i, t, wq[:, :, ds(t * 1536 + 384 * i, 384)],
                 lambda x: x[:, 0:1536].rearrange("p (k n) -> p k n", k=4))
    wk = a["w_ukv"][0].rearrange("(k p) n -> p k n", p=128)
    with sp.Fori(0, 2) as t:
        for i in range(4):
            load(S_UKV, i, t, wk[:, :, ds(t * 2048 + 512 * i, 512)], lambda x: x.rearrange("p (k n) -> p k n", k=4))
    sp.wait_ge(m.ctok_done, BASE["ctok_done"] + 6)
    small(a["ckv_p"][0, 0].rearrange("(c p) n -> p c n", p=128), m.ctok[:, 0:2, 0:512], m.o_c)
    small(a["ckv_s"][0].rearrange("b t n -> (b t) n"), m.ctok[0:NS, 2, 0:512], m.o_c)
    small(a["kpe_p"][0, 0].rearrange("(c p) n -> p c n", p=128), m.ctok[:, 0:2, 512:576], m.o_c)
    small(a["kpe_s"][0].rearrange("b t n -> (b t) n"), m.ctok[0:NS, 2, 512:576], m.o_c)
    wk4 = a["w_ukv"][0].rearrange("(k p) (h g n) -> p k h g n", p=128, h=HM, g=2)
    cache_pages(sp, m, a)
    sp.wait_ge(m.spv_mm, 6)
    for i in range(4):
        load(S_OV, i, 0, wk4[:, i, :, 1, :], lambda x: x.rearrange("p (h n) -> p h n", h=HM))
    k16(S_WO, a["w_o_c"][0], 0, 4)
    mlp_and_inputs(1, S_FFN1, S_PLE1, S_GATE1)

    sp.wait_ge(m.y_done, 12)
    small(a["y_prompt"][0].rearrange("(c p) n -> p c n", p=128), m.ytok[:, 0:2, :], m.o_y)
    small(a["y_sample"].rearrange("b t n -> (b t) n"), m.ytok[0:NS, 2, :], m.o_y)
    for s, n in ((m.o_cs, 4), (m.o_lru, 2), *((s, HG // 2) for s in (*m.o_s2, *m.o_s8)), (m.o_c, 4), (m.o_y, 2)):
        sp.wait_ge(s, 16 * n)


def cache_pages(sp, m, a):
    ck, kp = a["cache_ckv"][0], a["cache_kpe"][0]
    sp.wait_ge(m.l_pg, 16)

    def samples(t):
        for r in range(4):
            if t:
                sp.wait_ge(m.spv_mm, 4 * t + (r - 3))
            elif r == 0:
                sp.wait_ge(m.split_done, S_OV)
                sp.wait_ge(m.slot_used, S_OV)
            elif r == 2:
                sp.wait_ge(m.patt_out, 8)
            for n in range(NPG):
                page = sp.value_load(m.pgs[0:1, ds(t * 4 * NPG + (r * NPG + n), 1)], min_val=0,
                                     max_val=ck.shape[0] - 1)
                sp.dma_start(m.CK[r][:, n, :], ck[ds(page, 1), :, :].rearrange("g p n -> (g p) n")
                             ).then_inc(m.cache_full[r], 16)
                sp.dma_start(m.KP[r][:, n, :], kp[ds(page, 1), :, :].rearrange("g p n -> (g p) n")
                             ).then_inc(m.cache_full[r], 16)
    for t in range(BS // 4):
        samples(t)


def tensor_program(pe, m):
    mm, tr = pe_matmul(m), pe_transpose(m)
    pe.sem_inc(m.pa_o, 1)
    ps = m.ps
    TOK = ((0, 128, 0), (128, 128, 1), (256, NS, 2))

    def products(out, wh, wl, xh, xl, start, stop):
        mm(out, wh, xh, start, False)
        mm(out, wh, xl, False, False)
        return mm(out, wl, xh, False, stop)

    def slot_parts(S, i, k):
        j = ring(S, i) % 2
        n = 2048 // k
        return m.Wh[:, j, :].rearrange("p (k n) -> p k n", n=n), m.Wl[:, j, :].rearrange("p (k n) -> p k n", n=n)

    def k16(S, it, Xh, Xl, x_ready, X0, cols=256):
        for u in range(len(cols) if isinstance(cols, tuple) else 2):
            b = 2 * ((S // 2 + u) % 2)
            for half in range(2):
                i = 2 * u + half
                wh, wl = slot_parts(S, i, 8)
                pe.wait_ge(m.split_done, it * 4 + (S + i + 1))
                for k in range(8):
                    kt = 8 * half + k
                    if kt % 2 == 0 and x_ready is not None:
                        pe.wait_ge(x_ready, X0 + (kt // 2 + 1))
                    for n in range(2):
                        last = products(ps[:, b + n, 0:NT], wh[:, k, 128 * n:128 * n + 128],
                                        wl[:, k, 128 * n:128 * n + 128], m_x(Xh, kt), m_x(Xl, kt), kt == 0, kt == 15)
                last.then_inc(m.slot_used, 1)

    def m_x(X, kt):
        return X[:, kt, :]

    def one_tile(S, Xh, Xl, x_ready, X0, width, cols):
        b = 2 * (S // 2 % 2)
        for half in range(2):
            j = ring(S, half) % 2
            wh, wl = (x[:, j, 0:8 * width].rearrange("p (k c) -> p k c", k=8) for x in (m.Wh, m.Wl))
            pe.wait_ge(m.split_done, S + half + 1)
            for k in range(8):
                kt = 8 * half + k
                if kt % 2 == 0 and x_ready is not None:
                    pe.wait_ge(x_ready, X0 + (kt // 2 + 1))
                last = products(ps[0:cols, b, 0:NT], wh[:, k, 0:cols], wl[:, k, 0:cols], m_x(Xh, kt), m_x(Xl, kt),
                                kt == 0, kt == 15)
            last.then_inc(m.slot_used, 1)

    def norm_sum(n):
        pe.wait_ge(m.ss_done, 8 * n + 8)
        if n:
            pe.wait_ge(m.r_inv, n)
        mm(ps[:, 7, 0:NT], m.ones[:], m.ssacc[:, 0, :], True, False)
        mm(ps[:, 7, 0:NT], m.ones[:], m.ssacc[:, 1, :], False, True).then_inc(m.ss_mm, 1)

    pe.wait_ge(m.l_id, 16)
    pe.wait_ge(m.l_par, 16 * 13)
    at = 0
    for g, rows in enumerate((80, 96, 73, 64)):
        last = tr(ps[:, 4, at:at + rows], m.prow[0:rows, g, :], rows)
        at += rows
    last.then_inc(m.par_tr, 1)
    pe.wait_ge(m.l_x, 32)
    for n in range(8):
        if n >= 2:
            pe.wait_ge(m.h_ready, n - 1)
        for i in range(2):
            b, d = 2 * (n % 2) + i, 2 * n + i
            for c in range(2):
                tr(ps[:, b, 128 * c:128 * c + 128], m.xtok[:, c, 128 * d:128 * d + 128], 128)
            last = tr(ps[:, b, 256:NT], m.xstok[0:NS, 128 * d:128 * d + 128], NS)
        last.then_inc(m.x_tr, 1)
    pe.wait_ge(m.l_hist, 32)
    for k in range(32):
        last = tr(ps[:, 5 + k // 16, 24 * (k % 16):24 * (k % 16) + 24], m.hrow[0:24, 128 * k:128 * k + 128], 24)
    last.then_inc(m.hist_tr, 1)
    pe.wait_ge(m.ones_set, 1)
    norm_sum(0)
    pe.wait_ge(m.h_ready, 8)

    A, B = (m.Ah, m.Al), (m.Bh, m.Bl)
    with pe.Fori(0, 6) as t:
        k16(S_QKV, t, *A, m.fl_done, 0)
    with pe.Fori(0, 2) as t:
        k16(S_Z, t, *A, None, 0)
    one_tile(S_BA, *A, None, 0, 64, 40)
    for S in (S_LX, S_LY):
        with pe.Fori(0, 2) as t:
            k16(S, t, *A, None, 0)

    pe.wait_ge(m.pre_saved, 16)
    for g in range(2):
        if g:
            pe.wait_ge(m.csr_done, BASE["csr_done"] + 1)
        for k in range(16):
            last = tr(ps[0:27, 4 + k // 4, 128 * (k % 4):128 * (k % 4) + 128], m.cs[:, 16 * g + k, :], 128)
        last.then_inc(m.cs_tr, 1)

    pe.wait_ge(m.csr_done, BASE["csr_done"] + 2)
    pe.wait_ge(m.conv_act, 16)

    def gates(t):
        for u in range(2):
            pe.wait_ge(m.gw_full[u], 32 * t + 32)
            if not isinstance(t, int):
                pe.wait_ge(m.gate_act, 2 * t + (u - 1))
            for g in range(2):
                last = mm(ps[:, 4 + 2 * u + g, 0:NT], m.gw[:, u, g, :], m.xb[:, ds(2 * t + u, 1), :], True, True)
            last.then_inc(m.gate_mm, 1)
    gates(0)
    with pe.Fori(1, 4) as t:
        gates(t)
    pe.wait_ge(m.lo_done, BASE["lo_done"] + 2)
    pe.wait_ge(m.gate_act, 8)
    tr(ps[0:72, 4, 0:128], m.lo[:], 128).then_inc(m.lo_tr, 1)

    sel = m.cst0[:, NC0 - NT - 4 * HG:NC0 - NT]

    def head_sums(count):
        for h in range(count):
            last = mm(ps[0:16, 5, 0:NT], sel[:, 15 - h:31 - h], m.sqg[:, h, :], h == 0, h == count - 1)
        return last

    def to_all(row, h):
        n = row.shape[0]
        return mm(ps[:, h % 8, 0:NT], m.ident[0:n, h:h + 1].to_broadcast([n, 128]), row, True, True)
    pe.wait_ge(m.l_c0, 16)
    pe.wait_ge(m.l2_sq, BASE["l2_sq"] + 2)
    head_sums(16).then_inc(m.l2_sum, 1)
    pe.wait_ge(m.lrow_done, BASE["lrow_done"] + 1)
    pe.wait_ge(m.l2_rt, BASE["l2_rt"] + 1)
    for g in range(2):
        if g:
            pe.wait_ge(m.l2_done, BASE["l2_done"] + 1)
        for h in range(HG):
            last = to_all(m.rs16[0:16, :], 8 * g + h)
        last.then_inc(m.l2_mm, 1)
    pe.wait_ge(m.l2_done, BASE["l2_done"] + 2)
    pe.wait_ge(m.nbg_done, BASE["nbg_done"] + 1)
    pe.wait_ge(m.kde_done, BASE["kde_done"] + 1)
    for q, row in enumerate((m.betaR, m.gR, m.eR, m.gcR)):
        for c0, n, c in TOK:
            last = tr(ps[0:n, 0, (q * 3 + c) * 8:(q * 3 + c) * 8 + 8], row[0:8, c0:c0 + n], 8)
    last.then_inc(m.scal_tr, 1)
    pe.wait_ge(m.scal_done, BASE["scal_done"] + 1)

    def heads(t):
        both = [(x, 4 * x, g, g.qkv[:, 0, :], g.qkv[:, 1, :], g.qkv[:, 2, :]) for x, g in enumerate(m.g)]
        for x, b, g, q, k, v in both:
            pe.wait_ge(m.g_stage, 2 * t + (x + 1))
            for d, y in ((0, k), (1, v)):
                for c0, n, c in TOK:
                    last = tr(ps[0:n, b + d, 128 * c:128 * c + 128], y[:, c0:c0 + n], 128)
            last.then_inc(m.g_tr, 1)
            pe.wait_ge(m.g_row, 2 * t + (x + 1))
            for d in range(2):
                last = mm(ps[:, b + 2 + d, 0:NT], m.ones[0:8, :], g.rows[0:8, 1 - d, :], True, True)
            last.then_inc(m.g_bb, 1)
        for x, b, g, q, k, v in both:
            pe.wait_ge(m.g_eb, 2 * t + (x + 1))
            for d, y in ((2, k), (3, q)):
                for c0, n, c in TOK:
                    last = mm(ps[0:n, b + d, c0:c0 + n], k[:, c0:c0 + n], y[:, c0:c0 + n], True, True)
            last.then_inc(m.g_gram, 1)
        for x, b, g, q, k, v in both:
            pe.wait_ge(m.g_kd, 2 * t + (x + 1))
            pe.wait_ge(m.g_bt1, 2 * t + (x + 1))
            for c in range(2):
                tr(ps[:, b, 128 * c:128 * c + 128], g.Bt[:, c, :], 128)
            tr(ps[0:NS, b + 1, 0:NS], g.Bts[0:NS, :], NS).then_inc(m.g_t1, 1)
        for n in range(1, LEVELS):
            for x, b, g, q, k, v in both:
                pe.wait_ge(m.g_lt, 12 * t + (2 * n + x - 1))
                for c in range(2):
                    last = mm(ps[:, b, 128 * c:128 * c + 128], g.AQ[:, 0, 128 * c:128 * c + 128], g.TT[:, 0, c, :],
                              True, True)
                if n == 1:
                    last = mm(ps[0:NS, b + 1, 0:NS], g.AQ[0:NS, 0, SEQ:NT], g.Ts[0:NS, 0, :], True, True)
                last.then_inc(m.g_q, 1)
            for x, b, g, q, k, v in both:
                pe.wait_ge(m.g_qc, 12 * t + (2 * n + x - 1))
                for c in range(2):
                    mm(ps[:, b + 2, 128 * c:128 * c + 128], g.TT[:, 1, c, :], g.Qs[:, c, :], True, True)
                    last = mm(ps[:, b + 2, 256 + 128 * c:384 + 128 * c], g.Qs[:, c, :], g.TT[:, 1, c, :], True, True)
                if n == 1:
                    mm(ps[0:NS, b + 3, 0:NS], g.Ts[0:NS, 1, :], g.Qss[0:NS, :], True, True)
                    last = mm(ps[0:NS, b + 3, NS:2 * NS], g.Qss[0:NS, :], g.Ts[0:NS, 1, :], True, True)
                last.then_inc(m.g_tb, 1)
        for x, b, g, q, k, v in both:
            pe.wait_ge(m.g_inv, 2 * t + (x + 1))
            mm(ps[:, b, 0:128], g.TT[:, 1, 0, :], g.vb[:, 0, :], True, True).then_inc(m.g_v0, 1)
        for x, b, g, q, k, v in both:
            pe.wait_ge(m.s8_full[x], 16 * t + 16)
            for s in range(BS):
                last = mm(ps[:, b + 3, 64 + 8 * s:72 + 8 * s], g.S8[:, s, :],
                          g.kq[:, s, :, :].rearrange("p a t -> p (a t)"), True, True)
            last.then_inc(m.g_xs, 1)
        for x, b, g, q, k, v in both:
            pe.wait_ge(m.g_vn0, 2 * t + (x + 1))
            mm(ps[:, b, 128:256], g.kd[:, 0, :], g.vn[:, 0, :], True, True).then_inc(m.g_s1, 1)
            mm(ps[:, b + 1, 0:128], g.vn[:, 0, :], g.AQ[:, 1, 0:128], True, True)
            pe.wait_ge(m.g_xt, 2 * t + (x + 1))
            tr(ps[0:NS, b + 1, 384:512], g.XT[:], 128).then_inc(m.g_xtr, 1)
        for x, b, g, q, k, v in both:
            pe.wait_ge(m.g_s1c, 2 * t + (x + 1))
            mm(ps[:, b + 2, 0:128], k[:, 128:256], g.S1[:], True, True).then_inc(m.g_x1, 1)
        for x, b, g, q, k, v in both:
            pe.wait_ge(m.g_rs, 2 * t + (x + 1))
            mm(ps[:, b + 2, 128:256], g.TT[:, 1, 1, :], g.R1[:], True, True).then_inc(m.g_v1, 1)
            mm(ps[0:NS, b + 3, 384:512], g.Ts[0:NS, 1, :], g.Rs[0:NS, :], True, True).then_inc(m.g_vs, 1)
        for x, b, g, q, k, v in both:
            pe.wait_ge(m.g_vn1, 2 * t + (x + 1))
            mm(ps[:, b, 256:384], g.kd[:, 1, :], g.vn[:, 1, :], True, True).then_inc(m.g_s2, 1)
            mm(ps[:, b + 1, 128:256], g.S1[:], g.qe[:, 128:256], True, False)
            mm(ps[:, b + 1, 128:256], g.vn[:, 1, :], g.AQ[:, 1, 128:256], False, True)
            pe.wait_ge(m.g_vns, 2 * t + (x + 1))
            mm(ps[:, b + 1, 256:NT], g.vn[0:NS, 2, :], g.AQ[0:NS, 1, 256:NT], True, True).then_inc(m.g_o, 1)
        for x, b, g, q, k, v in both:
            pe.wait_ge(m.g_vm, 2 * t + (x + 1))
            for d in range(2):
                last = mm(ps[:, b + 2 + d, :], g.kd[0:NS, 2, :],
                          g.Vm[0:NS, 4 * d:4 * d + 4, :].rearrange("p b v -> p (b v)"), True, True)
            last.then_inc(m.g_ds, 1)
    with pe.Fori(0, HG // 2) as t:
        heads(t)
    pe.wait_ge(m.head_end, HG + 2)
    pe.wait_ge(m.on_sq, BASE["on_sq"] + 1)
    head_sums(HG).then_inc(m.on_sum, 1)
    pe.wait_ge(m.on_rt, BASE["on_rt"] + 1)
    for h in range(HG):
        last = to_all(m.rs16[0:8, :], h)
    last.then_inc(m.on_mm, 1)

    pe.wait_ge(m.og_done, BASE["og_done"] + 1)
    pe.wait_ge(m.mixl_done, 2)
    with pe.Fori(0, 4) as t:
        k16(S_OUT, t, *B, None, 0)
    norm_sum(1)

    def mlp(layer, S, S_P, S_G, X, Y, X0, U0):
        with pe.Fori(0, 4) as c:
            with pe.Fori(0, 4) as t:
                k16(S, c * 8 + t, *X, m.fl_done, X0)
            with pe.Fori(0, 4) as t:
                k16(S, c * 8 + t + 4, *Y, m.fu_done, c * 8 + U0)
        pe.wait_ge(m.l_p, 32 * layer + 32)
        for d in range(2):
            for c in range(2):
                tr(ps[:, 4 + d, 128 * c:128 * c + 128], m.ptok[:, c, 128 * d:128 * d + 128], 128)
            last = tr(ps[:, 4 + d, 256:NT], m.ptok[0:NS, 2, 128 * d:128 * d + 128], NS)
        last.then_inc(m.p_tr, 1)
        pe.wait_ge(m.pl_done, layer + 1)
        pe.wait_ge(m.h_ready, 24 * layer + 24)
        for i in range(2):
            wh, wl = slot_parts(S_P, i, 2)
            pe.wait_ge(m.split_done, S_P + i + 1)
            for n in range(4):
                q = 4 * i + n
                b = 2 * ((S_P // 2 + n) % 2)
                if q >= 2:
                    pe.wait_ge(m.ple_ev, 8 * layer + q - 1)
                for o in range(2):
                    c0 = 256 * n + 128 * o
                    for k in range(2):
                        last = products(ps[:, b + o, 0:NT], wh[:, k, c0:c0 + 128], wl[:, k, c0:c0 + 128],
                                        m.pTh[:, k, :], m.pTl[:, k, :], k == 0, k == 1)
                last.then_inc(m.slot_used if n == 3 else m.ple_mm, 1)
        pe.wait_ge(m.ple_ev, 8 * layer + 8)
        with pe.Fori(0, 4) as t:
            k16(S_G, t, *X, m.fl_done, X0 + 8)

    mlp(0, S_FFN0, S_PLE0, S_GATE0, A, B, 8, 0)
    norm_sum(2)

    with pe.Fori(0, 2) as t:
        k16(S_INC, t, *B, m.fl_done, 24)
    one_tile(S_KPE, *B, None, 0, 128, 128)
    for g in range(2):
        pe.wait_ge(m.c_sq, BASE["c_sq"] + g + 1)
        for k in range(4):
            last = mm(ps[:, 4 + g, 0:NT], m.ones[:], m.csq[:, 4 * g + k, :], k == 0, k == 3)
        last.then_inc(m.c_mm, 1)
    pe.wait_ge(m.kpr_done, BASE["kpr_done"] + 1)
    pe.wait_ge(m.l_c1, 16)
    ROT = m.cst1[:, NC1 - 128:NC1]
    mm(ps[:, 6, 0:NT], ROT, m.kpR[:], True, True).then_inc(m.kp_rot, 1)
    pe.wait_ge(m.cn_done, BASE["cn_done"] + 1)
    pe.wait_ge(m.kpe_done, BASE["kpe_done"] + 1)
    for c0, n, c in TOK:
        for k in range(4):
            last = tr(ps[0:n, (0, 1, 2)[c], 128 * k:128 * k + 128], m.c[:, 4 + k, c0:c0 + n], 128)
        last.then_inc(m.ctok_tr, 1)
    for c0, n, c in TOK:
        last = tr(ps[0:n, 7, 64 * c:64 * c + 64], m.kpe[0:64, c0:c0 + n], 64)
    last.then_inc(m.ctok_tr, 1)
    pe.wait_ge(m.ctok_done, BASE["ctok_done"] + 6)

    pe.wait_ge(m.cql_done, BASE["cql_done"] + 1)
    with pe.Fori(0, 2) as t:
        for i in range(4):
            j = ring(S_UQ, i) % 2
            wh, wl = (x[:, j, 0:1536].rearrange("p (k n) -> p k n", k=4) for x in (m.Wh, m.Wl))
            pe.wait_ge(m.split_done, t * 4 + (S_UQ + i + 1))
            b = 4 * (i % 2)
            for n in range(3):
                for k in range(4):
                    last = products(ps[:, b + n, 0:NT], wh[:, k, 128 * n:128 * n + 128],
                                    wl[:, k, 128 * n:128 * n + 128], m.cqh[:, k, :], m.cql[:, k, :], k == 0, k == 3)
            last.then_inc(m.slot_used, 1)
    pe.wait_ge(m.uq_ev, 8)
    for k in range(8):
        last = mm(ps[:, k, 0:NT], ROT, m.qp[:, k, :], True, True)
    last.then_inc(m.qp_rot, 1)

    pe.wait_ge(m.qp_done, BASE["qp_done"] + 1)
    pe.wait_ge(m.ckl_done, BASE["ckl_done"] + 1)
    pe.wait_ge(m.identr_set, BASE["identr_set"] + 1)
    with pe.Fori(0, 2) as t:
        for i in range(4):
            j = ring(S_UKV, i) % 2
            wh = m.Wh[:, j, :].rearrange("p (k h g n) -> p k h g n", k=4, h=2, g=2)
            wl = m.Wl[:, j, :].rearrange("p (k h g n) -> p k h g n", k=4, h=2, g=2)
            pe.wait_ge(m.split_done, t * 4 + (S_UKV + i + 1))
            pe.wait_ge(m.kv_ev, 4 * t + (i + 1))
            for h in range(2):
                for k in range(4):
                    mm(ps[:, h, 128 * k:128 * k + 128], wh[:, k, h, 0, :], m.identr[:], True, False)
                    last = mm(ps[:, h, 128 * k:128 * k + 128], wl[:, k, h, 0, :], m.identr[:], False, True)
            last.then_inc(m.kv_t, 1)
            for h in range(2):
                for k in range(4):
                    last = products(ps[:, 2, 256 * h:256 * h + 256], wh[:, k, h, 0, :], wl[:, k, h, 0, :],
                                    m.ckh[:, k, 0:SEQ], m.ckl[:, k, 0:SEQ], k == 0, k == 3)
            last.then_inc(m.kv_k, 1)
            for c in range(2):
                o = ps[:, 3, 256 * c:256 * c + 256]
                for k in range(4):
                    xh, xl = m.ckh[:, k, 128 * c:128 * c + 128], m.ckl[:, k, 128 * c:128 * c + 128]
                    mm(o, xh, wh[:, k, :, 1, :], k == 0, False)
                    mm(o, xh, wl[:, k, :, 1, :], False, False)
                    last = mm(o, xl, wh[:, k, :, 1, :], False, k == 3)
            last.then_inc(m.slot_used, 1)
            pe.wait_ge(m.kv_tc, 4 * t + (i + 1))
            for h in range(2):
                for k in range(4):
                    last = mm(ps[:, 4, 128 * h + 32 * k:128 * h + 32 * k + 32], m.wukT[:, h, 128 * k:128 * k + 128],
                              m.qn[:, ds(t * 8 + (2 * i + h), 1), SEQ:NT], True, True)
            last.then_inc(m.kv_q, 1)

    pe.wait_ge(m.kv_ev, 9)
    with pe.Fori(0, 8) as t:
        pe.wait_ge(m.pa_stage, 2 * t + 2)
        for u in range(2):
            qp, kp = m.qp2[64 * u:64 * u + 64, :], m.kpe[64 * u:64 * u + 64, :]
            for c0, at, n in ((0, 0, 128), (128, 128, 256)):
                mm(ps[:, u, at:at + n], m.qs2[:, u, c0:c0 + 128], m.kno[:, ds(2 * t + u, 1), 0:n], True, False)
                last = mm(ps[:, u, at:at + n], qp[:, c0:c0 + 128], kp[:, 0:n], False, True)
            last.then_inc(m.pa_s, 1)
        for u in range(2):
            pe.wait_ge(m.pa_p, 2 * t + (u + 1))
            for g in range(3):
                last = tr(ps[:, 2 + u, 128 * g:128 * g + 128], m.sc2[:, u, 128 * g:128 * g + 128], 128)
            last.then_inc(m.pa_t, 1)
        for u in range(2):
            pe.wait_ge(m.pa_tc, 2 * t + (u + 1))
            mm(ps[:, 4 + u, 0:128], m.vs2[:, 0, 128 * u:128 * u + 128], m.PT2[:, u, 0:128], True, True)
            mm(ps[:, 4 + u, 128:256], m.vs2[:, 0, 128 * u:128 * u + 128], m.PT2[:, u, 128:256], True, False)
            last = mm(ps[:, 4 + u, 128:256], m.vs2[:, 1, 128 * u:128 * u + 128], m.PT2[:, u, 256:384], False, True)
        last.then_inc(m.pa_o, 1)

    pe.wait_ge(m.patt_out, 8)
    for k in range(4):
        last = tr(ps[0:NS, 3, 128 * k:128 * k + 128], m.c[:, 4 + k, SEQ:NT], 128)
    last.then_inc(m.ckn_tr, 1)

    def scores(t, i):
        qr = m.qrs2[0:64, i % 2, :, :].rearrange("p h t -> p (h t)")
        ql = [m.qls[:, i % 2, k, :, :].rearrange("p h t -> p (h t)") for k in range(4)]
        pe.wait_ge(m.cache_full[i], 256 * t + 256)
        pe.wait_ge(m.sa_acc, 4 * t + max(i, 1))
        pe.wait_ge(m.sa_stage, 4 * t + (i + 1))
        for n in range(NPG):
            if n >= 2:
                pe.wait_ge(m.sa_ckc, 32 * t + (8 * i + n - 1))
            if n == 4:
                pe.wait_ge(m.sa_kpc, 8 * t + (2 * i + 1))
            for k in range(4):
                tr(ps[:, 4 + n % 2, 128 * k:128 * k + 128], m.CK[i][:, n, 128 * k:128 * k + 128], 128)
            tr(ps[0:64, 6, 128 * (n % 4):128 * (n % 4) + 128], m.KP[i][:, n, :], 128).then_inc(m.sa_t, 1)
        pe.wait_ge(m.sa_ckc, 32 * t + (8 * i + 8))
        pe.wait_ge(m.sa_kpc, 8 * t + (2 * i + 2))
        if i:
            pe.wait_ge(m.sa_e, 4 * t + i)
        for o, ck, kp in ((ps[0:64, 0, :], m.ckT[:, :, 0:512], m.kpT[0:64, 0:512]),
                          (ps[0:64, 1, :], m.ckT[:, :, 512:1024], m.kpT[0:64, 512:1024]),
                          (ps[0:64, 2, 0:NS], m.c[:, 4:8, SEQ:NT], m.kpe[0:64, SEQ:NT])):
            for k in range(4):
                mm(o, ql[k], ck[:, k, :], k == 0, False)
            last = mm(o, qr, kp, False, True)
        last.then_inc(m.sa_s, 1)

    def values(t, i):
        if i == 3:
            pe.wait_ge(m.sa_acc, 4 * t + 4)
        pe.wait_ge(m.sa_e, 4 * t + (i + 1))
        mm(ps[:, 3, 0:64], m.sc8[0:64, 0:128], m.ident[0:64, 0:64], True, True)
        for n in range(1, NPG):
            tr(ps[:, 3, 64 * n:64 * n + 64], m.sc8[0:64, 128 * n:128 * n + 128], 128)
        tr(ps[0:NS, 6, 0:64], m.sc8[0:64, PAST:PAST + NS], 64).then_inc(m.sa_pt, 1)
        pe.wait_ge(m.sa_ptc, 4 * t + (i + 1))
        pe.wait_ge(m.sa_nt, 4 * t + (i + 1))
        for n in range(NPG):
            mm(ps[0:64, 7, :], m.PT[:, n, :], m.CK[i][:, n, :], n == 0, False)
        mm(ps[0:64, 7, :], m.PTn[0:NS, :], m.ckn[0:NS, :], False, True).then_inc(m.spv_mm, 1)
        pe.wait_ge(m.sa_av, 4 * t + (i + 1))
        mm(ps[:, 6, 128:192], m.acc64[0:64, 0:128], m.ident[0:64, 0:64], True, True)
        for k in range(1, 4):
            last = tr(ps[:, 6, 128 + 64 * k:192 + 64 * k], m.acc64[0:64, 128 * k:128 * k + 128], 64)
        last.then_inc(m.sa_at, 1)
    pe.wait_ge(m.ckn_done, BASE["ckn_done"] + 1)
    with pe.Fori(0, 2) as t:
        for i in range(4):
            scores(t, i)
            if i:
                values(t, i - 1)
        values(t, 3)

    pe.wait_ge(m.acl_done, BASE["acl_done"] + 1)
    for i in range(4):
        j = ring(S_OV, i) % 2
        wh = m.Wh[:, j, :].rearrange("p (h n) -> p h n", h=HM)
        wl = m.Wl[:, j, :].rearrange("p (h n) -> p h n", h=HM)
        pe.wait_ge(m.split_done, S_OV + i + 1)
        for h in range(HM):
            last = products(ps[:, 0, NS * h:NS * h + NS], wh[:, h, :], wl[:, h, :], m.ach[:, i, h, :],
                            m.acl[:, i, h, :], i == 0 and h == 0, i == 3 and h == HM - 1)
        last.then_inc(m.slot_used, 1)
    pe.wait_ge(m.attl_done, BASE["attl_done"] + 1)
    with pe.Fori(0, 4) as t:
        k16(S_WO, t, *A, None, 0)
    norm_sum(3)
    mlp(1, S_FFN1, S_PLE1, S_GATE1, B, A, 32, 32)
    norm_sum(4)
    for g in range(4):
        pe.wait_ge(m.yn_done, 4 * g + 4)
        if g >= 2:
            pe.wait_ge(m.y_done, 3 * g - 3)
        for c0, n, c in TOK:
            for k in range(4):
                last = tr(ps[0:n, 3 * (g % 2) + c, 128 * k:128 * k + 128], m.hT[:, 4 * g + k, c0:c0 + n], 128)
            last.then_inc(m.y_tr, 1)


def pe_matmul(m):
    def mm(out, w, x, start, stop):
        if len(x.shape) == 3 and x.shape[1] == 1:
            x = x.rearrange("p a n -> p (a n)")
        return m.nc.tensor.matmul(out, w, x, start=start, stop=stop)
    return mm


def pe_transpose(m):
    def tr(out, x, rows):
        return m.nc.tensor.transpose(out, x, m.ident[0:x.shape[0], 0:x.shape[0]])
    return tr


def split_value(S, i, it):
    return 16 * ((S + i) // 4 + 1) + it * 16


def scalar_program(act, m):
    ps = m.ps
    A = m.nc.scalar.activation
    own = Own(act, m.act_own)

    def split(S, i, it):
        s = S + i
        j = ring(S, i)
        act.wait_ge(m.w_full[j], split_value(S, i, it))
        if not (isinstance(it, int) and s + 4 * it < 2):
            act.wait_ge(m.slot_used, it * 4 + (s - 1))
        for w, x in pieces(s + 4 * it if isinstance(it, int) else -1, m.W[:, j, :], m.Wh[:, j % 2, :]):
            last = A(x, w, ACT.Copy)
        last.then_inc(m.wh_done, 1)

    def k16(S, it, evac, more=True):
        for u in range(2):
            if more or u == 0:
                split(S, 2 * u + 2, it)
                split(S, 2 * u + 3, it)
            if evac:
                evac(u)

    def f_round(n, F, gcol, Xh):
        act.wait_ge(m.h_ready, n + (8 * F + 1))
        for i in range(2):
            g = 1.0 if gcol is None else m.par[:, ds(n * 2 + (gcol + i), 1)]
            last = A(Xh[:, ds(n * 2 + i, 1), :], m.hT[:, ds(n * 2 + i, 1), :], ACT.Copy, scale=g)
        last.then_inc(m.fh_done, 1)

    def root(n):
        act.wait_ge(m.r_inv, n + 1)
        A(m.rB[:], m.rB[:], ACT.Sqrt).then_inc(m.r_ready, 1)

    act.wait_ge(m.l_id, 16)
    A(m.identr[:], m.ident[:], ACT.Copy).then_inc(m.identr_set, 1)
    split(0, 0, 0)
    split(0, 1, 0)
    act.wait_ge(m.lam_abs, BASE["lam_abs"] + 1)
    own.after(A(m.lsp[:, 1, 0:8], m.lsp[:, 0, 8:16], ACT.Exp, scale=-1.0))
    A(m.lsp[:, 1, 8:16], m.lsp[:, 1, 0:8], ACT.Ln, bias=1.0).then_inc(m.lam_ln, 1)
    act.wait_ge(m.par_done, BASE["par_done"] + 1)
    with act.Fori(0, 8) as n:
        f_round(n, 0, C_MIX, m.Ah)
    root(0)

    def conv(n, k, dst):
        u = 0 if k is None else k[1]
        act.wait_ge(m.conv_done, n + 1)
        tail = m.acc[:, u, :, PADS:PRE].rearrange("p i (b s) -> p i b s", s=7)[:, :, :, 0:TS]
        if dst is m.conv:
            A(dst[:, ds(k[0] * 2, 2), 0:SEQ], m.acc[:, u, :, 0:SEQ], ACT.Silu)
            A(dst[:, ds(k[0] * 2, 2), SEQ:NT].rearrange("p i (b t) -> p i b t", t=TS), tail, ACT.Silu
              ).then_inc(m.conv_act, 1)
        else:
            for i in range(2):
                b = m.par[:, ds(k[0] * 2 + (C_LB + i), 1)]
                A(dst[:, ds(k[0] * 2 + i, 1), 0:SEQ].rearrange("p i n -> p (i n)"), m.acc[:, u, i, 0:SEQ],
                  ACT.Identity, bias=b)
                last = A(dst[:, ds(k[0] * 2 + i, 1), SEQ:NT].rearrange("p i (b t) -> p (i b) t", t=TS), tail[:, i],
                         ACT.Identity, bias=b)
            last.then_inc(m.conv_act, 1)

    with act.Fori(0, 6) as t:
        k16(S_QKV, t, lambda u: conv(t * 2 + u, (t * 2 + u, u), m.conv))

    def gated(x, func, raw, done):
        def turn(t):
            def evac(u):
                act.wait_ge(raw, t * 2 + (u + 1))
                A(x[:, ds(t * 4 + 2 * u, 2), :], x[:, ds(t * 4 + 2 * u, 2), :], func).then_inc(done, 1)
            return evac
        return turn
    zt, lyt = gated(m.z, ACT.Silu, m.z_raw, m.z_act), gated(m.ly, ACT.Gelu_apprx_tanh, m.ly_raw, m.ly_act)
    for t in range(2):
        k16(S_Z, t, zt(t))
    split(S_BA, 2, 0)
    split(S_BA, 3, 0)
    with act.Fori(0, 2) as t:
        k16(S_LX, t, lambda u: conv(t * 2 + (12 + u), (t * 2 + u, u), m.xb))
    with act.Fori(0, 2) as t:
        k16(S_LY, t, lyt(t))

    def gates(t):
        for u in range(2):
            act.wait_ge(m.gate_mm, 2 * t + (u + 1))
            for g in range(2):
                last = A(m.lm[:, g, ds(2 * t + u, 1), :].rearrange("p k n -> p (k n)"), ps[:, 4 + 2 * u + g, 0:NT],
                         ACT.Sigmoid, bias=m.par[:, ds(2 * t + (u + 8 * g + C_BA), 1)])
            last.then_inc(m.gate_act, 1)
    with act.Fori(0, 4) as t:
        gates(t)
    act.wait_ge(m.o_cs, 64)
    act.wait_ge(m.lm_done, BASE["lm_done"] + 1)
    A(m.la[:], m.lm[:, 0], ACT.Exp, scale=-1.0)
    A(m.lt[:], m.lm[:, 0], ACT.Tanh).then_inc(m.lat_done, 1)
    act.wait_ge(m.lt_done, BASE["lt_done"] + 1)
    A(m.lt[:], m.lt[:], ACT.Sqrt).then_inc(m.lroot_done, 1)
    act.wait_ge(m.ob_done, BASE["ob_done"] + 1)
    A(m.Bh[:, 8:16, :], m.la[:], ACT.Copy).then_inc(m.mixh_done, 1)

    act.wait_ge(m.conv_act, 12)
    for g in range(2):
        A(m.sqg[:, 8 * g:8 * g + 8, :], m.conv[:, 8 * g:8 * g + 8, :], ACT.Square).then_inc(m.l2_sq, 1)
    act.wait_ge(m.l2_inv, BASE["l2_inv"] + 1)
    A(m.rs16[0:16, :], m.rs16[0:16, :], ACT.Sqrt, scale=m.cst0[0:16, NC0 - NT - 1:NC0 - NT]).then_inc(m.l2_rt, 1)
    act.wait_ge(m.ba_done, BASE["ba_done"] + 1)
    A(m.betaR[0:8, :], m.betaR[0:8, :], ACT.Exp, scale=-1.0).then_inc(m.beta_e, 1)
    act.wait_ge(m.l_ab, 32)
    A(m.alog[0:8, 2:3], m.alog[0:8, 0:1], ACT.Exp)
    act.wait_ge(m.a_abs, BASE["a_abs"] + 1)
    own.after(A(m.eR[0:8, :], m.eR[0:8, :], ACT.Exp, scale=-1.0))
    A(m.eR[0:8, :], m.eR[0:8, :], ACT.Ln, bias=1.0).then_inc(m.a_ln, 1)
    act.wait_ge(m.gc_done, BASE["gc_done"] + 1)
    A(m.gR[0:8, :], m.gcR[0:8, :], ACT.Exp).then_inc(m.eg_done, 1)
    act.wait_ge(m.dl_done, BASE["dl_done"] + 1)
    A(m.eR[0:8, :], m.eR[0:8, :], ACT.Exp).then_inc(m.kde_done, 1)

    conv3 = m.conv[:].rearrange("p (a h) n -> p a h n", a=3)

    def heads(t):
        both = [(x, 4 * x, g) for x, g in enumerate(m.g)]
        for x, b, g in both:
            act.wait_ge(m.head_end, 2 * t + (x + 1))
            A(g.qkv[:], conv3[:, :, ds(2 * t + x, 1), :].rearrange("p a h n -> p a (h n)"), ACT.Copy
              ).then_inc(m.g_stage, 1)
        for x, b, g in both:
            act.wait_ge(m.g_row, 2 * t + (x + 1))
            act.wait_ge(m.g_tr, 2 * t + (x + 1))
            for c, n in ((0, 128), (1, 128), (2, NS)):
                last = A(g.kd[0:n, c, :], ps[0:n, b, 128 * c:128 * c + 128], ACT.Copy,
                         scale=g.sc1[0:n, 6 + c:7 + c])
            last.then_inc(m.g_kd, 1)
        for x, b, g in both:
            act.wait_ge(m.g_diff, 2 * t + (x + 1))
            A(g.Eb[:], ps[:, b + 2, 0:NT], ACT.Exp).then_inc(m.g_eb, 1)
            A(g.dec[:, 0:SEQ], g.dec[:, 0:SEQ], ACT.Exp)
            A(g.dec[0:NS, SEQ:NT], g.dec[0:NS, SEQ:NT], ACT.Exp).then_inc(m.g_dec, 1)
        for x, b, g in both:
            act.wait_ge(m.g_v0, 2 * t + (x + 1))
            A(g.vn[:, 0, :], ps[:, b, 0:128], ACT.Copy).then_inc(m.g_vn0, 1)
        for x, b, g in both:
            act.wait_ge(m.g_xs, 2 * t + (x + 1))
            old = ps[:, b + 3, 64:128].rearrange("p (b a t) -> p b a t", b=BS, a=2)
            A(g.XT[:].rearrange("p (b t) -> p b t", b=BS), old[:, :, 0, :], ACT.Copy).then_inc(m.g_xt, 1)
            A(g.oS[:].rearrange("p (b t) -> p b t", b=BS), old[:, :, 1, :], ACT.Copy)
        for x, b, g in both:
            act.wait_ge(m.g_s1, 2 * t + (x + 1))
            A(g.S1[:], ps[:, b, 128:256], ACT.Copy).then_inc(m.g_s1c, 1)
        for x, b, g in both:
            act.wait_ge(m.g_v1, 2 * t + (x + 1))
            A(g.vn[:, 1, :], ps[:, b + 2, 128:256], ACT.Copy).then_inc(m.g_vn1, 1)
            act.wait_ge(m.g_vs, 2 * t + (x + 1))
            A(g.vn[0:NS, 2, :], ps[0:NS, b + 3, 384:512], ACT.Copy).then_inc(m.g_vns, 1)
    with act.Fori(0, HG // 2) as t:
        heads(t)

    act.wait_ge(m.head_end, HG + 2)
    A(m.sqg[:, 0:8, :], m.conv[:, 0:8, :], ACT.Square).then_inc(m.on_sq, 1)
    act.wait_ge(m.on_inv, BASE["on_inv"] + 1)
    A(m.rs16[0:8, :], m.rs16[0:8, :], ACT.Sqrt).then_inc(m.on_rt, 1)
    act.wait_ge(m.og_done, BASE["og_done"] + 1)
    act.wait_ge(m.o_lru, 32)
    A(m.Bh[:, 0:8, :], m.conv[:, 0:8, :], ACT.Copy).then_inc(m.mixh_done, 1)

    for x in range(2):
        act.wait_ge(m.o_s2[x], 16 * HG // 2)
        act.wait_ge(m.o_s8[x], 16 * HG // 2)
    with act.Fori(0, 4) as t:
        k16(S_OUT, t, lambda u: f_round(t * 2 + u, 1, C_FFN, m.Ah))
    root(1)

    def mlp(layer, S, S_P, S_G, Xh, Yh, F):
        def up(c, t):
            def evac(u):
                act.wait_ge(m.u_done, c * 8 + t * 2 + (32 * layer + u + 1))
                own.after(A(m.usq[:], m.u[:], ACT.Square))
                A(Yh[:, ds(t * 4 + 2 * u, 2), :], m.usq[:], ACT.Copy).then_inc(m.fuh_done, 1)
            return evac

        def chunk(c):
            own.loop(4, 2, lambda t: k16(S, c * 8 + t, up(c, t)))
            with act.Fori(0, 4) as t:
                k16(S, c * 8 + t + 4, None)
        own.loop(3, 8, chunk)
        own.loop(4, 2, lambda t: k16(S, t + 24, up(3, t)))
        with act.Fori(0, 4) as t:
            k16(S, t + 28, lambda u: f_round(t * 2 + u, F, None, Xh))
        act.wait_ge(m.pt_done, layer + 1)
        A(m.pTh[:], m.usq[:], ACT.Copy).then_inc(m.ph_done, 1)
        split(S_P, 2, 0)
        split(S_P, 3, 0)

        def gate(t, last):
            def evac(u):
                n = t * 2 + u
                act.wait_ge(m.gt_raw, n + (8 * layer + 1))
                A(m.gt[:], m.gt[:], ACT.Sigmoid).then_inc(m.gt_act, 1)
                if layer == 0:
                    f_round(n, F + 1, C_MIX + 16, Yh)
            k16(S_G, t, evac, more=not last)
        with act.Fori(0, 3 + (layer == 0)) as t:
            gate(t, False)
        if layer:
            gate(3, True)

    mlp(0, S_FFN0, S_PLE0, S_GATE0, m.Ah, m.Bh, 2)
    root(2)

    for t in range(2):
        k16(S_INC, t, None)
    split(S_KPE, 2, 0)
    split(S_KPE, 3, 0)
    act.wait_ge(m.c_raw, 4)
    for g in range(2):
        A(m.csq[:, 4 * g:4 * g + 4, :], m.c[:, 4 * g:4 * g + 4, :], ACT.Square).then_inc(m.c_sq, 1)
    act.wait_ge(m.c_inv, BASE["c_inv"] + 1)
    A(m.rc[:], m.rc[:], ACT.Sqrt).then_inc(m.c_rt, 1)
    act.wait_ge(m.cn_done, BASE["cn_done"] + 1)
    A(m.cqh[:], m.c[:, 0:4, :], ACT.Copy).then_inc(m.cqh_done, 1)
    A(m.ckh[:], m.c[:, 4:8, :], ACT.Copy).then_inc(m.ckh_done, 1)
    for i in range(8):
        split(S_UQ, i + 2, 0)
    for i in range(8):
        act.wait_ge(m.kv_t, i + 1)
        A(m.wukT[:], ps[:, 0:2, :], ACT.Copy).then_inc(m.kv_tc, 1)
        if i < 6:
            split(S_UKV, i + 2, 0)

    act.wait_ge(m.o_c, 64)
    with act.Fori(0, 8) as t:
        act.wait_ge(m.pa_o, t + 1)
        act.wait_ge(m.kv_ev, 9)
        A(m.qs2[:], m.qn[:, ds(t * 2, 2), 0:SEQ], ACT.Copy)
        A(m.qp2[:], m.qp[:, ds(t, 1), 0:SEQ].rearrange("p k n -> p (k n)"), ACT.Copy).then_inc(m.pa_stage, 1)
        for u in range(2):
            act.wait_ge(m.pa_m, 2 * t + (u + 1))
            for g, (c0, c1) in enumerate(((0, 128), (128, 384))):
                w = m.mx2[:, 2 * u + g, :]
                last = A(m.sc2[:, u, c0:c1], m.sc2[:, u, c0:c1], ACT.Exp, bias=w[:, 1:2], scale=MLA_SCALE,
                         accum_out=w[:, 2:3])
            last.then_inc(m.pa_e, 1)
        for u in range(2):
            act.wait_ge(m.pa_t, 2 * t + (u + 1))
            A(m.PT2[:, u, :], ps[:, 2 + u, 0:384], ACT.Copy).then_inc(m.pa_tc, 1)
        act.wait_ge(m.pa_o, t + 2)
        A(m.Ah[:, ds(t * 2, 2), 0:SEQ], ps[:, 4:6, 0:SEQ], ACT.Copy).then_inc(m.pa_ah, 1)

    act.wait_ge(m.ckn_tr, BASE["ckn_tr"] + 1)
    act.wait_ge(m.patt_out, 8)
    A(m.ckn[0:NS, :], ps[0:NS, 3, :], ACT.Copy).then_inc(m.ckn_done, 1)

    def probs_t(t, i):
        act.wait_ge(m.sa_pt, 4 * t + (i + 1))
        A(m.PT[:].rearrange("p n r -> p (n r)"), ps[:, 3, :], ACT.Copy).then_inc(m.sa_ptc, 1)

    def values(t, i):
        act.wait_ge(m.spv_mm, 4 * t + (i + 1))
        act.wait_ge(m.sa_r, 4 * t + (i + 1))
        A(m.acc64[0:64, :], ps[0:64, 7, :], ACT.Copy, scale=m.mx8[0:64, i % 2, 6:7]).then_inc(m.sa_av, 1)

    with act.Fori(0, 2) as t:
        for i in range(4):
            for n in range(NPG):
                act.wait_ge(m.sa_t, 32 * t + (8 * i + n + 1))
                A(m.ckT[:, :, 128 * n:128 * n + 128], ps[:, 4 + n % 2, :].rearrange("p (k n) -> p k n", k=4),
                  ACT.Copy).then_inc(m.sa_ckc, 1)
            if i:
                probs_t(t, i - 1)
            act.wait_ge(m.sa_m, 4 * t + (i + 1))
            w = m.mx8[0:64, i % 2, :]
            A(m.sc8[0:64, 0:PAST], ps[0:64, 0:2, :].rearrange("p b n -> p (b n)"), ACT.Exp, bias=w[:, 2:3],
              scale=MLA_SCALE, accum_out=w[:, 3:4])
            A(m.sc8[0:64, PAST:], m.nsc[0:64, :], ACT.Exp, bias=w[:, 2:3], scale=MLA_SCALE, accum_out=w[:, 4:5]
              ).then_inc(m.sa_e, 1)
            if i:
                values(t, i - 1)
        probs_t(t, 3)
        values(t, 3)
    act.wait_ge(m.sa_acc, 9)
    A(m.ach[:], m.accT[:], ACT.Copy).then_inc(m.ach_done, 1)
    for i in range(6):
        split(S_OV, i, 0)
    act.wait_ge(m.slot_used, S_OV + 4)
    A(m.Ah[:, :, SEQ:NT], ps[:, 0, :].rearrange("p (h t) -> p h t", h=HM), ACT.Copy).then_inc(m.atth_done, 1)
    with act.Fori(0, 4) as t:
        k16(S_WO, t, lambda u: f_round(t * 2 + u, 4, C_FFN + 16, m.Bh))
    root(3)
    mlp(1, S_FFN1, S_PLE1, S_GATE1, m.Bh, m.Ah, 5)
    root(4)
    for g in range(4):
        for c, n in ((0, 128), (1, 128), (2, NS)):
            act.wait_ge(m.y_tr, 3 * g + c + 1)
            A(m.ytok[0:n, c, 512 * g:512 * g + 512], ps[0:n, 3 * (g % 2) + c, :], ACT.Copy).then_inc(m.y_done, 1)


def vector_program(dve, m):
    ps = m.ps
    V = m.nc.vector
    own = Own(dve, m.dve_own)
    TT, TS2, STT = V.tensor_tensor, V.tensor_scalar, V.scalar_tensor_tensor
    MUL, ADD, SUB, MAX = ALU.mult, ALU.add, ALU.subtract, ALU.max

    def f(x):
        return x.bitcast(F32)

    def over(ap, n):
        return ap.unsqueeze(1).to_broadcast([ap.shape[0], n, ap.shape[1]])

    def split(S, i, it):
        j = ring(S, i)
        dve.wait_ge(m.wh_done, it * 4 + (S + i + 1))
        parts = [pieces(S + i + 4 * it if isinstance(it, int) else -1, m.W[:, j, :], x[:, j % 2, :])
                 for x in (m.Wl, m.Wh)]
        for (w, low), (_, high) in zip(*parts):
            last = TT(low, w, f(high), SUB)
        last.then_inc(m.split_done, 1)

    def k16(S, it, evac, more=True):
        for u in range(2):
            if more or u == 0:
                split(S, 2 * u + 2, it)
                split(S, 2 * u + 3, it)
            dve.wait_ge(m.slot_used, it * 4 + (S + 2 * u + 2))
            b = 2 * ((S // 2 + u) % 2)
            evac(u, ps[:, b:b + 2, 0:NT])

    def f_low(n, F, gcol, Xh, Xl):
        dve.wait_ge(m.fh_done, n + (8 * F + 1))
        if gcol is None:
            last = TT(Xl[:, ds(n * 2, 2), :], m.hT[:, ds(n * 2, 2), :], f(Xh[:, ds(n * 2, 2), :]), SUB)
        else:
            for i in range(2):
                t = ds(n * 2 + i, 1)
                last = STT(Xl[:, t, :], m.hT[:, t, :], m.par[:, ds(n * 2 + (gcol + i), 1)], f(Xh[:, t, :]), MUL, SUB)
        last.then_inc(m.fl_done, 1)

    def add_to_h(n, x):
        TT(m.hT[:, ds(n * 2, 2), :], m.hT[:, ds(n * 2, 2), :], x, ADD).then_inc(m.h_ready, 1)

    def norm(n):
        dve.wait_ge(m.ss_mm, n + 1)
        own.after(TS2(m.rB[:], ps[:, 7, 0:NT], 1.0 / D_MODEL, EPS, MUL, ADD))
        V.reciprocal(m.rB[:], m.rB[:]).then_inc(m.r_inv, 1)

    dve.sem_inc(m.head_end, 2)
    dve.sem_inc(m.kv_ev, 1)
    dve.wait_ge(m.par_tr, BASE["par_tr"] + 1)
    V.tensor_copy(m.par[:, 0:NPAR], ps[:, 4, 0:NPAR]).then_inc(m.par_done, 1)
    dve.wait_ge(m.par_done, BASE["par_done"] + 1)
    lam, nl = m.par[:, C_LAM:C_LAM + 8], m.lsp[:, 0, 0:8]
    own.after(TS2(nl, lam, -1.0, None, MUL))
    TT(m.lsp[:, 0, 8:16], nl, lam, MAX).then_inc(m.lam_abs, 1)
    dve.wait_ge(m.lam_ln, BASE["lam_ln"] + 1)
    own.after(STT(m.lsp[:, 2, 0:8], nl, 0.0, m.lsp[:, 1, 8:16], MAX, ADD))
    own.after(TS2(m.lsp[:, 2, 8:16], m.lsp[:, 2, 0:8], 8.0, None, MUL))
    for n in range(8):
        dve.wait_ge(m.x_tr, n + 1)
        b = 2 * (n % 2)
        V.tensor_copy(m.hT[:, 2 * n:2 * n + 2, :], ps[:, b:b + 2, 0:NT]).then_inc(m.h_ready, 1)
        f_low(n, 0, C_MIX, m.Ah, m.Al)
    split(0, 0, 0)
    split(0, 1, 0)
    dve.wait_ge(m.hist_tr, BASE["hist_tr"] + 1)
    V.tensor_copy(m.hist[:, 0:16, :].rearrange("p k n -> p (k n)"), ps[:, 5, 0:384])
    V.tensor_copy(m.hist[:, 16:32, :].rearrange("p k n -> p (k n)"), ps[:, 6, 0:384]).then_inc(m.hist_done, 1)
    norm(0)
    dve.wait_ge(m.r_ready, 1)

    r_p, r_s = m.rB[:, 0:SEQ], m.rB[:, SEQ:NT]

    def conv(n, tile, col, taps):
        def evac(u, x):
            if not isinstance(n, int):
                dve.wait_ge(m.pre_saved, n + (u - 1))
            TT(m.pre[:, u, :, 3:3 + SEQ], x[:, :, 0:SEQ], over(r_p, 2), MUL)
            rows = m.pre[:, u, :, PADS:PRE].rearrange("p i (b s) -> p i b s", s=7)
            for i in range(2):
                last = TT(rows[:, i, :, 3:7], x[:, i, SEQ:NT].rearrange("p (b t) -> p b t", t=TS),
                          r_s.rearrange("p (b t) -> p b t", t=TS), MUL)
            last.then_inc(m.pre_ready, 1)
            dve.wait_ge(m.pre_ready, n + (u + 1))
            dve.wait_ge(m.hist_in, n + (u + 1))
            if not isinstance(n, int):
                dve.wait_ge(m.conv_act, n + (u - 1))
            for w in range(4):
                for i in range(2):
                    g = m.par[:, ds(tile + (2 * u + i + col + taps * w), 1)]
                    x_w, o = m.pre[:, u, i, w:w + PRE - 3], m.acc[:, u, i, 0:PRE - 3]
                    last = STT(o, x_w, g, o, MUL, ADD) if w else TS2(o, x_w, g, None, MUL)
                if w < 3:
                    own.after(last)
            last.then_inc(m.conv_done, 1)
        return evac
    k16(S_QKV, 0, conv(0, 0, C_CONV, 24))
    own.loop(6, 6, lambda t: k16(S_QKV, t, conv(t * 2, t * 4, C_CONV, 24)), first=1)

    def scaled(dst, sem):
        def turn(t):
            def evac(u, x):
                TT(dst[:, ds(t * 4 + 2 * u, 2), :], x, over(m.rB[:], 2), MUL).then_inc(sem, 1)
            return evac
        return turn
    zt, lyt, ct = scaled(m.z, m.z_raw), scaled(m.ly, m.ly_raw), scaled(m.c, m.c_raw)
    for t in range(2):
        k16(S_Z, t, zt(t))
    split(S_BA, 2, 0)
    split(S_BA, 3, 0)
    dve.wait_ge(m.slot_used, S_BA + 2)
    b = 2 * (S_BA // 2 % 2)
    TT(m.betaR[0:8, :], ps[0:8, b, 0:NT], m.rB[0:8, :], MUL)
    TT(m.gR[0:8, :], ps[32:40, b, 0:NT], m.rB[32:40, :], MUL).then_inc(m.ba_done, 1)
    own.loop(2, 6, lambda t: k16(S_LX, t, conv(t * 2 + 12, t * 4, C_LCONV, 8)))
    with dve.Fori(0, 2) as t:
        k16(S_LY, t, lyt(t))

    for g in range(2):
        dve.wait_ge(m.cs_tr, BASE["cs_tr"] + g + 1)
        V.tensor_copy(m.csrow[0:27, 2048 * g:2048 * g + 2048], ps[0:27, 4:8, :].rearrange("p b n -> p (b n)")
                      ).then_inc(m.csr_done, 1)

    dve.wait_ge(m.gate_act, 8)
    dve.wait_ge(m.conv_act, 16)
    sp8 = m.lsp[:, 2, 8:16].unsqueeze(2).to_broadcast([128, 8, NT])
    TT(m.lm[:, 0], m.lm[:, 0], sp8, MUL).then_inc(m.lm_done, 1)
    own.after(TT(m.lm[:, 1], m.lm[:, 1], m.xb[:], MUL))
    dve.wait_ge(m.lat_done, BASE["lat_done"] + 1)
    own.after(TT(m.lm[:, 0], m.la[:], m.la[:], MUL))
    STT(m.lt[:], m.lm[:, 0], 1.0, m.lt[:], ADD, MUL).then_inc(m.lt_done, 1)
    dve.wait_ge(m.lroot_done, BASE["lroot_done"] + 1)
    own.after(TT(m.lt[:], m.lt[:], m.lm[:, 1], MUL))
    hs = m.lm[:, 0]
    for k in range(8):
        V.tensor_tensor_scan(hs[:, k, 0:SEQ], m.la[:, k, 0:SEQ], m.lt[:, k, 0:SEQ], 0.0, MUL, ADD)
    row = lambda x, t: x[:, :, SEQ:NT].rearrange("p k (b t) -> p k b t", t=TS)[:, :, :, t]
    before = m.par[:, C_H0:C_H0 + 64].rearrange("p (b k) -> p k b", k=8)
    for t in range(TS):
        own.after(TT(row(hs, t), row(m.la, t), before, MUL))
        own.after(TT(row(hs, t), row(hs, t), row(m.lt, t), ADD))
        before = row(hs, t)
    V.tensor_copy(m.lo[:, 0:8], hs[:, :, SEQ - 1]).then_inc(m.lo_done, 1)
    V.tensor_copy(m.lo[:, 8:72].rearrange("p (b k) -> p k b", k=8), row(hs, TS - 1)).then_inc(m.lo_done, 1)
    dve.wait_ge(m.ly_act, 4)
    TT(m.la[:], hs, m.ly[:], MUL).then_inc(m.ob_done, 1)
    dve.wait_ge(m.lo_tr, BASE["lo_tr"] + 1)
    V.tensor_copy(m.lrow[0:72, :], ps[0:72, 4, 0:128]).then_inc(m.lrow_done, 1)
    dve.wait_ge(m.mixh_done, 1)
    TT(m.Bl[:, 8:16, :], m.la[:], f(m.Bh[:, 8:16, :]), SUB).then_inc(m.mixl_done, 1)

    dve.wait_ge(m.l2_sum, BASE["l2_sum"] + 1)
    own.after(TS2(m.rs16[0:16, :], ps[0:16, 5, 0:NT], EPS, None, ADD))
    V.reciprocal(m.rs16[0:16, :], m.rs16[0:16, :]).then_inc(m.l2_inv, 1)
    for g in range(2):
        dve.wait_ge(m.l2_mm, BASE["l2_mm"] + g + 1)
        x = m.conv[:, 8 * g:8 * g + 8, :]
        TT(x, x, ps[:, :, 0:NT], MUL).then_inc(m.l2_done, 1)
    be, g_, gc, e = m.betaR[0:8, :], m.gR[0:8, :], m.gcR[0:8, :], m.eR[0:8, :]
    dve.wait_ge(m.beta_e, BASE["beta_e"] + 1)
    own.after(TS2(be, be, 1.0, None, ADD))
    V.reciprocal(be, be).then_inc(m.beta_done, 1)
    dve.wait_ge(m.l_ab, 32)
    dve.wait_ge(m.ba_done, BASE["ba_done"] + 1)
    own.after(TS2(g_, g_, m.alog[0:8, 1:2], None, ADD))
    STT(e, g_, -1.0, g_, MUL, MAX).then_inc(m.a_abs, 1)
    dve.wait_ge(m.a_ln, BASE["a_ln"] + 1)
    own.after(STT(g_, g_, 0.0, e, MAX, ADD))
    own.after(TS2(g_, g_, m.alog[0:8, 2:3], -1.0, MUL, MUL))
    dve.wait_ge(m.l_c0, 16)
    V.tensor_tensor_scan(gc, m.cst0[0:8, NC0 - NT:NC0], g_, 0.0, MUL, ADD).then_inc(m.gc_done, 1)
    dve.wait_ge(m.gc_done, BASE["gc_done"] + 1)
    for c0, c1, n in ((0, SEQ, CHUNK), (SEQ, NT, TS)):
        x = gc[:, c0:c1].rearrange("p (c n) -> p c n", n=n)
        end = x[:, :, n - 1:n].to_broadcast([8, (c1 - c0) // n, n])
        last = TT(e[:, c0:c1].rearrange("p (c n) -> p c n", n=n), end, x, SUB)
    last.then_inc(m.dl_done, 1)
    dve.wait_ge(m.eg_done, BASE["eg_done"] + 1)
    dve.wait_ge(m.beta_done, BASE["beta_done"] + 1)
    STT(g_, g_, -1.0, be, MUL, MUL).then_inc(m.nbg_done, 1)
    own.after(V.memset(m.scal[:], 0.0))
    dve.wait_ge(m.scal_tr, BASE["scal_tr"] + 1)
    sc = m.scal[:].rearrange("p h (q c) -> p q c h", q=4)
    pv = ps[:, 0, 0:96].rearrange("p (q c h) -> p q c h", q=4, c=3)
    for c, n in ((0, 128), (1, 128), (2, NS)):
        last = V.tensor_copy(sc[0:n, :, c, :], pv[0:n, :, c, :])
    last.then_inc(m.scal_done, 1)
    dve.wait_ge(m.scal_done, BASE["scal_done"] + 1)

    lev = m.cst0[:, 0:LEVELS * 128].rearrange("p (n x) -> p n x", n=LEVELS)
    o0 = LEVELS * 128
    up, up_s = m.cst0[:, o0:o0 + 128], m.cst0[0:NS, o0 + 128:o0 + 128 + NS]
    belongs = m.cst0[0:NS, o0 + 128 + NS:o0 + 128 + NS + BS]

    def heads(t):
        def each():
            return [(x, 4 * x, g, [[g.sc1[:, 3 * q + c:3 * q + c + 1] for c in range(3)] for q in range(4)])
                    for x, g in enumerate(m.g)]
        CH = ((0, 128), (1, 128), (2, NS))
        for x, b, g, _ in each():
            dve.wait_ge(m.head_end, 2 * t + (x + 1))
            V.tensor_copy(g.sc1[:], m.scal[:, ds(2 * t + x, 1), :].rearrange("p h q -> p (h q)"))
            TS2(g.rows[0:8, :, :], m.bg[0:8, :, :], m.ident[0:8, ds(2 * t + x, 1)], None, MUL).then_inc(m.g_row, 1)
        for x, b, g, (beta, nbg, kde, gcs) in each():
            dve.wait_ge(m.g_bb, 2 * t + (x + 1))
            for c in range(2):
                STT(g.dec[:, 128 * c:128 * c + 128], ps[:, b + 2, 128 * c:128 * c + 128], gcs[c], up, SUB, ALU.min)
            STT(g.dec[0:NS, SEQ:NT], ps[0:NS, b + 2, SEQ:NT], gcs[2][0:NS], up_s, SUB, ALU.min)
            V.tensor_copy(g.BB[:], ps[:, b + 3, 0:NT]).then_inc(m.g_diff, 1)
            for c, n in CH:
                TS2(g.vb[0:n, c, :], ps[0:n, b + 1, 128 * c:128 * c + 128], beta[c][0:n], None, MUL)
        for x, b, g, _ in each():
            dve.wait_ge(m.g_eb, 2 * t + (x + 1))
            own.after(TT(g.qe[:], g.qkv[:, 0, :], g.Eb[:], MUL))
            for a, y in ((0, g.qkv[:, 1, SEQ:NT]), (1, g.qe[:, SEQ:NT])):
                V.tensor_copy(g.kq[:, :, a, :], y.rearrange("p (b t) -> p b t", t=TS))
        for x, b, g, _ in each():
            dve.wait_ge(m.g_gram, 2 * t + (x + 1))
            dve.wait_ge(m.g_dec, 2 * t + (x + 1))
            A0, ats = g.AQ[:, 0, 0:SEQ], g.AQ[0:NS, 0, SEQ:NT]
            TT(A0, ps[:, b + 2, 0:SEQ], g.dec[:, 0:SEQ], MUL)
            own.after(TT(ats, ps[0:NS, b + 2, SEQ:NT], g.dec[0:NS, SEQ:NT], MUL))
            TT(A0, A0, g.BB[:, 0:SEQ], MUL)
            own.after(TT(ats, ats, g.BB[0:NS, SEQ:NT], MUL))
            TT(g.Bt[:], A0.rearrange("p (c n) -> p c n", c=2), over(lev[:, 0], 2), MUL)
            TT(g.Bts[0:NS, :], ats, lev[0:NS, 0, 0:NS], MUL).then_inc(m.g_bt1, 1)
            TT(g.AQ[:, 1, 0:SEQ], ps[:, b + 3, 0:SEQ], g.dec[:, 0:SEQ], MUL)
            TT(g.AQ[0:NS, 1, SEQ:NT], ps[0:NS, b + 3, SEQ:NT], g.dec[0:NS, SEQ:NT], MUL)
            dve.wait_ge(m.g_bt1, 2 * t + (x + 1))
            TT(g.TT[:, 1], over(m.ident[:], 2), g.Bt[:], SUB)
            TT(g.Ts[0:NS, 1, :], m.ident[0:NS, 0:NS], g.Bts[0:NS, :], SUB)
        for x, b, g, _ in each():
            dve.wait_ge(m.g_t1, 2 * t + (x + 1))
            TT(g.Ts[0:NS, 0, :], m.ident[0:NS, 0:NS], ps[0:NS, b + 1, 0:NS], SUB)
            TT(g.TT[:, 0], over(m.ident[:], 2), ps[:, b, 0:256].rearrange("p (c n) -> p c n", c=2), SUB
               ).then_inc(m.g_lt, 1)
        for n in range(1, LEVELS):
            for x, b, g, _ in each():
                dve.wait_ge(m.g_q, 12 * t + (2 * n + x - 1))
                if n == 1:
                    TT(g.Qss[0:NS, :], ps[0:NS, b + 1, 0:NS], lev[0:NS, 1, 0:NS], MUL)
                TT(g.Qs[:], ps[:, b, 0:256].rearrange("p (c n) -> p c n", c=2), over(lev[:, n], 2), MUL
                   ).then_inc(m.g_qc, 1)
            for x, b, g, _ in each():
                dve.wait_ge(m.g_tb, 12 * t + (2 * n + x - 1))
                if n == 1:
                    fs = g.Ts[0:NS].rearrange("p a n -> p (a n)")
                    TT(fs, fs, ps[0:NS, b + 3, 0:2 * NS], SUB)
                flat = g.TT[:].rearrange("p a c n -> p (a c n)")
                TT(flat, flat, ps[:, b + 2, :], SUB).then_inc(m.g_lt if n < LEVELS - 1 else m.g_inv, 1)
        for x, b, g, _ in each():
            dve.wait_ge(m.g_xs, 2 * t + (x + 1))
            ends = g.Eb[:, SEQ:NT].rearrange("p (b t) -> p b t", t=TS)[:, :, TS - 1:TS].to_broadcast([128, BS, 128])
            TT(g.S8[:], g.S8[:], ends, MUL)
        for x, b, g, (beta, nbg, kde, gcs) in each():
            dve.wait_ge(m.g_xtr, 2 * t + (x + 1))
            STT(g.Rs[0:NS, :], ps[0:NS, b + 1, 384:512], nbg[2][0:NS], g.vb[0:NS, 2, :], MUL, ADD)
            dve.wait_ge(m.g_x1, 2 * t + (x + 1))
            STT(g.R1[:], ps[:, b + 2, 0:128], nbg[1], g.vb[:, 1, :], MUL, ADD).then_inc(m.g_rs, 1)
        for x, b, g, _ in each():
            dve.wait_ge(m.g_s2, 2 * t + (x + 1))
            STT(g.S2[:], g.S1[:], g.Eb[:, SEQ - 1:SEQ], ps[:, b, 256:384], MUL, ADD).then_inc(m.s2_done, 1)
            dve.wait_ge(m.g_vns, 2 * t + (x + 1))
            TT(g.Vm[0:NS], over(g.vn[0:NS, 2, :], BS), belongs.unsqueeze(2).to_broadcast([NS, BS, 128]), MUL
               ).then_inc(m.g_vm, 1)
        for x, b, g, _ in each():
            dve.wait_ge(m.g_o, 2 * t + (x + 1))
            o = m.conv[:, ds(2 * t + x, 1), :].rearrange("p h n -> p (h n)")
            V.tensor_copy(o[:, 0:SEQ], ps[:, b + 1, 0:SEQ])
            TT(o[:, SEQ:NT], ps[:, b + 1, SEQ:NT], g.oS[:], ADD)
            dve.wait_ge(m.g_ds, 2 * t + (x + 1))
            s8 = g.S8[:].rearrange("p b v -> p (b v)")
            TT(s8, s8, ps[:, b + 2:b + 4, :].rearrange("p b n -> p (b n)"), ADD).then_inc(m.s8_done, 1)
            dve.wait_ge(m.s8_done, 2 * t + (x + 1))
            V.tensor_copy(g.sc1[:, 0:1], m.scal[:, 0, 0:1]).then_inc(m.head_end, 1)
    own.loop(HG // 2, 6, heads)

    dve.wait_ge(m.on_sum, BASE["on_sum"] + 1)
    own.after(TS2(m.rs16[0:8, :], ps[0:8, 5, 0:NT], 1.0 / DK, EPS, MUL, ADD))
    V.reciprocal(m.rs16[0:8, :], m.rs16[0:8, :]).then_inc(m.on_inv, 1)
    dve.wait_ge(m.on_mm, BASE["on_mm"] + 1)
    dve.wait_ge(m.z_act, 4)
    o = m.conv[:, 0:8, :]
    own.after(TT(o, o, ps[:, :, 0:NT], MUL))
    STT(o, o, m.par[:, C_GN:C_GN + 1], m.z[:], MUL, MUL).then_inc(m.og_done, 1)
    dve.wait_ge(m.mixh_done, 2)
    TT(m.Bl[:, 0:8, :], o, f(m.Bh[:, 0:8, :]), SUB).then_inc(m.mixl_done, 1)

    def residual(F, gcol, Xh, Xl):
        def turn(t):
            def evac(u, x):
                add_to_h(t * 2 + u, x)
                f_low(t * 2 + u, F, gcol, Xh, Xl)
            return evac
        return turn
    res = residual(1, C_FFN, m.Ah, m.Al)
    with dve.Fori(0, 4) as t:
        k16(S_OUT, t, res(t))
    norm(1)

    def mlp(layer, S, S_P, S_G, X, Y, F):
        dve.wait_ge(m.r_ready, 2 + 2 * layer)

        def up(c, t):
            def evac(u, x):
                n = t * 2 + u
                STT(m.u[:], x, 0.0, over(m.rB[:], 2), MAX, MUL).then_inc(m.u_done, 1)
                dve.wait_ge(m.fuh_done, c * 8 + n + (32 * layer + 1))
                TT(Y[1][:, ds(n * 2, 2), :], m.usq[:], f(Y[0][:, ds(n * 2, 2), :]), SUB).then_inc(m.fu_done, 1)
            return evac

        def down(t):
            def evac(u, x):
                hh = m.hT[:, ds(t * 4 + 2 * u, 2), :]
                TT(hh, hh, x, ADD)
            return evac
        with dve.Fori(0, 3) as c:
            with dve.Fori(0, 4) as t:
                k16(S, c * 8 + t, up(c, t))
            with dve.Fori(0, 4) as t:
                k16(S, c * 8 + t + 4, down(t))
        with dve.Fori(0, 4) as t:
            k16(S, t + 24, up(3, t))
        res = residual(F, None, *X)
        with dve.Fori(0, 4) as t:
            k16(S, t + 28, res(t))
        dve.wait_ge(m.p_tr, layer + 1)
        V.tensor_copy(m.usq[:], ps[:, 4:6, 0:NT]).then_inc(m.pt_done, 1)
        dve.wait_ge(m.ph_done, layer + 1)
        TT(m.pTl[:], m.usq[:], f(m.pTh[:]), SUB).then_inc(m.pl_done, 1)
        for i in range(2):
            for n in range(4):
                if n < 3:
                    dve.wait_ge(m.ple_mm, 6 * layer + 3 * i + n + 1)
                else:
                    dve.wait_ge(m.slot_used, S_P + i + 1)
                b, q = 2 * ((S_P // 2 + n) % 2), 4 * i + n
                V.tensor_copy(m.ple[:, 2 * q:2 * q + 2, :], ps[:, b:b + 2, 0:NT]).then_inc(m.ple_ev, 1)
            split(S_P, i + 2, 0)
        dve.wait_ge(m.ple_ev, 8 * layer + 8)

        def gate(t):
            def evac(u, x):
                n = t * 2 + u
                dve.wait_ge(m.h_ready, n + 8 * (F + 1))
                V.tensor_copy(m.gt[:], x).then_inc(m.gt_raw, 1)
                dve.wait_ge(m.gt_act, n + (8 * layer + 1))
                own.after(TT(m.gt[:], m.gt[:], m.ple[:, ds(n * 2, 2), :], MUL))
                add_to_h(n, m.gt[:])
                if layer == 0:
                    f_low(n, F + 1, C_MIX + 16, *Y)
            return evac
        if layer:
            own.loop(3, 2, lambda t: k16(S_G, t, gate(t)))
            k16(S_G, 3, gate(3), more=False)
        else:
            own.loop(4, 2, lambda t: k16(S_G, t, gate(t)))

    mlp(0, S_FFN0, S_PLE0, S_GATE0, (m.Ah, m.Al), (m.Bh, m.Bl), 2)
    norm(2)
    dve.wait_ge(m.r_ready, 3)

    for t in range(2):
        k16(S_INC, t, ct(t))
    split(S_KPE, 2, 0)
    split(S_KPE, 3, 0)
    dve.wait_ge(m.slot_used, S_KPE + 2)
    TT(m.kpR[:], ps[:, 2 * (S_KPE // 2 % 2), 0:NT], m.rB[:], MUL).then_inc(m.kpr_done, 1)
    for g in range(2):
        dve.wait_ge(m.c_mm, BASE["c_mm"] + g + 1)
        last = TS2(m.rc[:, g, :], ps[:, 4 + g, 0:NT], 1.0 / QLORA, EPS, MUL, ADD)
    own.after(last)
    V.reciprocal(m.rc[:], m.rc[:]).then_inc(m.c_inv, 1)
    dve.wait_ge(m.c_rt, BASE["c_rt"] + 1)
    for g in range(2):
        x = m.c[:, 4 * g:4 * g + 4, :]
        last = TT(x, x, over(m.rc[:, g, :], 4), MUL)
    own.after(last)
    TT(m.c[:], m.c[:], m.par[:, C_QN:C_QN + 8].unsqueeze(2).to_broadcast([128, 8, NT]), MUL).then_inc(m.cn_done, 1)
    cm3, new = m.cst1[:, 0:384], m.cst1[:, 384:384 + 2 * NS - TS]
    cos, sin = m.cst1[:, NC1 - 128 - 2 * NT:NC1 - 128 - NT], m.cst1[:, NC1 - 128 - NT:NC1 - 128]
    dve.wait_ge(m.cqh_done, BASE["cqh_done"] + 1)
    TT(m.cql[:], m.c[:, 0:4, :], f(m.cqh[:]), SUB).then_inc(m.cql_done, 1)
    dve.wait_ge(m.l_c1, 16)
    dve.wait_ge(m.kpr_done, BASE["kpr_done"] + 1)
    TT(m.kpe[:], m.kpR[:], cos, MUL)
    dve.wait_ge(m.kp_rot, BASE["kp_rot"] + 1)
    own.after(TT(m.rtmp[:, 0, :], ps[:, 6, 0:NT], sin, MUL))
    TT(m.kpe[:], m.kpe[:], m.rtmp[:, 0, :], ADD).then_inc(m.kpe_done, 1)
    dve.wait_ge(m.ckh_done, BASE["ckh_done"] + 1)
    TT(m.ckl[:], m.c[:, 4:8, :], f(m.ckh[:]), SUB).then_inc(m.ckl_done, 1)
    for c, n in ((0, 128), (1, 128), (2, NS)):
        dve.wait_ge(m.ctok_tr, BASE["ctok_tr"] + c + 1)
        V.tensor_copy(m.ctok[0:n, c, 0:512], ps[0:n, c, :]).then_inc(m.ctok_done, 1)
    dve.wait_ge(m.ctok_tr, BASE["ctok_tr"] + 4)
    for c, n in ((0, 128), (1, 128), (2, NS)):
        V.tensor_copy(m.ctok[0:n, c, 512:576], ps[0:n, 7, 64 * c:64 * c + 64]).then_inc(m.ctok_done, 1)

    for i in range(8):
        dve.wait_ge(m.slot_used, S_UQ + i + 1)
        b = 4 * (i % 2)
        V.tensor_copy(m.qn[:, 2 * i:2 * i + 2, :], ps[:, b:b + 2, 0:NT])
        V.tensor_copy(m.qp[:, i, :], ps[:, b + 2, 0:NT]).then_inc(m.uq_ev, 1)
        split(S_UQ, i + 2, 0)
    dve.wait_ge(m.qp_rot, BASE["qp_rot"] + 1)
    TT(m.rtmp[:], ps[:, :, 0:NT], over(sin, 8), MUL)
    own.after(TT(m.qp[:], m.qp[:], over(cos, 8), MUL))
    TT(m.qp[:], m.qp[:], m.rtmp[:], ADD).then_inc(m.qp_done, 1)

    for i in range(8):
        dve.wait_ge(m.kv_k, i + 1)
        V.tensor_copy(m.kno[:, 2 * i:2 * i + 2, :], ps[:, 2, :].rearrange("p (h n) -> p h n", h=2))
        dve.wait_ge(m.slot_used, S_UKV + i + 1)
        V.tensor_copy(m.vtok[:, :, 256 * i:256 * i + 256], ps[:, 3, :].rearrange("p (c n) -> p c n", c=2))
        dve.wait_ge(m.kv_q, i + 1)
        V.tensor_copy(m.qlat[:, :, 2 * i:2 * i + 2, :],
                      ps[:, 4, 0:256].rearrange("p (h k n) -> p k h n", h=2, k=4)).then_inc(m.kv_ev, 1)
        if i < 6:
            split(S_UKV, i + 2, 0)

    def heads(t):
        for u in range(2):
            dve.wait_ge(m.pa_s, 2 * t + (u + 1))
            own.after(TT(m.sc2[:, u, :], ps[:, u, 0:384], cm3, ADD))
            V.reduce_max(m.mx2[:, 2 * u, 0:1], m.sc2[:, u, 0:128], AX.X)
            own.after(V.reduce_max(m.mx2[:, 2 * u + 1, 0:1], m.sc2[:, u, 128:384], AX.X))
            TS2(m.mx2[:, 2 * u:2 * u + 2, 1:2], m.mx2[:, 2 * u:2 * u + 2, 0:1], -MLA_SCALE, None, MUL
                ).then_inc(m.pa_m, 1)
        for u in range(2):
            dve.wait_ge(m.pa_e, 2 * t + (u + 1))
            own.after(V.reciprocal(m.mx2[:, 2 * u:2 * u + 2, 3:4], m.mx2[:, 2 * u:2 * u + 2, 2:3]))
            TS2(m.sc2[:, u, 0:128], m.sc2[:, u, 0:128], m.mx2[:, 2 * u, 3:4], None, MUL)
            TS2(m.sc2[:, u, 128:384], m.sc2[:, u, 128:384], m.mx2[:, 2 * u + 1, 3:4], None, MUL).then_inc(m.pa_p, 1)
        dve.wait_ge(m.pa_ah, t + 1)
        TT(m.Al[:, ds(t * 2, 2), 0:SEQ], ps[:, 4:6, 0:SEQ], f(m.Ah[:, ds(t * 2, 2), 0:SEQ]), SUB
           ).then_inc(m.patt_out, 1)
    own.loop(8, 6, heads)

    for g in range(2):
        x = m.qp[64 * g:64 * g + 64, :, SEQ:NT].rearrange("p k (b t) -> p b k t", t=TS)
        out = m.qrs[0:64].rearrange("p b (k g) t -> p b k g t", g=2)[:, :, :, g, :]
        last = V.tensor_copy(out, x)
    own.after(last)

    dve.sem_inc(m.sa_acc, 1)

    def probs_n(t, i):
        dve.wait_ge(m.sa_pt, 4 * t + (i + 1))
        V.tensor_copy(m.PTn[0:NS, :], ps[0:NS, 6, 0:64]).then_inc(m.sa_nt, 1)

    def values(t, i):
        dve.wait_ge(m.sa_at, 4 * t + (i + 1))
        V.tensor_copy(m.accT[:, :, :, ds(t * 16 + 4 * i, 4)],
                      ps[:, 6, 128:384].rearrange("p (k h t) -> p k h t", k=4, h=HM)).then_inc(m.sa_acc, 1)

    def samples(t):
        for i in range(4):
            V.tensor_copy(m.qls[:, i % 2], m.qlat[:, :, :, ds(t * 16 + 4 * i, 4)])
            V.tensor_copy(m.qrs2[0:64, i % 2], m.qrs[0:64, ds(t * 4 + i, 1)].rearrange("p b h t -> p (b h) t")
                          ).then_inc(m.sa_stage, 1)
            for g in range(2):
                dve.wait_ge(m.sa_t, 32 * t + (8 * i + 4 * g + 4))
                V.tensor_copy(m.kpT[0:64, 512 * g:512 * g + 512], ps[0:64, 6, :]).then_inc(m.sa_kpc, 1)
            if i:
                probs_n(t, i - 1)
            dve.wait_ge(m.sa_s, 4 * t + (i + 1))
            w = m.mx8[0:64, i % 2, :]
            V.reduce_max(w[:, 0:1], ps[0:64, 0:2, :].rearrange("p b n -> p (b n)"), AX.X)
            own.after(TT(m.nsc[0:64, :], ps[0:64, 2, 0:NS], new[0:64, ds(t * -16 + (NS - TS - 4 * i), NS)], ADD))
            own.after(V.reduce_max(w[:, 1:2], m.nsc[0:64, :], AX.X))
            own.after(TT(w[:, 0:1], w[:, 0:1], w[:, 1:2], MAX))
            TS2(w[:, 2:3], w[:, 0:1], -MLA_SCALE, None, MUL).then_inc(m.sa_m, 1)
            dve.wait_ge(m.sa_e, 4 * t + (i + 1))
            own.after(TT(w[:, 5:6], w[:, 3:4], w[:, 4:5], ADD))
            V.reciprocal(w[:, 6:7], w[:, 5:6]).then_inc(m.sa_r, 1)
            if i:
                values(t, i - 1)
        probs_n(t, 3)
        values(t, 3)
    own.loop(2, 16, samples)
    dve.wait_ge(m.ach_done, BASE["ach_done"] + 1)
    TT(m.acl[:], m.accT[:], f(m.ach[:]), SUB).then_inc(m.acl_done, 1)
    for i in range(6):
        split(S_OV, i, 0)
    dve.wait_ge(m.atth_done, BASE["atth_done"] + 1)
    TT(m.Al[:, :, SEQ:NT], ps[:, 0, :].rearrange("p (h t) -> p h t", h=HM), f(m.Ah[:, :, SEQ:NT]), SUB
       ).then_inc(m.attl_done, 1)

    res = residual(4, C_FFN + 16, m.Bh, m.Bl)
    with dve.Fori(0, 4) as t:
        k16(S_WO, t, res(t))
    norm(3)
    mlp(1, S_FFN1, S_PLE1, S_GATE1, (m.Bh, m.Bl), (m.Ah, m.Al), 5)
    norm(4)
    dve.wait_ge(m.r_ready, 5)
    for k in range(KT):
        STT(m.hT[:, k, :], m.hT[:, k, :], m.par[:, C_FIN + k:C_FIN + k + 1], m.rB[:], MUL, MUL
            ).then_inc(m.yn_done, 1)


def gpsimd_program(g, m):
    G = m.nc.gpsimd
    own = Own(g, m.pool_own)
    MUL, ADD = ALU.mult, ALU.add

    def squares(n, F):
        if n:
            g.wait_ge(m.ss_mm, n)
        own.after(G.memset(m.ssacc[:], 0.0))

        def tiles(t):
            g.wait_ge(m.h_ready, t + (8 * F + 1))
            x = m.hT[:, ds(t * 2, 2), :]
            own.after(G.tensor_tensor(m.sqt[:], x, x, MUL))
            G.tensor_tensor(m.ssacc[:], m.ssacc[:], m.sqt[:], ADD).then_inc(m.ss_done, 1)
            g.wait_ge(m.ss_done, t + (8 * n + 1))
        own.loop(8, 1, tiles)

    G.memset(m.ones[:], 1.0).then_inc(m.ones_set, 1)
    G.memset(m.pre[:, :, :, 0:3], 0.0)
    squares(0, 0)
    g.wait_ge(m.hist_done, BASE["hist_done"] + 1)

    def conv(n, tile):
        for u in range(2):
            if not isinstance(n, int):
                g.wait_ge(m.conv_done, n + (u - 1))
            rows = m.pre[:, u, :, PADS:PRE].rearrange("p i (b s) -> p i b s", s=7)
            x = m.hist[:, ds(tile + 2 * u, 2), :].rearrange("p i (b w) -> p i b w", w=3)
            G.tensor_copy(rows[:, :, :, 0:3], x).then_inc(m.hist_in, 1)
            g.wait_ge(m.pre_ready, n + (u + 1))
            out = m.cs[:, ds(tile + 2 * u, 2), :]
            G.tensor_copy(out[:, :, 0:3], m.pre[:, u, :, SEQ:SEQ + 3])
            G.tensor_copy(out[:, :, 3:27].rearrange("p i (b w) -> p i b w", w=3), rows[:, :, :, 4:7]
                          ).then_inc(m.pre_saved, 1)
    conv(0, 0)
    with g.Fori(1, 6) as t:
        conv(t * 2, t * 4)
    with g.Fori(0, 2) as t:
        conv(t * 2 + 12, t * 4 + 24)

    squares(1, 1)
    squares(2, 3)
    g.wait_ge(m.pa_o, 1)

    def stage(t):
        g.wait_ge(m.kv_ev, 9)
        g.wait_ge(m.pa_o, t + 1)
        G.tensor_copy(m.vs2[:], m.vtok[:, :, ds(t * 256, 256)]).then_inc(m.pa_stage, 1)
    with g.Fori(0, 8) as t:
        stage(t)
    g.wait_ge(m.acl_done, BASE["acl_done"] + 1)
    squares(3, 4)
    squares(4, 6)


def trunk(nc, a):
    with ExitStack() as ctx:
        m = memory(nc, ctx)
        block = ctx.enter_context(nc.Block())

        @block.sync
        def _(sp):
            sync_program(sp, m, a)

        @block.scalar
        def _(act):
            scalar_program(act, m)

        @block.vector
        def _(dve):
            vector_program(dve, m)

        @block.tensor
        def _(pe):
            tensor_program(pe, m)

        @block.gpsimd
        def _(g):
            gpsimd_program(g, m)


_OUTS = [("y_prompt", (1, SEQ, D_MODEL)), ("y_sample", (BS, TS, D_MODEL)), ("gdn_p", (1, 1, HG, DK, DK)),
         ("gdn_s", (1, BS, HG, DK, DK)), ("gdn_conv_p", (1, 1, 3, QKV)), ("gdn_conv_s", (1, BS, 3, QKV)),
         ("lru_p", (1, 1, LRU)), ("lru_s", (1, BS, LRU)), ("lru_conv_p", (1, 1, 3, LRU)),
         ("lru_conv_s", (1, BS, 3, LRU)), ("ckv_p", (1, 1, SEQ, KVLORA)), ("ckv_s", (1, BS, TS, KVLORA)),
         ("kpe_p", (1, 1, SEQ, ROPE)), ("kpe_s", (1, BS, TS, ROPE))]


def kernel(**inputs):
    import concourse.bacc as bacc
    from concourse.bass_utils import run_bass_kernel_spmd

    nc = bacc.Bacc("TRN2", target_bir_lowering=False, num_devices=1, dynamic_dma_scratch_size=1024)
    ident, c0, c1 = constants()
    arrays, aps = {}, {}
    for name, x in [*inputs.items(), ("ident", ident), ("cst0", c0), ("cst1", c1)]:
        x = np.ascontiguousarray(x)
        arrays[f"in_{name}"] = x
        aps[name] = nc.dram_tensor(f"in_{name}", x.shape, mybir.dt.from_np(x.dtype), kind="ExternalInput").ap()
    for name, shape in _OUTS:
        aps[name] = nc.dram_tensor(f"out_{name}", shape, F32, kind="ExternalOutput").ap()
    trunk(nc, aps)
    r = run_bass_kernel_spmd(nc, [arrays], core_ids=[0])
    return tuple(r.results[0][f"out_{name}"] for name, _ in _OUTS)
```
